# Optimizing a Trainium2 kernel written in Bass

```python
import math
import jax, jax.numpy as jnp
from jax import lax
import numpy as np

D_MODEL = 1024
BATCH = 1
SEQ = 256
DEPTH = 2

D_FF = 2816
FFN_RESIDUAL_SCALE = 0.5
EPS = 1e-6
BLOCK_Q = 128

A_WIDTH = 512
A_CONV = 3
B_WIDTH = 512
B_CONV = 31
C_HEADS = 4
C_QK_DIM = 64
C_V_DIM = 2 * C_QK_DIM
C_QK_WIDTH = C_HEADS * 2 * C_QK_DIM
C_V_WIDTH = C_HEADS * C_V_DIM
D_HEADS = 8
D_HEAD_DIM = 64
D_WIDTH = D_HEADS * D_HEAD_DIM
N_BRANCHES = 4

IN_SPLITS = (A_WIDTH, A_WIDTH, A_WIDTH,
             2 * B_WIDTH,
             C_QK_WIDTH, C_QK_WIDTH, C_V_WIDTH,
             D_WIDTH, D_WIDTH, D_WIDTH, D_HEADS,
             N_BRANCHES * D_MODEL)
IN_WIDTH = sum(IN_SPLITS)


def _split(x, sizes):
    idx = []
    acc = 0
    for s in sizes[:-1]:
        acc += s
        idx.append(acc)
    return jnp.split(x, idx, axis=-1)

def rms_norm(x, g):
    xf = x.astype(jnp.float32)
    y = xf * lax.rsqrt(jnp.mean(xf * xf, axis=-1, keepdims=True) + EPS)
    return (y * g.astype(jnp.float32)).astype(x.dtype)

def layer_norm(x, g, b):
    xf = x.astype(jnp.float32)
    mu = jnp.mean(xf, axis=-1, keepdims=True)
    xc = xf - mu
    var = jnp.mean(xc * xc, axis=-1, keepdims=True)
    return (xc * lax.rsqrt(var + EPS) * g.astype(jnp.float32) + b.astype(jnp.float32)).astype(x.dtype)

def swiglu(h, w_gate, w_up, w_down):
    return (jax.nn.silu(h @ w_gate) * (h @ w_up)) @ w_down

def causal_depthwise_conv(x, w):
    k_width, ch = w.shape
    return lax.conv_general_dilated(x, w[:, None, :], window_strides=(1,), padding=[(k_width - 1, 0)],
                                    dimension_numbers=('NWC', 'WIO', 'NWC'), feature_group_count=ch)

def short_conv_mixer(gate_b, gate_c, xin, conv_w, w_out):
    return (gate_b * causal_depthwise_conv(gate_c * xin, conv_w)) @ w_out

def conformer_conv_mixer(u, conv_w, conv_b, ln_g, ln_b, w_out):
    a, g = jnp.split(u, 2, axis=-1)
    y = a * jax.nn.sigmoid(g)
    y = causal_depthwise_conv(y, conv_w) + conv_b
    y = jax.nn.silu(layer_norm(y, ln_g, ln_b))
    return y @ w_out

def alibi_slopes(n_heads):
    return jnp.exp2(-8.0 / n_heads * jnp.arange(1, n_heads + 1, dtype=jnp.float32))

def diff_attention_mixer(q, k, v, lam_q1, lam_k1, lam_q2, lam_k2, subln_g, w_out, lambda_init):
    b, s, _ = q.shape
    q = q.reshape(b, s, C_HEADS, 2, C_QK_DIM)
    k = k.reshape(b, s, C_HEADS, 2, C_QK_DIM)
    v = v.reshape(b, s, C_HEADS, C_V_DIM)
    f32 = jnp.float32
    lam = (jnp.exp(jnp.sum(lam_q1.astype(f32) * lam_k1.astype(f32)))
           - jnp.exp(jnp.sum(lam_q2.astype(f32) * lam_k2.astype(f32))) + lambda_init)
    slopes = alibi_slopes(C_HEADS)[:, None, None]
    scale = C_QK_DIM ** -0.5
    outs = []
    for i in range(s // BLOCK_Q):
        q0, q1 = i * BLOCK_Q, (i + 1) * BLOCK_Q
        dist = (jnp.arange(q0, q1)[:, None] - jnp.arange(q1)[None, :]).astype(f32)
        bias = jnp.where(dist >= 0, -slopes * dist, -jnp.inf)
        logits = jnp.einsum('bqhmd,bkhmd->bmhqk', q[:, q0:q1], k[:, :q1]).astype(f32) * scale + bias
        p = jax.nn.softmax(logits, axis=-1)
        pd = p[:, 0] - lam * p[:, 1]
        outs.append(jnp.einsum('bhqk,bkhd->bqhd', pd.astype(v.dtype), v[:, :q1]))
    o = jnp.concatenate(outs, axis=1)
    o = rms_norm(o, subln_g) * (1.0 - lambda_init)
    return o.reshape(b, s, C_V_WIDTH) @ w_out

def forgetting_attention_mixer(q, k, v, f_logit, f_bias, w_out):
    b, s, _ = q.shape
    q = q.reshape(b, s, D_HEADS, D_HEAD_DIM)
    k = k.reshape(b, s, D_HEADS, D_HEAD_DIM)
    v = v.reshape(b, s, D_HEADS, D_HEAD_DIM)
    f32 = jnp.float32
    log_f = jax.nn.log_sigmoid(f_logit.astype(f32) + f_bias.astype(f32))
    cum = jnp.cumsum(log_f, axis=1).transpose(0, 2, 1)
    scale = D_HEAD_DIM ** -0.5
    outs = []
    for i in range(s // BLOCK_Q):
        q0, q1 = i * BLOCK_Q, (i + 1) * BLOCK_Q
        causal = jnp.arange(q0, q1)[:, None] >= jnp.arange(q1)[None, :]
        decay = cum[:, :, q0:q1, None] - cum[:, :, None, :q1]
        bias = jnp.where(causal, decay, -jnp.inf)
        logits = jnp.einsum('bqhd,bkhd->bhqk', q[:, q0:q1], k[:, :q1]).astype(f32) * scale + bias
        p = jax.nn.softmax(logits, axis=-1)
        outs.append(jnp.einsum('bhqk,bkhd->bqhd', p.astype(v.dtype), v[:, :q1]))
    o = jnp.concatenate(outs, axis=1)
    return o.reshape(b, s, D_WIDTH) @ w_out

def first_inputs(seed: int = 0) -> dict:
    key = jax.random.key(seed)
    ks = jax.random.split(key, 40)
    it = iter(range(40))

    def nk():
        return ks[next(it)]

    def w(shape, fan_in):
        return jax.random.normal(nk(), shape, jnp.float32) * (fan_in ** -0.5)

    def gain(shape):
        return 1.0 + 0.05 * jax.random.normal(nk(), shape, jnp.float32)

    def small(shape, scale=0.02, offset=0.0):
        return offset + scale * jax.random.normal(nk(), shape, jnp.float32)

    L = DEPTH
    return {
        'x': jax.random.normal(nk(), (BATCH, SEQ, D_MODEL), jnp.float32),
        'ffn1_pre_g': gain((L, D_MODEL)),
        'ffn1_post_g': gain((L, D_MODEL)),
        'ffn1_w_gate': w((L, D_MODEL, D_FF), D_MODEL),
        'ffn1_w_up': w((L, D_MODEL, D_FF), D_MODEL),
        'ffn1_w_down': w((L, D_FF, D_MODEL), D_FF),
        'mix_pre_g': gain((L, D_MODEL)),
        'mix_post_g': gain((L, D_MODEL)),
        'w_in': w((L, D_MODEL, IN_WIDTH), D_MODEL),
        'a_conv_w': w((L, A_CONV, A_WIDTH), A_CONV),
        'a_w_out': w((L, A_WIDTH, D_MODEL), A_WIDTH),
        'b_conv_w': w((L, B_CONV, B_WIDTH), B_CONV),
        'b_conv_b': small((L, B_WIDTH)),
        'b_ln_g': gain((L, B_WIDTH)),
        'b_ln_b': small((L, B_WIDTH)),
        'b_w_out': w((L, B_WIDTH, D_MODEL), B_WIDTH),
        'c_lam_q1': small((L, C_QK_DIM), 0.1),
        'c_lam_k1': small((L, C_QK_DIM), 0.1),
        'c_lam_q2': small((L, C_QK_DIM), 0.1),
        'c_lam_k2': small((L, C_QK_DIM), 0.1),
        'c_subln_g': gain((L, C_V_DIM)),
        'c_w_out': w((L, C_V_WIDTH, D_MODEL), C_V_WIDTH),
        'd_forget_b': small((L, D_HEADS), 0.5, 3.0),
        'd_w_out': w((L, D_WIDTH, D_MODEL), D_WIDTH),
        'w_o': w((L, D_MODEL, D_MODEL), D_MODEL),
        'ffn2_pre_g': gain((L, D_MODEL)),
        'ffn2_post_g': gain((L, D_MODEL)),
        'ffn2_w_gate': w((L, D_MODEL, D_FF), D_MODEL),
        'ffn2_w_up': w((L, D_MODEL, D_FF), D_MODEL),
        'ffn2_w_down': w((L, D_FF, D_MODEL), D_FF),
    }

def first_block(x, ffn1_pre_g, ffn1_post_g, ffn1_w_gate, ffn1_w_up, ffn1_w_down,
              mix_pre_g, mix_post_g, w_in, a_conv_w, a_w_out,
              b_conv_w, b_conv_b, b_ln_g, b_ln_b, b_w_out,
              c_lam_q1, c_lam_k1, c_lam_q2, c_lam_k2, c_subln_g, c_w_out,
              d_forget_b, d_w_out, w_o,
              ffn2_pre_g, ffn2_post_g, ffn2_w_gate, ffn2_w_up, ffn2_w_down):
    bsz, seq, _ = x.shape
    h = x
    for l in range(DEPTH):
        lambda_init = 0.8 - 0.6 * math.exp(-0.3 * l)
        f = swiglu(rms_norm(h, ffn1_pre_g[l]), ffn1_w_gate[l], ffn1_w_up[l], ffn1_w_down[l])
        h = h + FFN_RESIDUAL_SCALE * rms_norm(f, ffn1_post_g[l])
        u = rms_norm(h, mix_pre_g[l])
        (a_b, a_c, a_x, b_u, c_q, c_k, c_v,
         d_q, d_k, d_v, d_f, gate_logits) = _split(u @ w_in[l], IN_SPLITS)
        y_a = short_conv_mixer(a_b, a_c, a_x, a_conv_w[l], a_w_out[l])
        y_b = conformer_conv_mixer(b_u, b_conv_w[l], b_conv_b[l], b_ln_g[l], b_ln_b[l], b_w_out[l])
        y_c = diff_attention_mixer(c_q, c_k, c_v, c_lam_q1[l], c_lam_k1[l], c_lam_q2[l], c_lam_k2[l],
                                   c_subln_g[l], c_w_out[l], lambda_init)
        y_d = forgetting_attention_mixer(d_q, d_k, d_v, d_f, d_forget_b[l], d_w_out[l])
        g = jax.nn.sigmoid(gate_logits).reshape(bsz, seq, N_BRANCHES, D_MODEL)
        merged = g[:, :, 0] * y_a + g[:, :, 1] * y_b + g[:, :, 2] * y_c + g[:, :, 3] * y_d
        h = h + rms_norm(merged @ w_o[l], mix_post_g[l])
        f = swiglu(rms_norm(h, ffn2_pre_g[l]), ffn2_w_gate[l], ffn2_w_up[l], ffn2_w_down[l])
        h = h + FFN_RESIDUAL_SCALE * rms_norm(f, ffn2_post_g[l])
    return h


N_HEADS_A = 16
N_KV_A = 4
HEAD_DIM_A = 64
WINDOW = 128
N_HEADS_B = 8
KEY_DIM_B = 128
VAL_DIM_B = 128
CONV_K = 4
CHUNK = 64
NUM_BUCKETS = 32
MAX_DISTANCE = 128
DN_ALPHA = (2 * DEPTH) ** 0.25
DN_BETA = (8 * DEPTH) ** -0.25
LN_EPS = 1e-5
NORM_EPS = 1e-6
NEG_INF = -1e30

Q_A = N_HEADS_A * HEAD_DIM_A
KV_W = N_KV_A * HEAD_DIM_A
QK_B = N_HEADS_B * KEY_DIM_B
V_B = N_HEADS_B * VAL_DIM_B
CONV_CH = 2 * QK_B + V_B
SPLIT_SIZES = (Q_A, KV_W, KV_W, CONV_CH, N_HEADS_B, N_HEADS_B, V_B, 2 * D_MODEL)
N_IN = sum(SPLIT_SIZES)
SPLIT_POINTS = tuple(int(s) for s in np.cumsum(SPLIT_SIZES)[:-1])


def layernorm(x, g, b):
    xf = x.astype(jnp.float32)
    mu = xf.mean(-1, keepdims=True)
    var = jnp.square(xf - mu).mean(-1, keepdims=True)
    y = (xf - mu) * lax.rsqrt(var + LN_EPS) * g.astype(jnp.float32) + b.astype(jnp.float32)
    return y.astype(x.dtype)

def swiglu_2(x, w13, w2):
    gate, up = jnp.split(x @ w13, 2, axis=-1)
    return (jax.nn.silu(gate) * up) @ w2

def t5_bucket(rel):
    n = jnp.maximum(rel, 0)
    max_exact = NUM_BUCKETS // 2
    nf = jnp.maximum(n, 1).astype(jnp.float32)
    large = max_exact + (jnp.log(nf / max_exact) / math.log(MAX_DISTANCE / max_exact)
                         * (NUM_BUCKETS - max_exact)).astype(jnp.int32)
    large = jnp.minimum(large, NUM_BUCKETS - 1)
    return jnp.where(n < max_exact, n, large)

def band_rel():
    r = jnp.arange(WINDOW)[:, None]
    j = jnp.arange(2 * WINDOW)[None, :]
    return r + WINDOW - j

def sliding_window_attention(q, k, v, pos_bias, sink):
    b, l = q.shape[:2]
    nb = l // WINDOW
    grp = N_HEADS_A // N_KV_A
    qb = (q.astype(jnp.float32) * HEAD_DIM_A ** -0.5).reshape(b, nb, WINDOW, N_KV_A, grp, HEAD_DIM_A)
    kb = k.astype(jnp.float32).reshape(b, nb, WINDOW, N_KV_A, HEAD_DIM_A)
    vb = v.astype(jnp.float32).reshape(b, nb, WINDOW, N_KV_A, HEAD_DIM_A)

    def with_prev(t):
        prev = jnp.concatenate([jnp.zeros_like(t[:, :1]), t[:, :-1]], axis=1)
        return jnp.concatenate([prev, t], axis=2)

    kk, vv = with_prev(kb), with_prev(vb)
    rel = band_rel()
    in_band = (rel >= 0) & (rel < WINDOW)
    key_in_own_block = jnp.arange(2 * WINDOW) >= WINDOW
    bias = pos_bias.reshape(N_KV_A, grp, WINDOW, 2 * WINDOW)
    sk = sink.astype(jnp.float32).reshape(N_KV_A, grp, 1, 1)

    def one_block(args):
        qi, ki, vi, i = args
        s = jnp.einsum('bqkgd,bskd->bkgqs', qi, ki) + bias
        valid = in_band & ((i > 0) | key_in_own_block)
        s = jnp.where(valid, s, NEG_INF)
        m = jnp.maximum(s.max(-1, keepdims=True), sk)
        p = jnp.exp(s - m)
        p = p / (p.sum(-1, keepdims=True) + jnp.exp(sk - m))
        return jnp.einsum('bkgqs,bskd->bqkgd', p, vi)

    o = lax.map(one_block, (jnp.moveaxis(qb, 1, 0), jnp.moveaxis(kk, 1, 0),
                            jnp.moveaxis(vv, 1, 0), jnp.arange(nb)))
    return jnp.moveaxis(o, 0, 1).reshape(b, l, Q_A)

def causal_depthwise_conv_2(u, w):
    return lax.conv_general_dilated(u, w[:, None, :].astype(u.dtype), window_strides=(1,),
                                    padding=[(CONV_K - 1, 0)],
                                    dimension_numbers=('NWC', 'WIO', 'NWC'),
                                    feature_group_count=u.shape[-1])

def l2norm(t):
    t = t.astype(jnp.float32)
    return t * lax.rsqrt(jnp.sum(t * t, -1, keepdims=True) + NORM_EPS)

def gated_delta_rule(q, k, v, g, beta):
    b, l, h, dk = q.shape
    dv = v.shape[-1]
    n = l // CHUNK

    def chunked(t):
        return t.reshape(b, n, CHUNK, h, t.shape[-1]).transpose(0, 3, 1, 2, 4)

    q = chunked(q * dk ** -0.5)
    k = chunked(k)
    v = chunked(v)
    g = jnp.cumsum(g.reshape(b, n, CHUNK, h).transpose(0, 3, 1, 2), axis=-1)
    beta = beta.reshape(b, n, CHUNK, h).transpose(0, 3, 1, 2)[..., None]
    kb, vb = k * beta, v * beta

    causal = jnp.tril(jnp.ones((CHUNK, CHUNK), bool))
    strict = jnp.tril(jnp.ones((CHUNK, CHUNK), bool), -1)
    decay = jnp.exp(jnp.where(causal, g[..., :, None] - g[..., None, :], NEG_INF))
    lower = jnp.where(strict, jnp.einsum('bhncd,bhnmd->bhncm', kb, k) * decay, 0.0)
    eye = jnp.eye(CHUNK, dtype=jnp.float32)
    t_inv = lax.linalg.triangular_solve(lower + eye, jnp.broadcast_to(eye, lower.shape),
                                        left_side=True, lower=True, unit_diagonal=True)
    u = t_inv @ vb
    w = t_inv @ (kb * jnp.exp(g)[..., None])
    a_intra = jnp.where(causal, jnp.einsum('bhncd,bhnmd->bhncm', q, k) * decay, 0.0)
    g_last = g[..., -1]
    k_tail = k * jnp.exp(g_last[..., None] - g)[..., None]
    q_dec = q * jnp.exp(g)[..., None]

    def step(s, xs):
        qd, kt, uc, wc, ac, gl = xs
        v_new = uc - jnp.einsum('bhcd,bhde->bhce', wc, s)
        o = jnp.einsum('bhcd,bhde->bhce', qd, s) + jnp.einsum('bhcm,bhme->bhce', ac, v_new)
        s = s * jnp.exp(gl)[..., None, None] + jnp.einsum('bhcd,bhce->bhde', kt, v_new)
        return s, o

    xs = tuple(jnp.moveaxis(t, 2, 0) for t in (q_dec, k_tail, u, w, a_intra, g_last))
    s0 = jnp.zeros((b, h, dk, dv), jnp.float32)
    _, o = lax.scan(step, s0, xs)
    return o.transpose(1, 0, 3, 2, 4).reshape(b, l, h, dv)

def hybrid_mixer(x, w_in, conv_w, a_log, dt_bias, dn_norm_g, sink,
                 w_branch_a, w_branch_b, w_out, pos_bias):
    b, l, _ = x.shape
    hcat = x @ w_in
    qa, ka, va, qkv_b, beta_raw, dt_raw, z, gate_raw = jnp.split(hcat, SPLIT_POINTS, axis=-1)

    ya = sliding_window_attention(qa.reshape(b, l, N_HEADS_A, HEAD_DIM_A),
                                  ka.reshape(b, l, N_KV_A, HEAD_DIM_A),
                                  va.reshape(b, l, N_KV_A, HEAD_DIM_A), pos_bias, sink)
    ya = ya.astype(x.dtype) @ w_branch_a

    qkv_b = jax.nn.silu(causal_depthwise_conv_2(qkv_b, conv_w))
    qb, kb, vb = jnp.split(qkv_b, (QK_B, 2 * QK_B), axis=-1)
    qb = l2norm(qb.reshape(b, l, N_HEADS_B, KEY_DIM_B))
    kb = l2norm(kb.reshape(b, l, N_HEADS_B, KEY_DIM_B))
    vb = vb.reshape(b, l, N_HEADS_B, VAL_DIM_B).astype(jnp.float32)
    beta = jax.nn.sigmoid(beta_raw.astype(jnp.float32))
    g = -jnp.exp(a_log.astype(jnp.float32)) * jax.nn.softplus(
        dt_raw.astype(jnp.float32) + dt_bias.astype(jnp.float32))
    o = gated_delta_rule(qb, kb, vb, g, beta)
    o = (o * lax.rsqrt(jnp.mean(o * o, -1, keepdims=True) + NORM_EPS)
         * dn_norm_g.astype(jnp.float32)
         * jax.nn.silu(z.reshape(b, l, N_HEADS_B, VAL_DIM_B).astype(jnp.float32)))
    yb = o.reshape(b, l, V_B).astype(x.dtype) @ w_branch_b

    gate_a, gate_b = jnp.split(jax.nn.sigmoid(gate_raw), 2, axis=-1)
    return (gate_a * ya + gate_b * yb) @ w_out

def second_inputs(seed: int = 0) -> dict:
    key = jax.random.key(seed)
    ks = jax.random.split(key, 16)
    f32 = jnp.float32

    def nrm(k, shape, scale):
        return jax.random.normal(k, shape, f32) * scale

    dt = jnp.exp(jax.random.uniform(ks[9], (DEPTH, N_HEADS_B), f32, math.log(1e-3), math.log(1e-1)))
    return {
        "x": nrm(ks[0], (BATCH, SEQ, D_MODEL), 1.0),
        "rel_bias": nrm(ks[1], (NUM_BUCKETS, N_HEADS_A), 0.5),
        "ln_g": 1.0 + nrm(ks[2], (DEPTH, 3, D_MODEL), 0.05),
        "ln_b": nrm(ks[3], (DEPTH, 3, D_MODEL), 0.02),
        "ffn_w13": nrm(ks[4], (DEPTH, 2, D_MODEL, 2 * D_FF), D_MODEL ** -0.5),
        "ffn_w2": nrm(ks[5], (DEPTH, 2, D_FF, D_MODEL), DN_BETA * D_FF ** -0.5),
        "w_in": nrm(ks[6], (DEPTH, D_MODEL, N_IN), D_MODEL ** -0.5),
        "conv_w": nrm(ks[7], (DEPTH, CONV_K, CONV_CH), CONV_K ** -0.5),
        "a_log": jnp.log(jax.random.uniform(ks[8], (DEPTH, N_HEADS_B), f32, 1.0, 16.0)),
        "dt_bias": dt + jnp.log(-jnp.expm1(-dt)),
        "dn_norm_g": 1.0 + nrm(ks[10], (DEPTH, VAL_DIM_B), 0.05),
        "sinks": nrm(ks[11], (DEPTH, N_HEADS_A), 0.5),
        "w_branch_a": nrm(ks[12], (DEPTH, Q_A, D_MODEL), Q_A ** -0.5),
        "w_branch_b": nrm(ks[13], (DEPTH, V_B, D_MODEL), V_B ** -0.5),
        "w_out": nrm(ks[14], (DEPTH, D_MODEL, D_MODEL), DN_BETA * D_MODEL ** -0.5),
    }

def second_block(x, rel_bias, ln_g, ln_b, ffn_w13, ffn_w2, w_in, conv_w, a_log, dt_bias,
              dn_norm_g, sinks, w_branch_a, w_branch_b, w_out):
    pos_bias = jnp.transpose(rel_bias[t5_bucket(band_rel())], (2, 0, 1)).astype(jnp.float32)
    for i in range(DEPTH):
        x = layernorm(DN_ALPHA * x + 0.5 * swiglu_2(x, ffn_w13[i, 0], ffn_w2[i, 0]), ln_g[i, 0], ln_b[i, 0])
        y = hybrid_mixer(x, w_in[i], conv_w[i], a_log[i], dt_bias[i], dn_norm_g[i], sinks[i],
                         w_branch_a[i], w_branch_b[i], w_out[i], pos_bias)
        x = layernorm(DN_ALPHA * x + y, ln_g[i, 1], ln_b[i, 1])
        x = layernorm(DN_ALPHA * x + 0.5 * swiglu_2(x, ffn_w13[i, 1], ffn_w2[i, 1]), ln_g[i, 2], ln_b[i, 2])
    return x


def setup_inputs(seed=0):
    out = dict(first_inputs(seed))
    for name, value in second_inputs(seed + 1).items():
        if name != "x":
            out[name + "_2"] = value
    return out


def reference(
    x, ffn1_pre_g, ffn1_post_g, ffn1_w_gate, ffn1_w_up, ffn1_w_down, mix_pre_g, mix_post_g,
    w_in, a_conv_w, a_w_out, b_conv_w, b_conv_b, b_ln_g, b_ln_b, b_w_out, c_lam_q1, c_lam_k1,
    c_lam_q2, c_lam_k2, c_subln_g, c_w_out, d_forget_b, d_w_out, w_o, ffn2_pre_g, ffn2_post_g,
    ffn2_w_gate, ffn2_w_up, ffn2_w_down, rel_bias_2, ln_g_2, ln_b_2, ffn_w13_2, ffn_w2_2,
    w_in_2, conv_w_2, a_log_2, dt_bias_2, dn_norm_g_2, sinks_2, w_branch_a_2, w_branch_b_2,
    w_out_2,
):
    x = first_block(
        x, ffn1_pre_g, ffn1_post_g, ffn1_w_gate, ffn1_w_up, ffn1_w_down, mix_pre_g, mix_post_g,
        w_in, a_conv_w, a_w_out, b_conv_w, b_conv_b, b_ln_g, b_ln_b, b_w_out, c_lam_q1,
        c_lam_k1, c_lam_q2, c_lam_k2, c_subln_g, c_w_out, d_forget_b, d_w_out, w_o, ffn2_pre_g,
        ffn2_post_g, ffn2_w_gate, ffn2_w_up, ffn2_w_down,
    )
    return second_block(
        x, rel_bias_2, ln_g_2, ln_b_2, ffn_w13_2, ffn_w2_2, w_in_2, conv_w_2, a_log_2,
        dt_bias_2, dn_norm_g_2, sinks_2, w_branch_a_2, w_branch_b_2, w_out_2,
    )


_drawn_inputs = setup_inputs


def setup_inputs(seed=0):
    import zlib

    import numpy as np

    out = dict(_drawn_inputs(seed))
    spreads = {}
    factors = {'b_ln_b': 5.481,
     'c_lam_k2': 8.0,
     'dn_norm_g_2': 6.724,
     'sinks_2': 8.0,
     'rel_bias_2': 3.048}
    for name, (base, spread) in spreads.items():
        noise = np.random.default_rng([zlib.crc32(name.encode()), seed]).standard_normal(out[name].shape)
        drawn = base * np.exp(spread * noise) if base else spread * noise
        out[name] = __import__('jax').numpy.asarray(drawn.astype(out[name].dtype))
    for name, factor in factors.items():
        out[name] = (out[name] * factor).astype(out[name].dtype)
    return out
```

```python
import math
from contextlib import ExitStack

import numpy as np

import concourse.bass as bass
import concourse.mybir as mybir
from concourse.alu_op_type import AluOpType as ALU

ACT = mybir.ActivationFunctionType
F32 = mybir.dt.float32

P = 128
D = 1024
KB = D // P
S = 256
T = S // P
L = 2
FF = 2816
FB = FF // P
FP = FF // 256
EPS = 1e-6
LN_EPS = 1e-5
SLOTS = 8
UNIT = 2048
ALPHA = (2 * L) ** 0.25
MASKED = -1e30
HALF = 512
NH_C, NH_D, NH_A, NH_B = 4, 8, 16, 8
QK_SCALE = 0.125
LEVELS = 7

_c = 0


def _cols(table):
    out, at = {}, 0
    for name, n in table:
        out[name] = (at, at + n)
        at += n
    return out, at


COL1, NCOL1 = _cols([("g0", 8), ("g1", 8), ("g2", 8), ("aw", 12), ("bw", 124), ("bb", 4), ("blg", 4),
                     ("blb", 4), ("sub", 1), ("lami", 2), ("fb", 8), ("lam", 256), ("wf", 64)])
COL2, NCOL2 = _cols([("cw", 96), ("dng", 1), ("sink", 16), ("dtb", 8), ("alog", 8), ("ws", 128)])
CON1, NCON1 = _cols([("ident", 128), ("tri", 512), ("causal", 256), ("alibi", 1024), ("sel", 1024)])
CON2, NCON2 = _cols([("ident", 128), ("tri", 128), ("ones", 128), ("maskt", 128), ("strict", 128),
                     ("level", 896), ("sel", 1024)])
NCON = max(NCON1, NCON2)


class Job:

    def __init__(self, bank, turn, full, taken):
        self.bank, self.turn, self.full, self.taken = bank, turn, full, taken


class Step:

    def __init__(self, kind, last_of, a=None, acc=None, b=None, br=None, e=None, h=None, half=None, hp=None, i=None, j=None, k=None, p=None, root=None, s=None, src=None, w=None, what=None):
        self.kind, self.last_of, self.jobs, self.at = kind, last_of, [], {}
        self.a = a
        self.acc = acc
        self.b = b
        self.br = br
        self.e = e
        self.h = h
        self.half = half
        self.hp = hp
        self.i = i
        self.j = j
        self.k = k
        self.p = p
        self.root = root
        self.s = s
        self.src = src
        self.w = w
        self.what = what


class Now:

    def __init__(self):
        self.blk, self.l = 1, 0


class Plan:

    def __init__(self):
        self.steps, self.count, self.stream, self.named = [], {}, [], {}
        self.rot = {"lo": 0, "hi": 0, "s": 0}

    def tick(self, name, n):
        self.count[name] = self.count.get(name, 0) + n
        return self.count[name]

    def job(self, bank, fulls=1, takes=1):
        if isinstance(bank, str):
            pool = {"lo": (0, 1, 2, 3), "hi": (4, 5, 6, 7), "s": (4, 5)}[bank]
            self.rot[bank] += 1
            bank = pool[(self.rot[bank] - 1) % len(pool)]
        turn = self.count.get(("taken", bank), 0)
        return Job(bank, turn, self.tick(("full", bank), fulls), self.tick(("taken", bank), takes))

    def step(self, kind, name=None, banks=(), signals=(), last_of=(), **args):
        st = Step(kind, list(last_of), **args)
        st.jobs = [self.job(*(b if isinstance(b, tuple) else (b,))) for b in banks]
        st.at = {s: self.tick(s, n) for s, n in signals}
        self.stream += st.last_of
        self.steps.append(st)
        if name is not None:
            self.named[name] = st
        return st

    def close(self):
        self.units = len(self.stream)
        self.pads = -self.units % SLOTS
        self.place = {key: i for i, key in enumerate(self.stream)}
        assert len(self.place) == self.units


def plan_ffn(pl, s):
    def down(j):
        pl.step("down", ("down", s, j), s=s, j=j, last_of=[("d", s, j // 2)] if j % 2 else [])

    for j in range(FB):
        pl.step("gu", ("gu", s, j), banks=["hi"], s=s, j=j, signals=[("gate_silu_ready", 1)],
                last_of=[("g", s, j // 2), ("u", s, j // 2)] if j % 2 else [])
        if j >= 2:
            down(j - 2)
    down(FB - 2)
    down(FB - 1)


def weave(pl, chain, dense, every):
    dense = list(dense)
    for n, f in enumerate(chain):
        f()
        if n % every == every - 1 and dense:
            dense.pop(0)()
    for f in dense:
        f()


def plan_first():
    pl = Plan()
    acc_lo = [(b, 1, 1) for b in range(4)]
    acc_hi = [(b, 1, 1) for b in range(4, 8)]

    def norm_in(s):
        pl.step("norm", ("norm", s), s=s, signals=[("squares_summed", 1), ("rsqrt_ready", 1), ("normed_ready", 1)])
        pl.step("xt", ("xt", s), s=s, banks=["hi"] * 4)

    def post(s, acc, root):
        pl.step("post", ("post", s), s=s, acc=acc, root=root, banks=[],
                signals=[("squares_summed", 2), ("rsqrt_ready", 2), ("residual_ready", 2)])

    pl.step("params", signals=[("params_loaded", 16)])

    def ffn(s):
        pl.step("feature", signals=[("feature_rows_loaded", 16)], s=s)
        norm_in(s)
        acc = pl.step("acc", ("acc", s), banks=acc_lo, s=s)
        plan_ffn(pl, s)
        post(s, acc, 2 * D ** -0.5)

    ffn(0)
    pl.step("feature", signals=[("feature_rows_loaded", 16)], s=1)
    norm_in(1)
    pl.step("lam", "lam", signals=[("lambda_dots", 1), ("lambda_exps", 1), ("lambda_ready", 1)])
    for p in range(2):
        pl.step("pb", ("pb", p), banks=["lo", "lo"], signals=[("branch_gate_ready", 2)], p=p, last_of=[("w", 6 + p), ("w", 8 + p)])
    taps = [(t, min(t + 5, 31)) for t in range(0, 31, 5)]

    def conv_b():
        if taps:
            a, b = taps.pop(0)
            pl.step("convb", ("convb", a), a=a, b=b, signals=[("conv_b_ready", 1 if b == 31 else 0)])

    for p in range(2):
        pl.step("pc", ("cq", p), banks=["lo"], what="cq", p=p, last_of=[("w", 10 + p)])
    conv_b()
    for p in range(2):
        pl.step("pc", ("ck", p), banks=["lo"], what="ck", p=p, last_of=[("w", 12 + p)])
    conv_b()
    for p in range(2):
        pl.step("pc", ("cv", p), banks=["lo"], what="cv", p=p, last_of=[("w", 14 + p)])
    conv_b()
    pl.step("pf", "pf", banks=["lo"], signals=[("forget_log_ready", 1), ("log_forget_ready", 1)])
    for p in range(2):
        pl.step("pc", ("dq", p), banks=["lo"], what="dq", p=p, last_of=[("w", 16 + p)])
    conv_b()
    pl.step("cum", "cum", banks=["s"])

    def chain_of(br, heads):
        steps = []
        per = 2 if br == "c" else 1

        def score(h):
            for m in range(per):
                e = h * per + m
                pl.step("score", ("score", br, e), banks=["s"], br=br, e=e, signals=[("probs_ready", 1)])
            if br == "c":
                pl.step("diff", ("diff", h), h=h, signals=[("probs_combined", 1)])

        def turn(h):
            pl.step("turn", ("turn", br, h), banks=["s"], br=br, h=h)

        def value(h):
            pl.step("value", ("value", br, h), br=br, h=h, signals=[("values_summed", 1)])

        for n in range(heads + 2):
            if n < heads:
                steps.append(lambda n=n: score(n))
            if 1 <= n <= heads:
                steps.append(lambda n=n: turn(n - 1))
            if n >= 2:
                steps.append(lambda n=n: value(n - 2))
        return steps

    dense = []
    for p in range(2):
        dense.append(lambda p=p: pl.step("pc", ("dk", p), banks=["lo"], what="dk", p=p, last_of=[("w", 18 + p)]))
        dense.append(conv_b)
    for p in range(2):
        dense.append(lambda p=p: pl.step("pc", ("dv", p), banks=["lo"], what="dv", p=p, last_of=[("w", 20 + p)]))
        dense.append(conv_b)
    for p in range(2):
        dense.append(lambda p=p: pl.step("pa", ("pa", p), banks=["lo", "lo"], signals=[("branch_gate_ready", 2)], p=p, last_of=[("w", 2 + p), ("w", 4 + p)]))
    dense.append(lambda: pl.step("conva", "conva", banks=["lo", "lo"], last_of=[("w", 0), ("w", 1)],
                                 signals=[("branch_a_ready", 1)]))
    pl.step("out_open", ("oo", "c"), banks=[(6, 0, 1), (7, 0, 1)], br="c")
    weave(pl, chain_of("c", NH_C), dense, 1)
    pl.step("out_norm", ("on", "c"), br="c", signals=[("out_squares_summed", 1), ("out_rsqrt_ready", 1)])
    gates = []
    for i in range(4):
        for k in range(KB):
            p = k // 2
            last = [("w", 22 + 4 * i + p)] if k % 2 else []
            if k == 3 or k == 7:
                last = [("o", i, k // 4)] + last
            gates.append(lambda i=i, k=k, last=last: pl.step(
                "gy", ("gy", i, k), banks=["lo"], i=i, k=k, last_of=last, signals=[("gate_tanh_ready", 1)]))
    gates[0]()
    pl.step("out_turn", ("ot", "c"), banks=["s", "s"], br="c")
    pl.step("lnb1", "lnb1", banks=["s", "s"], signals=[("mean_var_ready", 2), ("branch_b_rsqrt_ready", 2)])
    gates[1]()
    pl.step("lnb3", "lnb3", banks=["s", "s"])
    pl.step("out_open", ("oo", "d"), banks=[(6, 0, 1), (7, 0, 1)], br="d")
    weave(pl, chain_of("d", NH_D), gates[2:24], 1)
    pl.step("out_norm", ("on", "d"), br="d", signals=[("out_squares_summed", 0), ("out_rsqrt_ready", 0)])
    pl.step("out_turn", ("ot", "d"), banks=["s", "s"], br="d")
    gates[24]()
    gates[25]()
    acc = pl.step("acc", ("acc", 1), banks=acc_hi, s=1)
    for k in range(KB):
        if k + 2 < KB:
            gates[24 + k + 2]()
        pl.step("wo", ("wo", k), k=k, last_of=[("wo", k // 2)] if k % 2 else [], src=[("gy", 3, k)])
    post(1, acc, D ** -0.5)
    ffn(2)
    pl.close()
    return pl


def plan_second():
    pl = Plan()
    acc_lo = [(b, 1, 1) for b in range(4)]
    acc_hi = [(b, 1, 1) for b in range(4, 8)]
    pl.step("params", signals=[("params_loaded", 16)])

    def begin(s):
        pl.step("feature", signals=[("feature_rows_loaded", 16)], s=s)
        pl.step("xt", ("xt", s), s=s, banks=["hi"] * 4)
        pl.step("scale_h", ("sh", s), s=s)

    def post(s, acc):
        pl.step("post2", ("post", s), s=s, acc=acc, signals=[("mean_var_ready", 2), ("rsqrt_ready", 2), ("residual_ready", 2)])

    def ffn(s):
        begin(s)
        acc = pl.step("acc", ("acc", s), banks=acc_lo, s=s)
        plan_ffn(pl, s)
        post(s, acc)

    ffn(0)
    begin(1)

    def conv(hp, w):
        pl.step("pconv", ("pconv", hp, w), banks=["lo"], hp=hp, w=w, last_of=[("w", 6 + 4 * w + hp)],
                signals=[("conv_ready", 1), ("conv_tanh_ready", 1), ("conv_silu_ready", 1)])

    pl.step("ps", "ps", banks=["lo"], signals=[("small_proj_ready", 1), ("small_logs_ready", 1), ("log_decay_ready", 1)])
    pl.step("pk", "pk", banks=["lo"], last_of=[("w", 4)])
    for p in range(4):
        pl.step("pq", ("pq", p), banks=["lo"], p=p, last_of=[("w", p)])
    pl.step("pv", "pv", banks=["lo"], last_of=[("w", 5)])
    pl.step("cumg", "cumg", banks=["s"], signals=[("decay_diff_ready", 1), ("decay_exps_ready", 1), ("decay_scalars_ready", 1)])
    dense = [lambda p=p: pl.step("pz", ("pz", p), banks=["lo"], p=p, last_of=[("w", 18 + p)], signals=[("z_tanh_ready", 1)])
             for p in range(4)]
    dense += [lambda w=w: conv(0, w) for w in range(3)]

    def chain_of(first):
        steps = []

        def score(h):
            pl.step("score", ("score", "a", h), banks=["s"], br="a", e=h, signals=[("probs_ready", 1), ("sink_exp_ready", 1)])

        def turn(h):
            pl.step("turn", ("turn", "a", h), banks=["s"], br="a", h=h)

        def value(h):
            pl.step("value", ("value", "a", h), br="a", h=h, signals=[("values_summed", 1)])

        for n in range(10):
            if n < 8:
                steps.append(lambda n=n: score(first + n))
            if 1 <= n <= 8:
                steps.append(lambda n=n: turn(first + n - 1))
            if n >= 2:
                steps.append(lambda n=n: value(first + n - 2))
        return steps

    for half in range(2):
        pl.step("out_open", ("oo", half), banks=[(6, 0, 1), (7, 0, 1)], br="a", half=half)
        weave(pl, chain_of(8 * half), dense[:4] if half == 0 else dense[4:], 4)
        pl.step("out_norm", ("on", half), br="a", half=half)
        pl.step("out_turn", ("ot", half), banks=["s", "s"], br="a", half=half)

    gates = []
    for i in range(2):
        for k in range(KB):
            last = [("w", 22 + 4 * i + k // 2), ("o", i, k // 2)] if k % 2 else []
            gates.append(lambda i=i, k=k, last=last: pl.step(
                "gy", ("gy", i, k), banks=["lo"], i=i, k=k, last_of=last, signals=[("gate_tanh_ready", 1)]))

    for hp in range(NH_B // 2):
        chain = []
        hs = (2 * hp, 2 * hp + 1)

        def both(kind, banks, signals=(), **a):
            for h in hs:
                chain.append(lambda h=h: pl.step(kind, (kind, h) + tuple(a.values()), banks=banks, h=h,
                                                 signals=signals, **a))

        both("dtr", ["hi", "hi"], [("qk_squares_summed", 1), ("qk_rsqrt_ready", 1)])
        both("dte", [], [("head_scalars_ready", 1)])
        both("ddc", ["hi"], [("decay_ready", 1), ("strict_decay_ready", 1)])
        both("dtf", ["hi", "hi"])
        both("dkk", ["hi"])
        both("dl0", ["hi"], [("level_masked", 1)])
        for s in range(1, LEVELS):
            both("dla", ["hi"], [("level_masked", 1)], s=s)
            both("dlb", ["hi"], s=s)
        both("du1", ["hi"])
        both("du2", ["hi"])
        both("du3", ["hi"])
        both("du4", ["hi"], [("out_squares_summed", 1), ("out_rsqrt_ready", 1)])
        both("dot", ["hi"])
        dense = []
        if hp + 1 < NH_B // 2:
            dense += [lambda w=w, hp=hp: conv(hp + 1, w) for w in range(3)]
        dense += gates[2 * hp:2 * hp + 2]
        weave(pl, chain, dense, len(chain) // len(dense))
    gates[8]()
    gates[9]()
    acc = pl.step("acc", ("acc", 1), banks=acc_hi, s=1)
    for k in range(KB):
        if k + 2 < KB:
            gates[8 + k + 2]()
        pl.step("wo", ("wo", k), k=k, last_of=[("wo", k // 2)] if k % 2 else [], src=[("gy", 1, k)])
    post(1, acc)
    ffn(2)
    pl.close()
    return pl


PLANS = {1: plan_first(), 2: plan_second()}


def bias_table():
    m = np.arange(384)
    rel = 255 - m
    n = np.maximum(rel, 0)
    nf = np.maximum(n, 1).astype(np.float32)
    large = 16 + (np.log(nf / np.float32(16)) / np.float32(math.log(8)) * np.float32(16)).astype(np.int32)
    bucket = np.where(n < 16, n, np.minimum(large, 31))
    seen = (rel >= 0) & (rel < 128)
    onehot = (bucket[None, :] == np.arange(32)[:, None]) & seen[None, :]
    return onehot.astype(np.float32), np.where(seen, 0.0, MASKED).astype(np.float32)


def constants():
    i = np.arange(P)
    j256 = np.arange(S)
    ident = np.eye(P, dtype=np.float32)
    tri = np.stack([(i[:, None] + P * t <= j256[None, :]) for t in range(T)], 1).astype(np.float32)
    dist = (P + i[:, None] - j256[None, :]).astype(np.float32)
    causal = np.where(dist >= 0, 0.0, MASKED).astype(np.float32)
    alibi = np.stack([np.where(dist >= 0, -(2.0 ** (-8.0 / NH_C * (h + 1))) / QK_SCALE * dist, MASKED)
                      for h in range(NH_C)], 1).astype(np.float32)
    sel = np.zeros((P, 8, P), np.float32)
    for h in range(8):
        sel[h, h, :] = 1.0
    maskt = np.where(i[None, :] >= i[:, None], 0.0, MASKED).astype(np.float32)
    strict = (i[None, :] > i[:, None]).astype(np.float32)
    level = []
    for s in range(LEVELS):
        same = (i[None, :] >> (s + 1)) == (i[:, None] >> (s + 1))
        level.append(same & (((i[None, :] >> s) & 1) == 1) & (((i[:, None] >> s) & 1) == 0))
    level = np.stack(level, 1).astype(np.float32)
    c1 = np.concatenate([a.reshape(P, -1) for a in (ident, tri, causal, alibi, sel)], 1)
    c2 = np.concatenate([a.reshape(P, -1) for a in (ident, tri[:, 0, :P], np.ones((P, P), np.float32),
                                                    maskt, strict, level, sel)], 1)
    con = np.zeros((2, P, NCON), np.float32)
    con[0, :, :NCON1], con[1, :, :NCON2] = c1, c2
    return con


def build_kernel(nc, x, stream1, stream2, prm1, prm2, feat1, feat2, con, onehot, rowmask, relb, toep, out):
    with ExitStack() as ctx:
        def sb(name, shape):
            return ctx.enter_context(nc.sbuf_tensor(name, shape, F32))

        def sem(name):
            return ctx.enter_context(nc.semaphore(name))

        H = sb("residual", [P, T, D])
        XT = sb("normed_t", [P, KB, S])
        RING = sb("weight_ring", [P, SLOTS, UNIT])
        PG = sb("feature_rows", [P, 2, D])
        PRM = sb("params", [P, max(NCOL1, NCOL2)])
        CON = sb("constants", [P, NCON])
        PS = ctx.enter_context(nc.psum_tensor("psum", [P, 8, HALF], F32))
        SMALL = sb("small", [P, 524])
        ARENA = 26700
        W = sb("work", [P, ARENA])

        def small(a, *dims):
            n = int(np.prod(dims))
            v = SMALL[:, a:a + n]
            return v if len(dims) == 1 else v.rearrange("p (a b) -> p a b", a=dims[0])

        SS, RS = small(0, 4), small(4, 4)
        MX, NM = small(8, 4, 2), small(16, 4, 2)
        LS = small(24, 16, 2)
        RL = small(56, 16, 2)
        RC = small(88, 4)
        SSO, RSO = small(92, 16), small(108, 16)
        MV = small(124, 2, 2)
        RSB = small(128, 2)
        LAM, ELAM = small(130, 2), small(132, 2)
        NLAM, SUBG = small(134, 1), small(135, 1)
        ZF, ZA_, ZL, LF = (small(136 + 16 * n, 2, 8) for n in range(4))
        ES = small(200, 16, 2)
        HALFNEG = small(232, 16)
        ST = small(248, 4, 6)
        GDH = small(272, 1)
        SINK8 = small(273, 16)
        SBT = small(289, 2, 16)
        BETA, HB, GG = small(321, 2, 8), small(337, 2, 8), small(353, 2, 8)
        G, GL = small(369, 2, 8), small(385, 2, 8)
        EG, ET, BEG = small(401, 2, 8), small(417, 2, 8), small(433, 2, 8)
        EAL = small(449, 8)
        SSD, RD = small(457, 2, 4), small(465, 2, 4)
        SC = small(473, 2, 12)
        EPS_AT = {EPS: 0, 4 * EPS: 1, LN_EPS: 2}
        EPSES = small(498, 3, 8)
        TOUCH = small(522, 1)

        pos = [0]

        def arena(*dims, at=None):
            if at is not None:
                pos[0] = at
            n = int(np.prod(dims))
            v = W[:, pos[0]:pos[0] + n]
            pos[0] += n
            assert pos[0] <= ARENA, pos[0]
            if len(dims) == 2:
                v = v.rearrange("p (a b) -> p a b", a=dims[0])
            if len(dims) == 3:
                v = v.rearrange("p (a b c) -> p a b c", a=dims[0], b=dims[1])
            return v

        MG = arena(KB, S)
        XN = W[:, 0:T * D].rearrange("p (t d) -> p t d", t=T)
        EX = arena(4, 384)
        SG = W[:, T * D:T * D + 2 * S].rearrange("p (a b) -> p a b", a=2)
        HT = W[:, T * D + 2 * S:T * D + 5 * S].rearrange("p (a b) -> p a b", a=3)
        PT = arena(3, 384)
        ON = arena(T, 512)
        TH = arena(2, 512)
        TMP = arena(2, S)
        common = pos[0]
        CQ, CK, CV = arena(4, S), arena(4, 2, S), arena(T, 512)
        DQ, DK, DV = arena(4, S), arena(4, 2, S), arena(T, 512)
        ZB, ACCB, ZA, ACCA = arena(4, S), arena(4, S), arena(4, S), arena(4, S)
        YB1, YC, YD = arena(4, S), arena(4, S), arena(4, S)
        NC = arena(S)
        JUNK = arena(P)
        BWH = arena(31, 4)
        Y1 = [ACCA, YB1, YC, YD]
        BN = ACCB.rearrange("p a b -> p (a b)").rearrange("p (t n) -> p t n", t=T)
        BIAS = arena(NH_A, S, at=common)
        YA, ZS = arena(KB, S), arena(KB, S)
        YBB = ZS
        CO = arena(2, 6, S)
        GTR = arena(S)
        TC = arena(2 * S)
        phase = pos[0]
        QA, KA, VA = arena(KB, S), arena(4, S), arena(T, S)
        arena(0, at=phase)
        TM = arena(2, 11, P)
        AL = arena(2, 4, P)
        TT = arena(2, 4, P)
        MT, DD = arena(2, 2, P), arena(2, 2, P)
        VW, VS, OD = arena(2, 2, P), arena(2, 2, P), DD
        arena(0, at=2 * D)
        FA, FBM, DEC, P1S = arena(2, 4, P), arena(2, 3, P), arena(2, 4, P), arena(2, 2, P)
        assert pos[0] <= common - 3 * HALF

        def prm(name, blk, *dims):
            a, b = (COL1 if blk == 1 else COL2)[name]
            v = PRM[:, a:b]
            return v if not dims else v.rearrange("p (a b) -> p a b", a=dims[0])

        def cst(name, blk, *dims):
            a, b = (CON1 if blk == 1 else CON2)[name]
            v = CON[:, a:b]
            return v if not dims else v.rearrange("p (a b) -> p a b", a=dims[0])

        IDENT = CON[:, 0:P]

        bank_full = [sem(f"bank{b}_full") for b in range(8)]
        bank_taken = [sem(f"bank{b}_taken") for b in range(8)]
        slot_loaded = [sem(f"slot{s}_loaded") for s in range(SLOTS)]
        slots_free = sem("slots_free")
        x_loaded, con_loaded, out_stored = sem("x_loaded"), sem("constants_loaded"), sem("out_stored")
        prologue_done, toeplitz_stored, bias_loaded = sem("prologue_done"), sem("toeplitz_stored"), sem("bias_loaded")
        prologue_row, zeros_set = sem("prologue_row"), sem("zeros_set")
        gate_silu_ready = sem("gate_silu_ready")
        branch_gate_ready = sem("branch_gate_ready")
        squares_summed = sem("squares_summed")
        rsqrt_ready = sem("rsqrt_ready")
        normed_ready = sem("normed_ready")
        residual_ready = sem("residual_ready")
        params_loaded = sem("params_loaded")
        feature_rows_loaded = sem("feature_rows_loaded")
        lambda_dots = sem("lambda_dots")
        lambda_exps = sem("lambda_exps")
        lambda_ready = sem("lambda_ready")
        conv_b_ready = sem("conv_b_ready")
        forget_log_ready = sem("forget_log_ready")
        log_forget_ready = sem("log_forget_ready")
        probs_ready = sem("probs_ready")
        probs_combined = sem("probs_combined")
        values_summed = sem("values_summed")
        branch_a_ready = sem("branch_a_ready")
        out_squares_summed = sem("out_squares_summed")
        out_rsqrt_ready = sem("out_rsqrt_ready")
        gate_tanh_ready = sem("gate_tanh_ready")
        mean_var_ready = sem("mean_var_ready")
        branch_b_rsqrt_ready = sem("branch_b_rsqrt_ready")
        sink_exp_ready = sem("sink_exp_ready")
        small_proj_ready = sem("small_proj_ready")
        small_logs_ready = sem("small_logs_ready")
        log_decay_ready = sem("log_decay_ready")
        decay_diff_ready = sem("decay_diff_ready")
        decay_exps_ready = sem("decay_exps_ready")
        decay_scalars_ready = sem("decay_scalars_ready")
        z_tanh_ready = sem("z_tanh_ready")
        conv_ready = sem("conv_ready")
        conv_tanh_ready = sem("conv_tanh_ready")
        conv_silu_ready = sem("conv_silu_ready")
        qk_squares_summed = sem("qk_squares_summed")
        qk_rsqrt_ready = sem("qk_rsqrt_ready")
        head_scalars_ready = sem("head_scalars_ready")
        decay_ready = sem("decay_ready")
        strict_decay_ready = sem("strict_decay_ready")
        level_masked = sem("level_masked")
        CREDIT = {"residual_ready": 1, **{("taken", b): 1 for b in range(8)}}
        now = Now()

        def reach(key, k):
            per = [PLANS[b].count.get(key, 0) for b in (1, 2)]
            base = CREDIT.get(key, 0) + (L * per[0] if now.blk == 2 else 0) + k
            return now.l * per[now.blk - 1] + base

        def full_at(job):
            return reach(("full", job.bank), job.full)

        def taken_at(job):
            return reach(("taken", job.bank), job.taken)

        def turn_at(job):
            return reach(("taken", job.bank), job.turn)

        def named(key):
            return PLANS[now.blk].named[key]

        def walk(eng, kinds, blk):
            now.blk = blk
            with eng.Fori(0, L) as l:
                now.l = l
                for st in PLANS[blk].steps:
                    if st.kind in kinds:
                        kinds[st.kind](st)

        block = ctx.enter_context(nc.Block())

        @block.sync
        def _(sp):
            sp.dma_start(H[:], x.rearrange("o (t p) d -> p (o t) d", p=P)).then_inc(x_loaded, 16)
            for blk, src in ((1, stream1), (2, stream2)):
                pl = PLANS[blk]
                total = [PLANS[b].units + PLANS[b].pads for b in (1, 2)]
                with sp.Fori(0, L) as l:
                    for i in range(pl.units):
                        s = i % SLOTS
                        sp.wait_ge(slots_free, l * total[blk - 1] + (L * total[0] if blk == 2 else 0) + i + 1)
                        sp.dma_start(RING[:, s, :], src[bass.ds(l, 1), i].rearrange("a p n -> (a p) n")
                                     ).then_inc(slot_loaded[s], 16)
            now.blk, now.l = 2, L - 1
            sp.wait_ge(residual_ready, reach("residual_ready", 6))
            sp.dma_start(out.rearrange("o (t p) d -> p (o t) d", p=P), H[:]).then_inc(out_stored, 16)
            sp.wait_ge(out_stored, 16)

        @block.gpsimd
        def _(pool):
            def rsqrt(dst, src, eps, signal):
                n = dst.shape[1]
                pool.tensor_tensor(dst, src, EPSES[:, EPS_AT[eps], 0:n], ALU.add)
                pool.drain()
                pool.tensor_tensor(dst, dst, HALFNEG[:, 0:dst.shape[1]], ALU.pow).then_inc(signal, 1)

            def params(st):
                pool.wait_ge(residual_ready, reach("residual_ready", 0))
                src, n = (prm1, NCOL1) if now.blk == 1 else (prm2, NCOL2)
                pool.dma_start(PRM[:, 0:n], src[bass.ds(now.l, 1)].rearrange("a p n -> (a p) n")
                               ).then_inc(params_loaded, 16)

            def feature(st):
                pool.wait_ge(residual_ready, reach("residual_ready", 2 * st.s))
                if now.blk == 1:
                    row = feat1[bass.ds(now.l, 1), st.s:st.s + 1, :].rearrange("a b n -> (a b) n")
                    pool.dma_start(PG[:, 0, :], row.to_broadcast([P, D])).then_inc(feature_rows_loaded, 16)
                else:
                    row = feat2[bass.ds(now.l, 1), st.s].rearrange("a c n -> a (c n)")
                    pool.dma_start(PG[:].rearrange("p c n -> p (c n)"), row.to_broadcast([P, 2 * D])
                                   ).then_inc(feature_rows_loaded, 16)

            def norm(st):
                pool.wait_ge(squares_summed, reach("squares_summed", st.at["squares_summed"]))
                rsqrt(RS[:, 0:2], SS[:, 0:2], EPS, rsqrt_ready)

            def post(st):
                for t in range(T):
                    pool.wait_ge(squares_summed, reach("squares_summed", st.at["squares_summed"] - 1 + t))
                    rsqrt(RS[:, 2 + t:3 + t], SS[:, 2 + t:3 + t], 4 * EPS, rsqrt_ready)

            def post2(st):
                for t in range(T):
                    pool.wait_ge(mean_var_ready, reach("mean_var_ready", st.at["mean_var_ready"] - 1 + t))
                    rsqrt(RS[:, 2 + t:3 + t], MV[:, t, 1:2], LN_EPS, rsqrt_ready)

            def lnb1(st):
                for t in range(T):
                    pool.wait_ge(mean_var_ready, reach("mean_var_ready", st.at["mean_var_ready"] - 1 + t))
                    rsqrt(RSB[:, t:t + 1], MV[:, t, 1:2], EPS, branch_b_rsqrt_ready)

            def out_norm(st):
                if st.br == "c":
                    pool.wait_ge(out_squares_summed, reach("out_squares_summed", st.at["out_squares_summed"]))
                    rsqrt(RSO[:, 0:8], SSO[:, 0:8], EPS, out_rsqrt_ready)

            def dtr(st):
                i = st.h % 2
                pool.wait_ge(qk_squares_summed, reach("qk_squares_summed", st.at["qk_squares_summed"]))
                if st.h >= 2:
                    pool.wait_ge(head_scalars_ready, reach("head_scalars_ready", named(("dte", st.h - 2)).at["head_scalars_ready"]))
                rsqrt(RD[:, i, :], SSD[:, i, :], 4 * EPS, qk_rsqrt_ready)

            def ddc(st):
                i = st.h % 2
                dec = DEC[:, i].rearrange("p (t k) n -> p t k n", t=T)
                pool.wait_ge(decay_ready, reach("decay_ready", st.at["decay_ready"]))
                for t in range(T):
                    last = pool.tensor_tensor(dec[:, t, 0, :], dec[:, t, 1, :], cst("strict", 2), ALU.mult)
                last.then_inc(strict_decay_ready, 1)

            def level(st, s):
                i = st.h % 2
                al = AL[:, i].rearrange("p (t k) n -> p t k n", t=T)
                if s == 0:
                    ready = named(("dkk", st.h)).jobs[0]
                    pool.wait_ge(bank_taken[ready.bank], taken_at(ready))
                if s > 0:
                    done = named(("dla", st.h, s - 1) if s > 1 else ("dl0", st.h)).jobs[0]
                    pool.wait_ge(bank_full[done.bank], full_at(done))
                if s == 1:
                    ready = named(("dl0", st.h)).jobs[0]
                    pool.wait_ge(bank_taken[ready.bank], taken_at(ready))
                for t in range(T):
                    last = pool.tensor_tensor(MT[:, i, t, :], al[:, t, 0, :], cst("level", 2, LEVELS)[:, s, :],
                                              ALU.mult)
                last.then_inc(level_masked, 1)

            def du4(st):
                i = st.h % 2
                pool.wait_ge(out_squares_summed, reach("out_squares_summed", st.at["out_squares_summed"]))
                rsqrt(RSO[:, 2 * i:2 * i + 2], SSO[:, 2 * i:2 * i + 2], EPS, out_rsqrt_ready)

            pool.dma_start(CON[:, 0:NCON1], con[0, :, 0:NCON1]).then_inc(con_loaded, 16)
            pool.memset(HALFNEG[:, :], -0.5)
            for eps, at in EPS_AT.items():
                pool.drain()
                pool.memset(EPSES[:, at, :], eps)
            pool.drain()
            pool.memset(CK[64:128, :, 0, :], 0.0)
            pool.drain()
            pool.memset(CK[0:64, :, 1, :], 0.0)
            pool.drain()
            pool.memset(DK[64:128, :, 0, :], 0.0)
            pool.drain()
            pool.memset(DK[0:64, :, 1, :], 0.0)
            pool.drain()
            pool.memset(NC[:, :], 0.0).then_inc(zeros_set, 1)
            pool.drain()
            kinds = {"params": params, "feature": feature, "norm": norm, "post": post, "lnb1": lnb1,
                     "out_norm": out_norm}
            walk(pool, kinds, 1)
            now.blk, now.l = 2, 0
            pool.wait_ge(residual_ready, reach("residual_ready", 0))
            pool.dma_start(CON[:, 0:NCON2], con[1, :, 0:NCON2]).then_inc(con_loaded, 16)
            pool.dma_start(ZS[0:32, 0:2, :].rearrange("p a b -> p (a b)")[:, 0:384], onehot).then_inc(con_loaded, 16)
            pool.dma_start(ZS[0:32, 2, 0:NH_A], relb).then_inc(con_loaded, 16)
            pool.dma_start(ZS[0:NH_A, 4:6, :].rearrange("p a b -> p (a b)")[:, 0:384],
                           rowmask.to_broadcast([NH_A, 384])).then_inc(con_loaded, 16)
            pool.memset(GTR[:, :], 0.0)
            pool.wait_ge(prologue_done, 1)
            row = ZS[0:NH_A, 6:8, :].rearrange("p a b -> p (a b)")[:, 0:384]
            pool.dma_start(toep, row.unsqueeze(1).to_broadcast([NH_A, P, 384])).then_inc(toeplitz_stored, 16)
            pool.wait_ge(toeplitz_stored, 16)
            pool.dma_start(BIAS[:, :, :], bass.AP(toep.tensor, P - 1, [[383, P], [P * 384, NH_A], [1, S]])
                           ).then_inc(bias_loaded, 16)
            pool.drain().then_inc(zeros_set, 1)
            walk(pool, {"params": params, "feature": feature, "post2": post2, "dtr": dtr, "ddc": ddc,
                        "dl0": lambda st: level(st, 0), "dla": lambda st: level(st, st.s), "du4": du4}, 2)

        @block.tensor
        def _(pe):
            owed = [0]

            def mm(dst, lhsT, rhs, start=True, stop=True):
                return pe.matmul(dst, lhsT, rhs, start=start, stop=stop, skip_group_check=True)

            def transpose(dst, src):
                return pe.transpose(dst, src, IDENT)

            def release(st):
                pl = PLANS[now.blk]
                for key in st.last_of:
                    owed[0] += 1 + (pl.pads if pl.place[key] == pl.units - 1 else 0)

            def weights(key, *dims):
                pl = PLANS[now.blk]
                i = pl.place[key]
                s = i % SLOTS
                per = [16 * len(range(s, PLANS[b].units, SLOTS)) for b in (1, 2)]
                base = 16 * (i // SLOTS + 1) + (L * per[0] if now.blk == 2 else 0)
                if key not in loaded:
                    pe.wait_ge(slot_loaded[s], now.l * per[now.blk - 1] + base)
                    loaded.add(key)
                return RING[:, s, :].rearrange("p (a b) -> p a b", a=dims[0])

            loaded = set()

            def cols_product(bank, at, w, c, src, n):
                for k in range(n):
                    ins = mm(PS[:, bank, at:at + S], w[:, k, c * P:(c + 1) * P], src[:, k, :], k == 0, k == n - 1)
                    if k == 0 and owed[0]:
                        ins.then_inc(slots_free, owed[0])
                        owed[0] = 0
                return ins

            def xt(st):
                blk, src = now.blk, (XN if now.blk == 1 else H)
                if blk == 1:
                    pe.wait_ge(normed_ready, reach("normed_ready", named(("norm", st.s)).at["normed_ready"]))
                else:
                    pe.wait_ge(residual_ready, reach("residual_ready", 2 * st.s))
                for k2, job in enumerate(st.jobs):
                    pe.wait_ge(bank_taken[job.bank], turn_at(job))
                    for kk in range(2):
                        for t in range(T):
                            k = 2 * k2 + kk
                            ins = transpose(PS[:, job.bank, (kk * T + t) * P:(kk * T + t + 1) * P],
                                            src[:, t, k * P:(k + 1) * P])
                            if (kk, t) == (1, T - 1):
                                ins.then_inc(bank_full[job.bank], 1)

            def acc(st):
                for job in st.jobs:
                    pe.wait_ge(bank_taken[job.bank], turn_at(job))

            def wait_xt(s):
                for job in named(("xt", s)).jobs:
                    pe.wait_ge(bank_taken[job.bank], taken_at(job))

            def gu(st):
                job = st.jobs[0]
                if st.j == 0:
                    wait_xt(st.s)
                g = weights(("g", st.s, st.j // 2), KB)
                pe.wait_ge(bank_taken[job.bank], turn_at(job))
                cols_product(job.bank, 0, g, st.j % 2, XT, KB)
                u = weights(("u", st.s, st.j // 2), KB)
                cols_product(job.bank, S, u, st.j % 2, XT, KB).then_inc(bank_full[job.bank], 1)
                release(st)

            def down(st):
                d = weights(("d", st.s, st.j // 2), 2)
                jobs = named(("acc", st.s)).jobs
                ready = named(("gu", st.s, st.j)).jobs[0]
                pe.wait_ge(bank_taken[ready.bank], taken_at(ready))
                rows_product(st, d, st.j % 2, HT[:, st.j % 3, :], jobs, st.j == 0, st.j == FB - 1)
                release(st)
                if st.j == FB - 1:
                    flush()

            def rows_product(st, w, r, src, jobs, start, stop):
                for t in range(T):
                    for n in range(2):
                        b = jobs[2 * t + n].bank
                        ins = mm(PS[:, b, :], src[:, t * P:(t + 1) * P], w[:, r, n * HALF:(n + 1) * HALF],
                                 start, stop)
                        if stop:
                            ins.then_inc(bank_full[b], 1)
                        elif owed[0]:
                            ins.then_inc(slots_free, owed[0])
                            owed[0] = 0

            def flush():
                if owed[0]:
                    pe.drain().then_inc(slots_free, owed[0])
                    owed[0] = 0

            def pb(st):
                if st.p == 0:
                    wait_xt(1)
                a, g = weights(("w", 6 + st.p), KB), weights(("w", 8 + st.p), KB)
                for c, job in enumerate(st.jobs):
                    pe.wait_ge(bank_taken[job.bank], turn_at(job))
                    cols_product(job.bank, 0, a, c, XT, KB)
                    cols_product(job.bank, S, g, c, XT, KB).then_inc(bank_full[job.bank], 1)
                release(st)

            def project(st, key, tokens=False):
                job = st.jobs[0]
                w = weights(key, KB)
                pe.wait_ge(bank_taken[job.bank], turn_at(job))
                b = job.bank
                for c in range(2):
                    for k in range(KB):
                        if tokens:
                            ins = mm(PS[:, b, c * S:(c + 1) * S], XT[:, k, c * P:(c + 1) * P], w[:, k, :],
                                     k == 0, k == KB - 1)
                        else:
                            ins = mm(PS[:, b, c * S:(c + 1) * S], w[:, k, c * P:(c + 1) * P], XT[:, k, :],
                                     k == 0, k == KB - 1)
                        if (c, k) == (0, 0) and owed[0]:
                            ins.then_inc(slots_free, owed[0])
                            owed[0] = 0
                ins.then_inc(bank_full[b], 1)
                release(st)

            def pc(st):
                first = {"cq": 10, "ck": 12, "cv": 14, "dq": 16, "dk": 18, "dv": 20}[st.what]
                project(st, ("w", first + st.p), st.what[1] == "v")

            def small_project(st, w, n):
                job = st.jobs[0]
                pe.wait_ge(params_loaded, reach("params_loaded", 16))
                pe.wait_ge(bank_taken[job.bank], turn_at(job))
                for t in range(T):
                    for k in range(KB):
                        ins = mm(PS[:, job.bank, t * n:(t + 1) * n], XT[:, k, t * P:(t + 1) * P], w[:, k, :],
                                 k == 0, k == KB - 1)
                        if (t, k) == (T - 1, KB - 1):
                            ins.then_inc(bank_full[job.bank], 1)

            def pf(st):
                small_project(st, prm("wf", 1, KB), 8)

            def cum(st):
                job = st.jobs[0]
                pe.wait_ge(log_forget_ready, reach("log_forget_ready", 1))
                pe.wait_ge(bank_taken[job.bank], turn_at(job))
                for t in range(T):
                    ins = mm(PS[0:8, job.bank, 0:S], LF[:, t, :], cst("tri", 1, T)[:, t, :], t == 0, t == T - 1)
                    if t == T - 1:
                        ins.then_inc(bank_full[job.bank], 1)

            def pa(st):
                c_, x_ = weights(("w", 2 + st.p), KB), weights(("w", 4 + st.p), KB)
                for c, job in enumerate(st.jobs):
                    pe.wait_ge(bank_taken[job.bank], turn_at(job))
                    cols_product(job.bank, 0, c_, c, XT, KB)
                    cols_product(job.bank, S, x_, c, XT, KB).then_inc(bank_full[job.bank], 1)
                release(st)

            def conva(st):
                for p, job in enumerate(st.jobs):
                    b_ = weights(("w", p), KB)
                    pe.wait_ge(bank_taken[job.bank], turn_at(job))
                    cols_product(job.bank, 0, b_, 0, XT, KB)
                    cols_product(job.bank, S, b_, 1, XT, KB).then_inc(bank_full[job.bank], 1)
                release(st)

            def score(st):
                job, e = st.jobs[0], st.e
                b = job.bank
                if st.br == "c":
                    h = e // 2
                    q, k = CQ[:, h, :], CK[:, h, e % 2, :]
                    if e % 4 == 0:
                        ready = named(("cq", h // 2)).jobs[0]
                        pe.wait_ge(bank_taken[ready.bank], taken_at(ready))
                        ready = named(("ck", h // 2)).jobs[0]
                        pe.wait_ge(bank_taken[ready.bank], taken_at(ready))
                elif st.br == "d":
                    q, k = DQ[:, e // 2, :], DK[:, e // 2, e % 2, :]
                    if e % 4 == 0:
                        ready = named(("dq", e // 4)).jobs[0]
                        pe.wait_ge(bank_taken[ready.bank], taken_at(ready))
                        ready = named(("dk", e // 4)).jobs[0]
                        pe.wait_ge(bank_taken[ready.bank], taken_at(ready))
                    if e == 0:
                        ready = named("cum").jobs[0]
                        pe.wait_ge(bank_taken[ready.bank], taken_at(ready))
                else:
                    g = e // 4
                    blk_ = (g // 2) * 4 + e % 4
                    rows = slice(64 * (g % 2), 64 * (g % 2) + 64)
                    q, k = QA[rows, blk_, :], KA[rows, g, :]
                    if e % 2 == 0:
                        ready = named(("pq", blk_ // 2)).jobs[0]
                        pe.wait_ge(bank_taken[ready.bank], taken_at(ready))
                    if e == 0:
                        ready = named("pk").jobs[0]
                        pe.wait_ge(bank_taken[ready.bank], taken_at(ready))
                pe.wait_ge(bank_taken[job.bank], turn_at(job))
                for t in range(T):
                    dst = PS[:, b, 0:P] if t == 0 else PS[:, b, P:P + S]
                    keys = (t + 1) * P
                    extra = st.br == "d"
                    ins = mm(dst, q[:, t * P:(t + 1) * P], k[:, 0:keys], True, not extra)
                    if extra:
                        ins = mm(dst, cst("sel", 1, 8)[:, e, :], NC[:, 0:keys], False, True)
                ins.then_inc(bank_full[b], 1)

            def turn_(st):
                job = st.jobs[0]
                b = job.bank
                e = 2 * st.h if st.br == "c" else st.h
                if st.br == "c":
                    pe.wait_ge(probs_combined, reach("probs_combined", named(("diff", st.h)).at["probs_combined"]))
                else:
                    pe.wait_ge(probs_ready, reach("probs_ready", named(("score", st.br, e)).at["probs_ready"]))
                pe.wait_ge(bank_taken[job.bank], turn_at(job))
                for n in range(3):
                    ins = transpose(PS[:, b, n * P:(n + 1) * P], EX[:, e % 4, n * P:(n + 1) * P])
                    if n == 2:
                        ins.then_inc(bank_full[b], 1)

            def out_open(st):
                for job in st.jobs:
                    pe.wait_ge(bank_taken[job.bank], turn_at(job))

            def value(st):
                h = st.h
                ready = named(("turn", st.br, h)).jobs[0]
                pe.wait_ge(bank_taken[ready.bank], taken_at(ready))
                pt = PT[:, st.at["values_summed"] % 3, :]
                if st.br == "c":
                    v, c, w = [CV[:, t, h * P:(h + 1) * P] for t in range(T)], h * P, P
                    if h % 2 == 0:
                        ready = named(("cv", h // 2)).jobs[0]
                        pe.wait_ge(bank_taken[ready.bank], taken_at(ready))
                elif st.br == "d":
                    v, c, w = [DV[:, t, h * 64:(h + 1) * 64] for t in range(T)], h * 64, 64
                    if h % 4 == 0:
                        ready = named(("dv", h // 4)).jobs[0]
                        pe.wait_ge(bank_taken[ready.bank], taken_at(ready))
                else:
                    g = h // 4
                    v, c, w = [VA[:, t, g * 64:(g + 1) * 64] for t in range(T)], (h % 8) * 64, 64
                    if h == 0:
                        ready = named("pv").jobs[0]
                        pe.wait_ge(bank_taken[ready.bank], taken_at(ready))
                mm(PS[:, 6, c:c + w], pt[:, 0:P], v[0])
                mm(PS[:, 7, c:c + w], pt[:, P:2 * P], v[0], True, False)
                mm(PS[:, 7, c:c + w], pt[:, 2 * P:3 * P], v[1], False, True).then_inc(values_summed, 1)

            def out_turn(st):
                for job in named(("oo", st.half if st.br == "a" else st.br)).jobs:
                    pe.wait_ge(bank_taken[job.bank], taken_at(job))
                for p, job in enumerate(st.jobs):
                    pe.wait_ge(bank_taken[job.bank], turn_at(job))
                    for n in range(4):
                        c, t = 2 * p + n // 2, n % 2
                        ins = transpose(PS[:, job.bank, n * P:(n + 1) * P], ON[:, t, c * P:(c + 1) * P])
                        if n == 3:
                            ins.then_inc(bank_full[job.bank], 1)

            def lnb1(st):
                pe.wait_ge(conv_b_ready, reach("conv_b_ready", 1))
                for t, job in enumerate(st.jobs):
                    pe.wait_ge(bank_taken[job.bank], turn_at(job))
                    for c in range(4):
                        ins = transpose(PS[:, job.bank, c * P:(c + 1) * P], ACCB[:, c, t * P:(t + 1) * P])
                        if c == 3:
                            ins.then_inc(bank_full[job.bank], 1)

            def lnb3(st):
                assert [job.bank for job in st.jobs] == [job.bank for job in named("lnb1").jobs]
                for job in st.jobs:
                    pe.wait_ge(bank_taken[job.bank], turn_at(job))
                for p, job in enumerate(st.jobs):
                    for n in range(4):
                        c, t = 2 * p + n // 2, n % 2
                        ins = transpose(PS[:, job.bank, n * P:(n + 1) * P], BN[:, t, c * P:(c + 1) * P])
                        if n == 3:
                            ins.then_inc(bank_full[job.bank], 1)

            def gy(st):
                job, i, k = st.jobs[0], st.i, st.k
                g = weights(("w", 22 + 4 * i + k // 2), KB)
                pe.wait_ge(bank_taken[job.bank], turn_at(job))
                cols_product(job.bank, 0, g, k % 2, XT, KB)
                if k == 0:
                    if now.blk == 1 and i == 0:
                        pe.wait_ge(branch_a_ready, reach("branch_a_ready", 1))
                    elif now.blk == 1:
                        for j2 in named({1: "lnb3", 2: ("ot", "c"), 3: ("ot", "d")}[i]).jobs:
                            pe.wait_ge(bank_taken[j2.bank], taken_at(j2))
                    elif i == 0:
                        for j2 in named(("ot", 1)).jobs:
                            pe.wait_ge(bank_taken[j2.bank], taken_at(j2))
                    else:
                        ready = named(("dot", NH_B - 1)).jobs[0]
                        pe.wait_ge(bank_taken[ready.bank], taken_at(ready))
                if now.blk == 1:
                    o = weights(("o", i, k // 4), 4)
                    cols_product(job.bank, S, o, k % 4, Y1[i], 4).then_inc(bank_full[job.bank], 1)
                else:
                    o = weights(("o", i, k // 2), KB)
                    cols_product(job.bank, S, o, k % 2, YA if i == 0 else YBB, KB).then_inc(bank_full[job.bank], 1)
                release(st)

            def wo(st):
                w = weights(("wo", st.k // 2), 2)
                ready = named(st.src[0]).jobs[0]
                pe.wait_ge(bank_taken[ready.bank], taken_at(ready))
                rows_product(st, w, st.k % 2, MG[:, st.k, :], named(("acc", 1)).jobs, st.k == 0, st.k == KB - 1)
                release(st)
                if st.k == KB - 1:
                    flush()

            def ps(st):
                wait_xt(1)
                small_project(st, prm("ws", 2, KB), 16)

            def pconv(st):
                project(st, ("w", 6 + 4 * st.w + st.hp))

            def cumg(st):
                job = st.jobs[0]
                b = job.bank
                pe.wait_ge(log_decay_ready, reach("log_decay_ready", 1))
                pe.wait_ge(bank_taken[job.bank], turn_at(job))
                tri = cst("tri", 2)
                gg = GG.rearrange("p a b -> p (a b)")
                mm(PS[:, b, 0:16], tri, gg)
                mm(PS[:, b, 16:32], cst("ones", 2), gg)
                for t in range(T):
                    ins = mm(PS[0:8, b, 64 + t * P:64 + (t + 1) * P], GG[:, t, :], tri)
                    if t == T - 1:
                        ins.then_inc(bank_full[b], 1)

            def dtr(st):
                h, i, j1, j2 = st.h, st.h % 2, st.jobs[0], st.jobs[1]
                hp, c = h // 2, h % 2
                pe.wait_ge(conv_silu_ready, reach("conv_silu_ready", named(("pconv", hp, 2)).at["conv_silu_ready"]))
                pe.wait_ge(bank_taken[j1.bank], turn_at(j1))
                pe.wait_ge(bank_taken[j2.bank], turn_at(j2))
                for w, job, at in ((0, j1, 0), (2, j1, 2), (1, j2, 0)):
                    for t in range(T):
                        ins = transpose(PS[:, job.bank, (at + t) * P:(at + t + 1) * P],
                                        CO[:, hp % 2, 2 * w + c, t * P:(t + 1) * P])
                        if t == 1 and w > 0:
                            ins.then_inc(bank_full[job.bank], 1)

            def dtf(st):
                h, i = st.h, st.h % 2
                tr = named(("dtr", h)).jobs
                j1, j2 = st.jobs
                ready = tr[0]
                pe.wait_ge(bank_taken[ready.bank], taken_at(ready))
                ready = tr[1]
                pe.wait_ge(bank_taken[ready.bank], taken_at(ready))
                pe.wait_ge(bank_taken[j1.bank], turn_at(j1))
                for n, src in enumerate((TM[:, i, 4, :], TM[:, i, 0, :], TM[:, i, 5, :], TM[:, i, 1, :])):
                    ins = transpose(PS[:, j1.bank, n * P:(n + 1) * P], src)
                    if n == 3:
                        ins.then_inc(bank_full[j1.bank], 1)
                pe.wait_ge(bank_taken[j2.bank], turn_at(j2))
                for n, src in enumerate((TM[:, i, 2, :], TM[:, i, 3, :], TM[:, i, 8, :])):
                    ins = transpose(PS[:, j2.bank, n * P:(n + 1) * P], src)
                    if n == 2:
                        ins.then_inc(bank_full[j2.bank], 1)

            def ddc(st):
                job = st.jobs[0]
                if st.h == 0:
                    ready = named("cumg").jobs[0]
                    pe.wait_ge(bank_taken[ready.bank], taken_at(ready))
                pe.wait_ge(bank_taken[job.bank], turn_at(job))
                mm(PS[:, job.bank, 0:S], cst("sel", 2, 8)[:, st.h, :], GTR[:, :]).then_inc(bank_full[job.bank], 1)

            def dkk(st):
                job, i = st.jobs[0], st.h % 2
                for j2 in named(("dtf", st.h)).jobs:
                    if j2.bank != job.bank:
                        pe.wait_ge(bank_taken[j2.bank], taken_at(j2))
                pe.wait_ge(bank_taken[job.bank], turn_at(job))
                for t in range(T):
                    ins = mm(PS[:, job.bank, t * S:(t + 1) * S], FBM[:, i, t, :],
                             FA[:, i, 2 * t:2 * t + 2, :].rearrange("p a b -> p (a b)"))
                    if t == 1:
                        ins.then_inc(bank_full[job.bank], 1)

            def dl0(st):
                job, i = st.jobs[0], st.h % 2
                pe.wait_ge(level_masked, reach("level_masked", st.at["level_masked"]))
                pe.wait_ge(bank_taken[job.bank], turn_at(job))
                for t in range(T):
                    ins = mm(PS[:, job.bank, t * P:(t + 1) * P], MT[:, i, t, :], IDENT)
                    if t == 1:
                        ins.then_inc(bank_full[job.bank], 1)

            def dla(st):
                job, i, s = st.jobs[0], st.h % 2, st.s
                pe.wait_ge(level_masked, reach("level_masked", st.at["level_masked"]))
                ready = named(("dlb", st.h, s - 1) if s > 1 else ("dl0", st.h)).jobs[0]
                pe.wait_ge(bank_taken[ready.bank], taken_at(ready))
                pe.wait_ge(bank_taken[job.bank], turn_at(job))
                for t in range(T):
                    ins = mm(PS[:, job.bank, t * P:(t + 1) * P], MT[:, i, t, :], TT[:, i, t, :])
                    if t == 1:
                        ins.then_inc(bank_full[job.bank], 1)

            def dlb(st):
                job, i, s = st.jobs[0], st.h % 2, st.s
                ready = named(("dla", st.h, s)).jobs[0]
                pe.wait_ge(bank_taken[ready.bank], taken_at(ready))
                pe.wait_ge(bank_taken[job.bank], turn_at(job))
                b = job.bank
                if s < LEVELS - 1:
                    for t in range(T):
                        mm(PS[:, b, t * P:(t + 1) * P], TT[:, i, 2 + t, :], P1S[:, i, t, :])
                for t in range(T):
                    ins = mm(PS[:, b, S + t * P:S + (t + 1) * P], P1S[:, i, t, :], TT[:, i, 2 + t, :])
                    if t == 1:
                        ins.then_inc(bank_full[b], 1)

            def du1(st):
                job, i = st.jobs[0], st.h % 2
                b = job.bank
                ready = named(("dlb", st.h, LEVELS - 1)).jobs[0]
                pe.wait_ge(bank_taken[ready.bank], taken_at(ready))
                pe.wait_ge(bank_taken[job.bank], turn_at(job))
                mm(PS[:, b, 0:P], TT[:, i, 2, :], TM[:, i, 9, :])
                mm(PS[:, b, P:S], TM[:, i, 7, :], TT[:, i, 3, :]).then_inc(bank_full[b], 1)

            def du2(st):
                job, i = st.jobs[0], st.h % 2
                ready = named(("du1", st.h)).jobs[0]
                pe.wait_ge(bank_taken[ready.bank], taken_at(ready))
                pe.wait_ge(bank_taken[job.bank], turn_at(job))
                mm(PS[:, job.bank, 0:P], TM[:, i, 6, :], VW[:, i, 0, :]).then_inc(bank_full[job.bank], 1)

            def du3(st):
                job, i = st.jobs[0], st.h % 2
                ready = named(("du2", st.h)).jobs[0]
                pe.wait_ge(bank_taken[ready.bank], taken_at(ready))
                pe.wait_ge(bank_taken[job.bank], turn_at(job))
                mm(PS[:, job.bank, 0:P], TT[:, i, 3, :], TM[:, i, 10, :], True, False)
                mm(PS[:, job.bank, 0:P], VW[:, i, 1, :], VS[:, i, 0, :], False, True).then_inc(bank_full[job.bank], 1)

            def du4(st):
                job, i = st.jobs[0], st.h % 2
                b = job.bank
                ready = named(("du3", st.h)).jobs[0]
                pe.wait_ge(bank_taken[ready.bank], taken_at(ready))
                pe.wait_ge(bank_taken[job.bank], turn_at(job))
                mm(PS[:, b, 0:P], AL[:, i, 1, :], VW[:, i, 0, :])
                mm(PS[:, b, P:S], FBM[:, i, 2, :], VS[:, i, 0, :], True, False)
                mm(PS[:, b, P:S], AL[:, i, 3, :], VS[:, i, 1, :], False, True).then_inc(bank_full[b], 1)

            def dot(st):
                job, i = st.jobs[0], st.h % 2
                ready = named(("du4", st.h)).jobs[0]
                pe.wait_ge(bank_taken[ready.bank], taken_at(ready))
                pe.wait_ge(bank_taken[job.bank], turn_at(job))
                for t in range(T):
                    ins = transpose(PS[:, job.bank, t * P:(t + 1) * P], OD[:, i, t, :])
                    if t == 1:
                        ins.then_inc(bank_full[job.bank], 1)

            pe.drain().then_inc(slots_free, SLOTS)
            for b in range(8):
                pe.drain().then_inc(bank_taken[b], 1)
            pe.wait_ge(con_loaded, 16)
            pe.wait_ge(zeros_set, 1)
            walk(pe, {"xt": xt, "acc": acc, "gu": gu, "down": down, "pb": pb, "pc": pc, "pf": pf, "cum": cum,
                      "pa": pa, "conva": conva, "score": score, "turn": turn_, "out_open": out_open,
                      "value": value, "out_turn": out_turn, "lnb1": lnb1, "lnb3": lnb3, "gy": gy, "wo": wo}, 1)
            loaded.clear()
            pe.wait_ge(con_loaded, 16 * 5)
            now.blk, now.l = 2, 0
            pe.wait_ge(bank_taken[0], reach(("taken", 0), 0))
            pe.matmul(PS[0:NH_A, 0, 0:384], ZS[0:32, 2, 0:NH_A],
                      ZS[0:32, 0:2, :].rearrange("p a b -> p (a b)")[:, 0:384], start=True, stop=True
                      ).then_inc(prologue_row, 1)
            pe.wait_ge(prologue_done, 1)
            pe.wait_ge(zeros_set, 2)
            walk(pe, {"xt": xt, "acc": acc, "gu": gu, "down": down, "score": score, "turn": turn_,
                      "out_open": out_open, "value": value, "out_turn": out_turn, "gy": gy, "wo": wo, "ps": ps,
                      "pk": lambda st: project(st, ("w", 4)), "pq": lambda st: project(st, ("w", st.p)),
                      "pv": lambda st: project(st, ("w", 5), True), "pz": lambda st: project(st, ("w", 18 + st.p)),
                      "pconv": pconv, "cumg": cumg, "dtr": dtr, "dtf": dtf, "ddc": ddc, "dkk": dkk, "dl0": dl0,
                      "dla": dla, "dlb": dlb, "du1": du1, "du2": du2, "du3": du3, "du4": du4, "dot": dot}, 2)

        @block.scalar
        def _(act):
            def copy(dst, src, scale=1.0):
                return act.activation(dst, src, ACT.Copy, scale=scale)

            def norm(st):
                act.wait_ge(residual_ready, reach("residual_ready", 2 * st.s))
                for t in range(T):
                    last = act.activation(XN[:, t, :], H[:, t, :], ACT.Square, scale=D ** -0.5,
                                          accum_out=SS[:, t:t + 1])
                last.then_inc(squares_summed, 1)

            def xt(st):
                act.wait_ge(params_loaded, reach("params_loaded", 16))
                for k2, job in enumerate(st.jobs):
                    if k2 % 2:
                        continue
                    act.wait_ge(bank_full[job.bank], full_at(job))
                    b = job.bank
                    if now.blk == 1:
                        g = prm(f"g{st.s}", 1)
                        for kk in range(2):
                            k = 2 * k2 + kk
                            last = copy(XT[:, k, :], PS[:, b, kk * S:(kk + 1) * S], g[:, k:k + 1])
                    else:
                        last = copy(XT[:, 2 * k2:2 * k2 + 2, :].rearrange("p a b -> p (a b)"), PS[:, b, :])
                    last.then_inc(bank_taken[b], 1)

            def gu(st):
                job = st.jobs[0]
                act.wait_ge(bank_full[job.bank], full_at(job))
                if st.j >= 2:
                    ready = named(("gu", st.s, st.j - 2)).jobs[0]
                    act.wait_ge(bank_taken[ready.bank], taken_at(ready))
                act.activation(SG[:, st.j % 2, :], PS[:, job.bank, 0:S], ACT.Silu).then_inc(gate_silu_ready, 1)

            def post(st):
                for t in range(T):
                    j0, j1 = st.acc.jobs[2 * t], st.acc.jobs[2 * t + 1]
                    act.wait_ge(bank_full[j0.bank], full_at(j0))
                    act.wait_ge(bank_full[j1.bank], full_at(j1))
                    act.activation(XN[:, t, :], PS[:, j0.bank:j0.bank + 2, :].rearrange("p a b -> p (a b)"),
                                   ACT.Square, scale=st.root, accum_out=SS[:, 2 + t:3 + t]).then_inc(squares_summed, 1)

            def lam(st):
                act.wait_ge(lambda_dots, reach("lambda_dots", 1))
                act.activation(ELAM[:, :], LAM[:, :], ACT.Exp).then_inc(lambda_exps, 1)

            def pb(st):
                for c, job in enumerate(st.jobs):
                    act.wait_ge(bank_full[job.bank], full_at(job))
                    if st.p:
                        ready = named(("pb", st.p - 1)).jobs[c]
                        act.wait_ge(bank_taken[ready.bank], taken_at(ready))
                    act.activation(TH[:, c, 0:S], PS[:, job.bank, S:2 * S], ACT.Tanh, scale=0.5
                                   ).then_inc(branch_gate_ready, 1)

            def pc(st):
                job, p = st.jobs[0], st.p
                act.wait_ge(bank_full[job.bank], full_at(job))
                src = PS[:, job.bank, :].rearrange("p (a b) -> p a b", a=2)
                if st.what in ("cq", "dq"):
                    dst = CQ if st.what == "cq" else DQ
                    last = copy(dst[:, 2 * p:2 * p + 2, :], src)
                elif st.what in ("ck", "dk"):
                    dst = CK if st.what == "ck" else DK
                    for m in range(2):
                        rows = slice(64 * m, 64 * m + 64)
                        last = copy(dst[rows, 2 * p:2 * p + 2, m, :], src[rows])
                else:
                    dst = CV if st.what == "cv" else DV
                    last = copy(dst[:, :, p * S:(p + 1) * S], src)
                last.then_inc(bank_taken[job.bank], 1)

            def pf(st):
                ready = st.jobs[0]
                act.wait_ge(bank_taken[ready.bank], taken_at(ready))
                act.activation(ZA_[:, :, :], ZF[:, :, :], ACT.Abs)
                act.drain()
                act.activation(ZA_[:, :, :], ZA_[:, :, :], ACT.Exp, scale=-1.0)
                act.drain()
                act.activation(ZL[:, :, :], ZA_[:, :, :], ACT.Ln, bias=1.0).then_inc(forget_log_ready, 1)

            def cum(st):
                job = st.jobs[0]
                act.wait_ge(bank_full[job.bank], full_at(job))
                copy(NC[0:8, :], PS[0:8, job.bank, 0:S], -1.0 / QK_SCALE).then_inc(bank_taken[job.bank], 1)

            def pa(st):
                for c, job in enumerate(st.jobs):
                    act.wait_ge(bank_full[job.bank], full_at(job))
                    if st.p:
                        ready = named(("pa", st.p - 1)).jobs[c]
                        act.wait_ge(bank_taken[ready.bank], taken_at(ready))
                    copy(TH[:, c, 0:S], PS[:, job.bank, 0:S]).then_inc(branch_gate_ready, 1)

            def score(st):
                e = st.e
                ready = st.jobs[0]
                act.wait_ge(bank_taken[ready.bank], taken_at(ready))
                ls = LS[:, e % 16, :]
                act.activation(EX[:, e % 4, 0:P], EX[:, e % 4, 0:P], ACT.Exp, bias=NM[:, e % 4, 0:1],
                               scale=QK_SCALE, accum_out=ls[:, 0:1])
                act.activation(EX[:, e % 4, P:384], EX[:, e % 4, P:384], ACT.Exp, bias=NM[:, e % 4, 1:2],
                               scale=QK_SCALE, accum_out=ls[:, 1:2]).then_inc(probs_ready, 1)
                if st.br == "a":
                    act.activation(ES[:, e, :], NM[:, e % 4, :], ACT.Exp, bias=prm("sink", 2)[:, e:e + 1]
                                   ).then_inc(sink_exp_ready, 1)

            def turn_(st):
                job = st.jobs[0]
                n = named(("value", st.br, st.h)).at["values_summed"]
                act.wait_ge(bank_full[job.bank], full_at(job))
                if n > 3:
                    act.wait_ge(values_summed, reach("values_summed", n - 3))
                copy(PT[:, n % 3, :], PS[:, job.bank, 0:384]).then_inc(bank_taken[job.bank], 1)

            def out_norm(st):
                if st.br != "c":
                    return
                act.wait_ge(values_summed, reach("values_summed", named(("value", "c", NH_C - 1)).at["values_summed"]))
                for t in range(T):
                    for h in range(NH_C):
                        last = act.activation(JUNK[:, :], PS[:, 6 + t, h * P:(h + 1) * P], ACT.Square,
                                              scale=P ** -0.5, accum_out=SSO[:, t * 4 + h:t * 4 + h + 1])
                        if (t, h) != (T - 1, NH_C - 1):
                            act.drain()
                last.then_inc(out_squares_summed, 1)

            def out_turn(st):
                for p, job in enumerate(st.jobs):
                    act.wait_ge(bank_full[job.bank], full_at(job))
                    c = 2 * p + (4 * st.half if st.br == "a" else 0)
                    dst = {"a": YA, "c": YC, "d": YD}[st.br][:, c:c + 2, :].rearrange("p a b -> p (a b)")
                    copy(dst, PS[:, job.bank, :], SUBG[:, 0:1] if st.br == "c" else 1.0
                         ).then_inc(bank_taken[job.bank], 1)

            def lnb3(st):
                for p, job in enumerate(st.jobs):
                    act.wait_ge(bank_full[job.bank], full_at(job))
                    for n in range(2):
                        c = 2 * p + n
                        last = act.activation(YB1[:, c, :], PS[:, job.bank, n * S:(n + 1) * S], ACT.Silu,
                                              bias=prm("blb", 1)[:, c:c + 1], scale=prm("blg", 1)[:, c:c + 1])
                    last.then_inc(bank_taken[job.bank], 1)

            def gy(st):
                job, k = st.jobs[0], st.k
                act.wait_ge(bank_full[job.bank], full_at(job))
                n = st.i * KB + k
                if n >= 2:
                    ready = named(("gy", (n - 2) // KB, (n - 2) % KB)).jobs[0]
                    act.wait_ge(bank_taken[ready.bank], taken_at(ready))
                act.activation(TH[:, n % 2, 0:S], PS[:, job.bank, 0:S], ACT.Tanh, scale=0.5).then_inc(gate_tanh_ready, 1)

            def ps(st):
                ready = st.jobs[0]
                act.wait_ge(bank_taken[ready.bank], taken_at(ready))
                act.activation(BETA[:, :, :], SBT[:, :, 0:8], ACT.Tanh, scale=0.5)
                act.activation(EAL[:, :], prm("alog", 2), ACT.Exp)
                act.activation(ZA_[:, :, :], SBT[:, :, 8:16], ACT.Abs)
                act.drain()
                act.activation(ZA_[:, :, :], ZA_[:, :, :], ACT.Exp, scale=-1.0)
                act.drain()
                act.activation(ZL[:, :, :], ZA_[:, :, :], ACT.Ln, bias=1.0).then_inc(small_logs_ready, 1)

            def pk(st):
                job = st.jobs[0]
                act.wait_ge(bank_full[job.bank], full_at(job))
                src = PS[:, job.bank, :].rearrange("p (a b) -> p a b", a=2)
                for m in range(2):
                    rows = slice(64 * m, 64 * m + 64)
                    for c in range(2):
                        last = copy(KA[rows, 2 * c + m, :], src[rows, c, :])
                last.then_inc(bank_taken[job.bank], 1)

            def pq(st):
                job = st.jobs[0]
                act.wait_ge(bank_full[job.bank], full_at(job))
                copy(QA[:, 2 * st.p:2 * st.p + 2, :].rearrange("p a b -> p (a b)"), PS[:, job.bank, :]
                     ).then_inc(bank_taken[job.bank], 1)

            def pv(st):
                job = st.jobs[0]
                act.wait_ge(bank_full[job.bank], full_at(job))
                copy(VA[:, :, :].rearrange("p a b -> p (a b)"), PS[:, job.bank, :]).then_inc(bank_taken[job.bank], 1)

            def cumg(st):
                act.wait_ge(decay_diff_ready, reach("decay_diff_ready", 1))
                act.activation(ET[:, :, :], ET[:, :, :], ACT.Exp)
                act.activation(EG[:, :, :], G[:, :, :], ACT.Exp).then_inc(decay_exps_ready, 1)

            def pz(st):
                job = st.jobs[0]
                act.wait_ge(bank_full[job.bank], full_at(job))
                if st.p >= 2:
                    ready = named(("pz", st.p - 2)).jobs[0]
                    act.wait_ge(bank_taken[ready.bank], taken_at(ready))
                act.activation(TH[:, st.p % 2, :], PS[:, job.bank, :], ACT.Tanh, scale=0.5).then_inc(z_tanh_ready, 1)

            def pconv(st):
                act.wait_ge(conv_ready, reach("conv_ready", st.at["conv_ready"]))
                if st.at["conv_silu_ready"] > 1:
                    act.wait_ge(conv_silu_ready, reach("conv_silu_ready", st.at["conv_silu_ready"] - 1))
                co = CO[:, st.hp % 2, 2 * st.w:2 * st.w + 2, :].rearrange("p a b -> p (a b)")
                act.activation(TC[:, :], co, ACT.Tanh, scale=0.5).then_inc(conv_tanh_ready, 1)

            def dtr(st):
                i = st.h % 2
                done = st.jobs[0]
                act.wait_ge(bank_full[done.bank], full_at(done))
                done = st.jobs[1]
                act.wait_ge(bank_full[done.bank], full_at(done))
                if st.h >= 2:
                    act.wait_ge(qk_rsqrt_ready, reach("qk_rsqrt_ready", named(("dtr", st.h - 2)).at["qk_rsqrt_ready"]))
                for n in range(4):
                    b = st.jobs[n // 2].bank
                    last = act.activation(P1S[:, i, 0, :], PS[:, b, n % 2 * P:(n % 2 + 1) * P], ACT.Square,
                                          accum_out=SSD[:, i, n:n + 1])
                    if n < 3:
                        act.drain()
                last.then_inc(qk_squares_summed, 1)

            def dte(st):
                i, h = st.h % 2, st.h
                b = named(("dtr", h)).jobs[0].bank
                act.wait_ge(head_scalars_ready, reach("head_scalars_ready", st.at["head_scalars_ready"]))
                sc = SC[:, i, :]
                for n, src, scale in ((0, 0, sc[:, 0:1]), (1, 1, sc[:, 1:2]), (8, 1, sc[:, 8:9]),
                                      (9, 2, HB[:, 0, h:h + 1]), (10, 3, HB[:, 1, h:h + 1])):
                    last = copy(TM[:, i, n, :], PS[:, b, src * P:(src + 1) * P], scale)
                last.then_inc(bank_taken[b], 1)

            def dtf(st):
                job = st.jobs[0]
                act.wait_ge(bank_full[job.bank], full_at(job))
                copy(FA[:, st.h % 2].rearrange("p a b -> p (a b)"), PS[:, job.bank, :]
                     ).then_inc(bank_taken[job.bank], 1)

            def ddc(st):
                i = st.h % 2
                ready = st.jobs[0]
                act.wait_ge(bank_taken[ready.bank], taken_at(ready))
                if st.h >= 2:
                    ready = named(("dkk", st.h - 2)).jobs[0]
                    act.wait_ge(bank_taken[ready.bank], taken_at(ready))
                act.activation(DEC[:, i].rearrange("p (t k) n -> p t k n", t=T)[:, :, 1, :], DD[:, i], ACT.Exp
                               ).then_inc(decay_ready, 1)

            def dla(st):
                job = st.jobs[0]
                act.wait_ge(bank_full[job.bank], full_at(job))
                copy(P1S[:, st.h % 2].rearrange("p a b -> p (a b)"), PS[:, job.bank, 0:S]
                     ).then_inc(bank_taken[job.bank], 1)

            def evac(dst, n):
                def run(st):
                    job, i = st.jobs[0], st.h % 2
                    act.wait_ge(bank_full[job.bank], full_at(job))
                    copy(dst(i), PS[:, job.bank, 0:n]).then_inc(bank_taken[job.bank], 1)
                return run

            def du4(st):
                job, i = st.jobs[0], st.h % 2
                act.wait_ge(bank_full[job.bank], full_at(job))
                for t in range(T):
                    last = act.activation(P1S[:, i, t, :], PS[:, job.bank, t * P:(t + 1) * P], ACT.Square,
                                          scale=P ** -0.5, accum_out=SSO[:, 2 * i + t:2 * i + t + 1])
                last.then_inc(out_squares_summed, 1)

            act.wait_ge(x_loaded, 16)
            act.wait_ge(zeros_set, 1)
            walk(act, {"norm": norm, "xt": xt, "gu": gu, "post": post, "lam": lam, "pb": pb, "pc": pc, "pf": pf,
                       "cum": cum, "pa": pa, "score": score, "turn": turn_, "out_norm": out_norm,
                       "out_turn": out_turn, "lnb3": lnb3, "gy": gy}, 1)
            now.blk, now.l = 2, 0
            act.wait_ge(residual_ready, reach("residual_ready", 0))
            act.wait_ge(zeros_set, 2)
            walk(act, {"xt": xt, "gu": gu, "score": score, "turn": turn_, "out_turn": out_turn, "gy": gy, "ps": ps,
                       "pk": pk, "pq": pq, "pv": pv, "cumg": cumg, "pz": pz, "pconv": pconv, "dtr": dtr, "dte": dte,
                       "dtf": dtf, "ddc": ddc, "dla": dla,
                       "du1": evac(lambda i: VW[:, i].rearrange("p a b -> p (a b)"), S),
                       "du2": evac(lambda i: VS[:, i, 0, :], P), "du3": evac(lambda i: VS[:, i, 1, :], P),
                       "du4": du4}, 2)

        @block.vector
        def _(dve):
            def norm(st):
                dve.wait_ge(rsqrt_ready, reach("rsqrt_ready", st.at["rsqrt_ready"]))
                for t in range(T):
                    last = dve.tensor_scalar(XN[:, t, :], H[:, t, :], RS[:, t:t + 1], None, ALU.mult)
                last.then_inc(normed_ready, 1)

            def xt(st):
                dve.wait_ge(params_loaded, reach("params_loaded", 16))
                for k2, job in enumerate(st.jobs):
                    if k2 % 2 == 0:
                        continue
                    dve.wait_ge(bank_full[job.bank], full_at(job))
                    b = job.bank
                    if now.blk == 1:
                        g = prm(f"g{st.s}", 1)
                        for kk in range(2):
                            k = 2 * k2 + kk
                            last = dve.tensor_scalar(XT[:, k, :], PS[:, b, kk * S:(kk + 1) * S], g[:, k:k + 1],
                                                     None, ALU.mult)
                    else:
                        last = dve.tensor_copy(XT[:, 2 * k2:2 * k2 + 2, :].rearrange("p a b -> p (a b)"), PS[:, b, :])
                    last.then_inc(bank_taken[b], 1)

            def gu(st):
                job = st.jobs[0]
                dve.wait_ge(gate_silu_ready, reach("gate_silu_ready", st.at["gate_silu_ready"]))
                dve.tensor_tensor(HT[:, st.j % 3, :], SG[:, st.j % 2, :], PS[:, job.bank, S:2 * S], ALU.mult
                                  ).then_inc(bank_taken[job.bank], 1)

            def post(st):
                dve.wait_ge(feature_rows_loaded, reach("feature_rows_loaded", 16 * (st.s + 1)))
                for t in range(T):
                    dve.wait_ge(rsqrt_ready, reach("rsqrt_ready", st.at["rsqrt_ready"] - 1 + t))
                    for n in range(2):
                        b = st.acc.jobs[2 * t + n].bank
                        cols = slice(n * HALF, (n + 1) * HALF)
                        dve.scalar_tensor_tensor(out=XN[:, t, cols], in0=PS[:, b, :], scalar=RS[:, 2 + t:3 + t],
                                                 in1=PG[:, 0, cols], op0=ALU.mult, op1=ALU.mult
                                                 ).then_inc(bank_taken[b], 1)
                    dve.drain()
                    dve.tensor_tensor(H[:, t, :], H[:, t, :], XN[:, t, :], ALU.add).then_inc(residual_ready, 1)

            def lam(st):
                lv = prm("lam", 1, 4)
                for n in range(2):
                    last = dve.tensor_tensor_reduce(TMP[:, n, 0:64], lv[:, 2 * n, :], lv[:, 2 * n + 1, :], 1.0, 0.0,
                                                    ALU.mult, ALU.add, LAM[:, n:n + 1])
                last.then_inc(lambda_dots, 1)
                dve.tensor_scalar(BWH.rearrange("p a b -> p (a b)"), prm("bw", 1), 0.5, None, ALU.mult)
                dve.tensor_tensor(SUBG[:, :], prm("sub", 1), prm("lami", 1)[:, 1:2], ALU.mult)
                dve.wait_ge(lambda_exps, reach("lambda_exps", 1))
                dve.tensor_tensor(NLAM[:, :], ELAM[:, 1:2], ELAM[:, 0:1], ALU.subtract)
                dve.drain()
                dve.tensor_tensor(NLAM[:, :], NLAM[:, :], prm("lami", 1)[:, 0:1], ALU.subtract
                                  ).then_inc(lambda_ready, 1)
                dve.drain()

            def pb(st):
                for c, job in enumerate(st.jobs):
                    dve.wait_ge(branch_gate_ready, reach("branch_gate_ready", st.at["branch_gate_ready"] - 1 + c))
                    dve.scalar_tensor_tensor(out=ZB[:, 2 * st.p + c, :], in0=TH[:, c, 0:S], scalar=1.0,
                                             in1=PS[:, job.bank, 0:S], op0=ALU.add, op1=ALU.mult
                                             ).then_inc(bank_taken[job.bank], 1)

            def convb(st):
                for n in range(st.a, st.b):
                    tap = 30 - n
                    dve.drain()
                    for c in range(4):
                        w = BWH[:, tap, c:c + 1]
                        if n == 0:
                            last = dve.tensor_scalar(ACCB[:, c, :], ZB[:, c, :], w, prm("bb", 1)[:, c:c + 1],
                                                     ALU.mult, ALU.add)
                        else:
                            last = dve.scalar_tensor_tensor(out=ACCB[:, c, n:S], in0=ZB[:, c, 0:S - n], scalar=w,
                                                            in1=ACCB[:, c, n:S], op0=ALU.mult, op1=ALU.add)
                if st.b == 31:
                    last.then_inc(conv_b_ready, 1)

            def pf(st):
                job = st.jobs[0]
                dve.wait_ge(bank_full[job.bank], full_at(job))
                for t in range(T):
                    last = dve.tensor_tensor(ZF[:, t, :], PS[:, job.bank, t * 8:(t + 1) * 8], prm("fb", 1), ALU.add)
                last.then_inc(bank_taken[job.bank], 1)
                dve.drain()
                dve.tensor_scalar(LF[:, :, :], ZF[:, :, :], 0.0, None, ALU.min)
                dve.drain()
                dve.wait_ge(forget_log_ready, reach("forget_log_ready", 1))
                dve.tensor_tensor(LF[:, :, :], LF[:, :, :], ZL[:, :, :], ALU.subtract).then_inc(log_forget_ready, 1)

            def pa(st):
                for c, job in enumerate(st.jobs):
                    dve.wait_ge(branch_gate_ready, reach("branch_gate_ready", st.at["branch_gate_ready"] - 1 + c))
                    dve.tensor_tensor(ZA[:, 2 * st.p + c, :], TH[:, c, 0:S], PS[:, job.bank, S:2 * S], ALU.mult
                                      ).then_inc(bank_taken[job.bank], 1)

            def conva(st):
                aw = prm("aw", 1, 3)
                for n in range(3):
                    dve.drain()
                    for c in range(4):
                        w = aw[:, 2 - n, c:c + 1]
                        if n == 0:
                            dve.tensor_scalar(ACCA[:, c, :], ZA[:, c, :], w, None, ALU.mult)
                        else:
                            dve.scalar_tensor_tensor(out=ACCA[:, c, n:S], in0=ZA[:, c, 0:S - n], scalar=w,
                                                     in1=ACCA[:, c, n:S], op0=ALU.mult, op1=ALU.add)
                dve.drain()
                for p, job in enumerate(st.jobs):
                    dve.wait_ge(bank_full[job.bank], full_at(job))
                    dst = ACCA[:, 2 * p:2 * p + 2, :].rearrange("p a b -> p (a b)")
                    dve.tensor_tensor(dst, dst, PS[:, job.bank, :], ALU.mult).then_inc(bank_taken[job.bank], 1)
                dve.drain().then_inc(branch_a_ready, 1)

            def score(st):
                job, e = st.jobs[0], st.e
                b = job.bank
                dve.wait_ge(bank_full[job.bank], full_at(job))
                if e >= 4:
                    done = named(("turn", st.br, (e - 4) // (2 if st.br == "c" else 1))).jobs[0]
                    dve.wait_ge(bank_full[done.bank], full_at(done))
                    if st.br == "a":
                        dve.wait_ge(sink_exp_ready, reach("sink_exp_ready", named(("score", "a", e - 4)).at["sink_exp_ready"]))
                elif st.br == "d":
                    done = named(("turn", "c", NH_C - 1)).jobs[0]
                    dve.wait_ge(bank_full[done.bank], full_at(done))
                bias = {"c": lambda: cst("alibi", 1, NH_C)[:, e // 2, :], "d": lambda: cst("causal", 1),
                        "a": lambda: BIAS[:, e, :]}[st.br]()
                dve.memset(TOUCH[:, :], 0.0)
                dve.tensor_tensor_reduce(EX[:, e % 4, 0:P], PS[:, b, 0:P], bias[:, P:S], 1.0, -3e38, ALU.add,
                                         ALU.max, MX[:, e % 4, 0:1])
                dve.tensor_tensor_reduce(EX[:, e % 4, P:384], PS[:, b, P:384], bias, 1.0, -3e38, ALU.add,
                                         ALU.max, MX[:, e % 4, 1:2])
                dve.drain()
                if st.br == "a":
                    last = dve.tensor_scalar(NM[:, e % 4, :], MX[:, e % 4, :], SINK8[:, e:e + 1], -QK_SCALE,
                                             ALU.max, ALU.mult)
                else:
                    last = dve.tensor_scalar(NM[:, e % 4, :], MX[:, e % 4, :], -QK_SCALE, None, ALU.mult)
                last.then_inc(bank_taken[b], 1)

            def diff(st):
                h = st.h
                e0, e1 = 2 * h % 4, (2 * h + 1) % 4
                dve.drain()
                dve.wait_ge(probs_ready, reach("probs_ready", named(("score", "c", 2 * h + 1)).at["probs_ready"]))
                if h == 0:
                    dve.wait_ge(lambda_ready, reach("lambda_ready", 1))
                dve.reciprocal(RC[:, 0:4], LS[:, 2 * h:2 * h + 2, :].rearrange("p a b -> p (a b)"))
                dve.drain()
                dve.tensor_scalar(RC[:, 2:4], RC[:, 2:4], NLAM[:, 0:1], None, ALU.mult)
                parts = ((0, slice(0, P)), (1, slice(P, 384)))
                for t, c in parts:
                    dve.tensor_scalar(EX[:, e0, c], EX[:, e0, c], RC[:, t:t + 1], None, ALU.mult)
                dve.drain()
                for t, c in parts:
                    last = dve.scalar_tensor_tensor(out=EX[:, e0, c], in0=EX[:, e1, c], scalar=RC[:, 2 + t:3 + t],
                                                    in1=EX[:, e0, c], op0=ALU.mult, op1=ALU.add)
                last.then_inc(probs_combined, 1)

            def out_norm(st):
                key = st.half if st.br == "a" else st.br
                jobs = named(("oo", key)).jobs
                if st.br == "c":
                    dve.wait_ge(out_rsqrt_ready, reach("out_rsqrt_ready", st.at["out_rsqrt_ready"]))
                    n, w = 4, P
                else:
                    n, w = 8, 64
                    first = 8 * st.half if st.br == "a" else 0
                    dve.wait_ge(values_summed, reach("values_summed", named(("value", st.br, first + 7)).at["values_summed"]))
                    if st.br == "a":
                        dve.wait_ge(sink_exp_ready, reach("sink_exp_ready", named(("score", "a", first + 7)).at["sink_exp_ready"]))
                        ls = LS[:, first:first + 8, :]
                        dve.tensor_tensor(ls, ls, ES[:, first:first + 8, :], ALU.add)
                        dve.drain()
                    dve.reciprocal(RL[:, first:first + 8, :], LS[:, first:first + 8, :])
                    dve.drain()
                    before = {"d": ("ot", "c"), "a": ("ot", 0)}[st.br]
                    if not (st.br == "a" and st.half == 0):
                        for job in named(before).jobs:
                            dve.wait_ge(bank_full[job.bank], full_at(job))
                for t in range(T):
                    if st.br == "c":
                        r = RSO[:, t * 4:t * 4 + 4].unsqueeze(2)
                    else:
                        r = RL[:, first:first + 8, t].unsqueeze(2)
                    dve.tensor_tensor(ON[:, t, :].rearrange("p (a b) -> p a b", a=n),
                                      PS[:, 6 + t, :].rearrange("p (a b) -> p a b", a=n),
                                      r.to_broadcast([P, n, w]), ALU.mult).then_inc(bank_taken[6 + t], 1)

            def lnb1(st):
                for t, job in enumerate(st.jobs):
                    dve.wait_ge(bank_full[job.bank], full_at(job))
                    dve.bn_stats(ST[:, t, :], PS[:, job.bank, :])
                    dve.drain()
                    dve.bn_aggr(MV[:, t, :], ST[:, t, :]).then_inc(mean_var_ready, 1)
                dve.drain()
                for t, job in enumerate(st.jobs):
                    dve.wait_ge(branch_b_rsqrt_ready, reach("branch_b_rsqrt_ready", st.at["branch_b_rsqrt_ready"] - 1 + t))
                    dve.tensor_scalar(BN[:, t, :], PS[:, job.bank, :], MV[:, t, 0:1], RSB[:, t:t + 1],
                                      ALU.subtract, ALU.mult).then_inc(bank_taken[job.bank], 1)

            def gy(st):
                job, k, i = st.jobs[0], st.k, st.i
                n = i * KB + k
                dve.wait_ge(gate_tanh_ready, reach("gate_tanh_ready", st.at["gate_tanh_ready"]))
                dst = MG[:, k, :] if i == 0 else TMP[:, n % 2, :]
                ins = dve.scalar_tensor_tensor(out=dst, in0=TH[:, n % 2, 0:S], scalar=1.0,
                                               in1=PS[:, job.bank, S:2 * S], op0=ALU.add, op1=ALU.mult)
                if i:
                    dve.drain()
                    ins = dve.tensor_tensor(MG[:, k, :], MG[:, k, :], TMP[:, n % 2, :], ALU.add)
                ins.then_inc(bank_taken[job.bank], 1)

            def scale_h(st):
                for job in named(("xt", st.s)).jobs:
                    dve.wait_ge(bank_full[job.bank], full_at(job))
                dve.tensor_scalar(H[:, :, :], H[:, :, :], ALPHA, None, ALU.mult)
                if st.s == 1:
                    dve.tensor_scalar(GDH[:, :], prm("dng", 2), 0.5, None, ALU.mult)
                    dve.tensor_scalar(SINK8[:, :], prm("sink", 2), 1.0 / QK_SCALE, None, ALU.mult)
                dve.drain()

            def post2(st):
                dve.wait_ge(feature_rows_loaded, reach("feature_rows_loaded", 16 * (st.s + 1)))
                for t in range(T):
                    for n in range(2):
                        job = st.acc.jobs[2 * t + n]
                        cols = slice(n * HALF, (n + 1) * HALF)
                        dve.wait_ge(bank_full[job.bank], full_at(job))
                        dve.scalar_tensor_tensor(out=XN[:, t, cols], in0=PS[:, job.bank, :], scalar=0.5,
                                                 in1=H[:, t, cols], op0=ALU.mult, op1=ALU.add
                                                 ).then_inc(bank_taken[job.bank], 1)
                    dve.drain()
                    for n in range(2):
                        dve.bn_stats(ST[:, 2 * t + n, :], XN[:, t, n * HALF:(n + 1) * HALF])
                    dve.drain()
                    dve.bn_aggr(MV[:, t, :], ST[:, 2 * t:2 * t + 2, :]).then_inc(mean_var_ready, 1)
                dve.drain()
                for t in range(T):
                    dve.wait_ge(rsqrt_ready, reach("rsqrt_ready", st.at["rsqrt_ready"] - 1 + t))
                    dve.tensor_scalar(XN[:, t, :], XN[:, t, :], MV[:, t, 0:1], RS[:, 2 + t:3 + t],
                                      ALU.subtract, ALU.mult)
                    dve.drain()
                    dve.tensor_tensor(XN[:, t, :], XN[:, t, :], PG[:, 0, :], ALU.mult)
                    dve.drain()
                    dve.tensor_tensor(H[:, t, :], XN[:, t, :], PG[:, 1, :], ALU.add).then_inc(residual_ready, 1)

            def ps(st):
                job = st.jobs[0]
                dve.wait_ge(bank_full[job.bank], full_at(job))
                for t in range(T):
                    c = t * 16
                    dve.tensor_copy(SBT[:, t, 0:8], PS[:, job.bank, c:c + 8])
                    last = dve.tensor_tensor(SBT[:, t, 8:16], PS[:, job.bank, c + 8:c + 16], prm("dtb", 2), ALU.add)
                last.then_inc(bank_taken[job.bank], 1)
                dve.drain()
                dve.tensor_scalar(GG[:, :, :], SBT[:, :, 8:16], 0.0, None, ALU.max)
                dve.drain()
                dve.wait_ge(small_logs_ready, reach("small_logs_ready", 1))
                dve.tensor_tensor(GG[:, :, :], GG[:, :, :], ZL[:, :, :], ALU.add)
                dve.tensor_scalar(BETA[:, :, :], BETA[:, :, :], 0.5, 0.5, ALU.mult, ALU.add)
                dve.drain()
                for t in range(T):
                    last = dve.scalar_tensor_tensor(out=GG[:, t, :], in0=GG[:, t, :], scalar=-1.0, in1=EAL[:, :],
                                                    op0=ALU.mult, op1=ALU.mult)
                last.then_inc(log_decay_ready, 1)
                dve.tensor_scalar(HB[:, :, :], BETA[:, :, :], 0.5, None, ALU.mult)
                dve.drain()

            def cumg(st):
                job = st.jobs[0]
                dve.wait_ge(bank_full[job.bank], full_at(job))
                dve.tensor_copy(G[:, :, :].rearrange("p a b -> p (a b)"), PS[:, job.bank, 0:16])
                dve.tensor_copy(GL[:, :, :].rearrange("p a b -> p (a b)"), PS[:, job.bank, 16:32])
                dve.tensor_copy(GTR[0:8, :], PS[0:8, job.bank, 64:64 + S]
                                ).then_inc(bank_taken[job.bank], 1)
                dve.drain()
                dve.tensor_tensor(ET[:, :, :], GL[:, :, :], G[:, :, :], ALU.subtract).then_inc(decay_diff_ready, 1)
                dve.wait_ge(decay_exps_ready, reach("decay_exps_ready", 1))
                dve.tensor_tensor(BEG[:, :, :], BETA[:, :, :], EG[:, :, :], ALU.mult).then_inc(decay_scalars_ready, 1)
                dve.drain()

            def pz(st):
                job = st.jobs[0]
                dve.wait_ge(z_tanh_ready, reach("z_tanh_ready", st.at["z_tanh_ready"]))
                dve.scalar_tensor_tensor(out=ZS[:, 2 * st.p:2 * st.p + 2, :].rearrange("p a b -> p (a b)"),
                                         in0=TH[:, st.p % 2, :], scalar=1.0, in1=PS[:, job.bank, :],
                                         op0=ALU.add, op1=ALU.mult).then_inc(bank_taken[job.bank], 1)

            def pconv(st):
                job, w = st.jobs[0], st.w
                b = job.bank
                cw = prm("cw", 2, 4)
                co = CO[:, st.hp % 2, 2 * w:2 * w + 2, :]
                dve.wait_ge(bank_full[job.bank], full_at(job))
                if st.hp >= 2:
                    for h in (2 * st.hp - 4, 2 * st.hp - 3):
                        done = named(("dtr", h)).jobs[1]
                        dve.wait_ge(bank_full[done.bank], full_at(done))
                for n in range(4):
                    for c in range(2):
                        tap = cw[:, 3 - n, 8 * w + 2 * st.hp + c:8 * w + 2 * st.hp + c + 1]
                        src = PS[:, b, c * S:(c + 1) * S - n]
                        if n == 0:
                            last = dve.tensor_scalar(co[:, c, :], src, tap, None, ALU.mult)
                        else:
                            last = dve.scalar_tensor_tensor(out=co[:, c, n:S], in0=src, scalar=tap,
                                                            in1=co[:, c, n:S], op0=ALU.mult, op1=ALU.add)
                    if n < 3:
                        dve.drain()
                last.then_inc(bank_taken[b], 1)
                dve.drain().then_inc(conv_ready, 1)
                dve.wait_ge(conv_tanh_ready, reach("conv_tanh_ready", st.at["conv_tanh_ready"]))
                flat = co.rearrange("p a b -> p (a b)")
                dve.scalar_tensor_tensor(out=flat, in0=TC[:, :], scalar=1.0, in1=flat, op0=ALU.add, op1=ALU.mult
                                         ).then_inc(conv_silu_ready, 1)

            def dte(st):
                i, h = st.h % 2, st.h
                b = named(("dtr", h)).jobs[1].bank
                sc, rd = SC[:, i, :], RD[:, i, :]
                dve.wait_ge(qk_rsqrt_ready, reach("qk_rsqrt_ready", named(("dtr", h)).at["qk_rsqrt_ready"]))
                dve.tensor_scalar(sc[:, 0:2], rd[:, 0:2], 128.0 ** -0.5, None, ALU.mult)
                dve.tensor_copy(sc[:, 2:4], rd[:, 2:4])
                dve.tensor_tensor(sc[:, 4:6], rd[:, 2:4], BETA[:, :, h], ALU.mult)
                dve.tensor_tensor(sc[:, 6:7], rd[:, 2:3], ET[:, 0, h:h + 1], ALU.mult)
                dve.tensor_scalar(sc[:, 7:8], rd[:, 3:4], BEG[:, 1, h:h + 1], -1.0, ALU.mult, ALU.mult)
                dve.tensor_scalar(sc[:, 8:9], rd[:, 1:2], EG[:, 1, h:h + 1], 128.0 ** -0.5, ALU.mult, ALU.mult
                                  ).then_inc(head_scalars_ready, 1)
                dve.drain()
                for n, src, s in ((2, 0, 2), (3, 1, 3), (4, 0, 4), (5, 1, 5), (6, 0, 6), (7, 1, 7)):
                    last = dve.tensor_scalar(TM[:, i, n, :], PS[:, b, src * P:(src + 1) * P], sc[:, s:s + 1], None,
                                             ALU.mult)
                last.then_inc(bank_taken[b], 1)

            def ddc(st):
                job, i, h = st.jobs[0], st.h % 2, st.h
                dve.wait_ge(bank_full[job.bank], full_at(job))
                for t in range(T):
                    last = dve.scalar_tensor_tensor(out=DD[:, i, t, :], in0=PS[:, job.bank, t * P:(t + 1) * P],
                                                    scalar=G[:, t, h:h + 1], in1=cst("maskt", 2),
                                                    op0=ALU.subtract, op1=ALU.add)
                last.then_inc(bank_taken[job.bank], 1)

            def dtf(st):
                job = st.jobs[1]
                dve.wait_ge(bank_full[job.bank], full_at(job))
                dve.tensor_copy(FBM[:, st.h % 2].rearrange("p a b -> p (a b)"), PS[:, job.bank, 0:384]
                                ).then_inc(bank_taken[job.bank], 1)

            def dkk(st):
                job, i = st.jobs[0], st.h % 2
                dve.wait_ge(bank_full[job.bank], full_at(job))
                dve.wait_ge(strict_decay_ready, reach("strict_decay_ready", named(("ddc", st.h)).at["strict_decay_ready"]))
                dve.tensor_tensor(AL[:, i].rearrange("p a b -> p (a b)"), PS[:, job.bank, :],
                                  DEC[:, i].rearrange("p a b -> p (a b)"), ALU.mult
                                  ).then_inc(bank_taken[job.bank], 1)

            def dl0(st):
                job, i = st.jobs[0], st.h % 2
                dve.wait_ge(bank_full[job.bank], full_at(job))
                for t in range(T):
                    dve.tensor_tensor(TT[:, i, t, :], IDENT, PS[:, job.bank, t * P:(t + 1) * P], ALU.subtract)
                for t in range(T):
                    last = dve.tensor_tensor(TT[:, i, 2 + t, :], IDENT, MT[:, i, t, :], ALU.subtract)
                last.then_inc(bank_taken[job.bank], 1)

            def dlb(st):
                job, i = st.jobs[0], st.h % 2
                dve.wait_ge(bank_full[job.bank], full_at(job))
                tt = TT[:, i].rearrange("p a b -> p (a b)")
                c = slice(0, 2 * S) if st.s < LEVELS - 1 else slice(S, 2 * S)
                dve.tensor_tensor(tt[:, c], tt[:, c], PS[:, job.bank, c], ALU.subtract
                                  ).then_inc(bank_taken[job.bank], 1)

            def du4(st):
                job, i = st.jobs[0], st.h % 2
                dve.wait_ge(out_rsqrt_ready, reach("out_rsqrt_ready", st.at["out_rsqrt_ready"]))
                for t in range(T):
                    last = dve.tensor_scalar(OD[:, i, t, :], PS[:, job.bank, t * P:(t + 1) * P],
                                             RSO[:, 2 * i + t:2 * i + t + 1], None, ALU.mult)
                last.then_inc(bank_taken[job.bank], 1)

            def dot(st):
                job, i, h = st.jobs[0], st.h % 2, st.h
                dve.wait_ge(bank_full[job.bank], full_at(job))
                dve.scalar_tensor_tensor(out=YBB[:, h, :], in0=PS[:, job.bank, 0:S], scalar=GDH[:, 0:1],
                                         in1=ZS[:, h, :], op0=ALU.mult, op1=ALU.mult
                                         ).then_inc(bank_taken[job.bank], 1)

            dve.wait_ge(x_loaded, 16)
            dve.drain().then_inc(residual_ready, 1)
            dve.wait_ge(con_loaded, 16)
            walk(dve, {"norm": norm, "xt": xt, "gu": gu, "post": post, "lam": lam, "pb": pb, "convb": convb,
                       "pf": pf, "pa": pa, "conva": conva, "score": score, "diff": diff, "out_norm": out_norm,
                       "lnb1": lnb1, "gy": gy}, 1)
            dve.wait_ge(prologue_row, 1)
            dve.scalar_tensor_tensor(out=ZS[0:NH_A, 6:8, :].rearrange("p a b -> p (a b)")[:, 0:384],
                                     in0=PS[0:NH_A, 0, 0:384], scalar=1.0 / QK_SCALE,
                                     in1=ZS[0:NH_A, 4:6, :].rearrange("p a b -> p (a b)")[:, 0:384],
                                     op0=ALU.mult, op1=ALU.add).then_inc(prologue_done, 1)
            dve.wait_ge(bias_loaded, 16)
            walk(dve, {"xt": xt, "gu": gu, "score": score, "out_norm": out_norm, "gy": gy, "scale_h": scale_h,
                       "post2": post2, "ps": ps, "cumg": cumg, "pz": pz, "pconv": pconv, "dte": dte, "ddc": ddc,
                       "dtf": dtf, "dkk": dkk, "dl0": dl0, "dlb": dlb, "du4": du4, "dot": dot}, 2)


def _cols_unit(w, c):
    return w[:, c * 256:(c + 1) * 256].reshape(-1, P, 256).transpose(1, 0, 2).reshape(P, UNIT)


def _rows_unit(w, r):
    return w[r * 256:(r + 1) * 256].reshape(2, P, D).transpose(1, 0, 2).reshape(P, UNIT)


def _by_feature(v):
    v = v.reshape(-1, v.shape[-1] // P, P)
    return v.transpose(2, 0, 1).reshape(P, -1)


def _rows(v):
    return np.broadcast_to(v.reshape(1, -1), (P, v.size))


def lay_out(a):
    s1 = np.empty((L, PLANS[1].units, P, UNIT), np.float32)
    s2 = np.empty((L, PLANS[2].units, P, UNIT), np.float32)
    prm1, prm2 = np.empty((L, P, NCOL1), np.float32), np.empty((L, P, NCOL2), np.float32)
    order = [8 * (b // 4) + b % 4 + 4 * u for b in range(8) for u in range(2)]
    for l in range(L):
        w_in = a["w_in"][l]
        w_main = np.concatenate([w_in[:, :5632], w_in[:, 5640:]], 1)
        outs = [a[n][l] for n in ("a_w_out", "b_w_out", "c_w_out", "d_w_out")]
        for i, key in enumerate(PLANS[1].stream):
            if key[0] == "g":
                u = _cols_unit(a["ffn1_w_gate" if key[1] == 0 else "ffn2_w_gate"][l], key[2])
            elif key[0] == "u":
                u = _cols_unit(a["ffn1_w_up" if key[1] == 0 else "ffn2_w_up"][l], key[2])
            elif key[0] == "d":
                u = _rows_unit(a["ffn1_w_down" if key[1] == 0 else "ffn2_w_down"][l], key[2])
            elif key[0] == "w":
                u = _cols_unit(w_main, key[1])
            elif key[0] == "o":
                w = outs[key[1]][:, key[2] * 512:(key[2] + 1) * 512]
                u = w.reshape(4, P, 512).transpose(1, 0, 2).reshape(P, UNIT)
            else:
                u = _rows_unit(a["w_o"][l], key[1])
            s1[l, i] = u
        lam_init = 0.8 - 0.6 * math.exp(-0.3 * l)
        parts = {"g0": _by_feature(a["ffn1_pre_g"][l]), "g1": _by_feature(a["mix_pre_g"][l]),
                 "g2": _by_feature(a["ffn2_pre_g"][l]), "aw": _by_feature(a["a_conv_w"][l]),
                 "bw": _by_feature(a["b_conv_w"][l]), "bb": _by_feature(a["b_conv_b"][l]),
                 "blg": _by_feature(a["b_ln_g"][l]), "blb": _by_feature(a["b_ln_b"][l]),
                 "sub": _by_feature(a["c_subln_g"][l]),
                 "lami": _rows(np.array([lam_init, 1.0 - lam_init], np.float32)),
                 "fb": _rows(a["d_forget_b"][l]),
                 "lam": _rows(np.concatenate([a[n][l] for n in ("c_lam_q1", "c_lam_k1", "c_lam_q2", "c_lam_k2")])),
                 "wf": w_in[:, 5632:5640].reshape(KB, P, 8).transpose(1, 0, 2).reshape(P, 64)}
        for name, (c0, c1) in COL1.items():
            prm1[l, :, c0:c1] = parts[name]
        w_in = a["w_in_2"][l]
        qa = w_in[:, :1024].reshape(D, NH_A, 64)[:, order].reshape(D, 1024)
        w_main = np.concatenate([qa, w_in[:, 1024:4608], w_in[:, 4624:]], 1)
        for i, key in enumerate(PLANS[2].stream):
            if key[0] in "gu" and len(key) == 3:
                f = 0 if key[1] == 0 else 1
                w13 = a["ffn_w13_2"][l, f]
                u = _cols_unit(w13[:, :FF] if key[0] == "g" else w13[:, FF:], key[2])
            elif key[0] == "d":
                u = _rows_unit(a["ffn_w2_2"][l, 0 if key[1] == 0 else 1], key[2])
            elif key[0] == "w":
                u = _cols_unit(w_main, key[1])
            elif key[0] == "o":
                u = _cols_unit(a["w_branch_a_2" if key[1] == 0 else "w_branch_b_2"][l], key[2])
            else:
                u = _rows_unit(a["w_out_2"][l], key[1])
            s2[l, i] = u
        parts = {"cw": _by_feature(a["conv_w_2"][l]), "dng": _by_feature(a["dn_norm_g_2"][l]),
                 "sink": _rows(a["sinks_2"][l]), "dtb": _rows(a["dt_bias_2"][l]), "alog": _rows(a["a_log_2"][l]),
                 "ws": w_in[:, 4608:4624].reshape(KB, P, 16).transpose(1, 0, 2).reshape(P, 128)}
        for name, (c0, c1) in COL2.items():
            prm2[l, :, c0:c1] = parts[name]
    feat1 = np.stack([a["ffn1_post_g"], a["mix_post_g"], a["ffn2_post_g"]], 1)
    feat2 = np.stack([a["ln_g_2"], a["ln_b_2"]], 2)
    onehot, rowmask = bias_table()
    return {"x": a["x"], "stream1": s1, "stream2": s2, "prm1": prm1, "prm2": prm2, "feat1": feat1, "feat2": feat2,
            "con": constants(), "onehot": onehot, "rowmask": rowmask.reshape(1, 384), "relb": a["rel_bias_2"]}


def kernel(**inputs):
    import concourse.bacc as _bacc
    from concourse.bass_utils import run_bass_kernel_spmd as _run

    a = {k: np.asarray(v) for k, v in inputs.items()}
    arrays = {k: np.ascontiguousarray(v) for k, v in lay_out(a).items()}
    nc = _bacc.Bacc("TRN2", target_bir_lowering=False, num_devices=1)
    aps = {n: nc.dram_tensor(n, v.shape, F32, kind="ExternalInput").ap() for n, v in arrays.items()}
    aps["toep"] = nc.dram_tensor("toeplitz_rows", (NH_A, P, 384), F32, kind="Internal").ap()
    aps["out"] = nc.dram_tensor("out", (1, S, D), F32, kind="ExternalOutput").ap()
    build_kernel(nc, **aps)
    r = _run(nc, [arrays], core_ids=[0])
    return r.results[0]["out"]
```

```python
import math
from contextlib import ExitStack

import numpy as np

import concourse.bass as bass
import concourse.mybir as mybir
from concourse.alu_op_type import AluOpType as ALU

ACT = mybir.ActivationFunctionType
F32 = mybir.dt.float32
F32R = mybir.dt.float32r

P = 128
D = 1024
KB = D // P
S = 256
T = S // P
L = 2
FF = 2816
FB = FF // P
FP = FF // 256
EPS = 1e-6
LN_EPS = 1e-5
SLOTS = 4
AHEAD = 3
UNIT = 2048
ALPHA = (2 * L) ** 0.25
MASKED = -1e30
HALF = 512
NH_C, NH_D, NH_A, NH_B = 4, 8, 16, 8
QK_SCALE = 0.125
LEVELS = 7

_c = 0


def _cols(table):
    out, at = {}, 0
    for name, n in table:
        out[name] = (at, at + n)
        at += n
    return out, at


COL1, NCOL1 = _cols([("g0", 8), ("g1", 8), ("g2", 8), ("aw", 12), ("bw", 124), ("bb", 4), ("blg", 4),
                     ("blb", 4), ("sub", 1), ("lami", 2), ("fb", 8), ("lam", 256), ("wf", 64)])
COL2, NCOL2 = _cols([("cw", 96), ("dng", 1), ("sink", 16), ("dtb", 8), ("alog", 8), ("ws", 128)])
CON1, NCON1 = _cols([("ident", 128), ("tri", 512), ("causal", 256), ("alibi", 1024)])
CON2, NCON2 = _cols([("ident", 128), ("tri", 128), ("ones", 128), ("maskt", 128), ("strict", 128),
                     ("level", 896)])
NCON = max(NCON1, NCON2)


class Job:

    def __init__(self, bank, turn, full, taken):
        self.bank, self.turn, self.full, self.taken = bank, turn, full, taken


class Step:

    def __init__(self, kind, unit, a=None, acc=None, b=None, br=None, e=None, h=None, half=None, hp=None, i=None, j=None, k=None, p=None, root=None, s=None, src=None, w=None, what=None):
        self.kind, self.unit, self.jobs, self.at, self.split = kind, unit, [], {}, []
        self.a = a
        self.acc = acc
        self.b = b
        self.br = br
        self.e = e
        self.h = h
        self.half = half
        self.hp = hp
        self.i = i
        self.j = j
        self.k = k
        self.p = p
        self.root = root
        self.s = s
        self.src = src
        self.w = w
        self.what = what


class Now:

    def __init__(self):
        self.blk, self.l = 1, 0


class Plan:

    def __init__(self):
        self.steps, self.count, self.stream, self.named = [], {}, [], {}
        self.by_pool = ("w", "ba", "aa", "gy")
        self.rot = {"lo": 0, "hi": 0, "s": 0}

    def tick(self, name, n):
        self.count[name] = self.count.get(name, 0) + n
        return self.count[name]

    def job(self, bank, fulls=1, takes=1):
        if isinstance(bank, str):
            pool = {"lo": (0, 1, 2, 3), "hi": (4, 5, 6, 7), "s": (4, 5)}[bank]
            self.rot[bank] += 1
            bank = pool[(self.rot[bank] - 1) % len(pool)]
        turn = self.count.get(("taken", bank), 0)
        return Job(bank, turn, self.tick(("full", bank), fulls), self.tick(("taken", bank), takes))

    def step(self, kind, name=None, banks=(), signals=(), unit=None, **args):
        st = Step(kind, unit, **args)
        st.jobs = [self.job(*(b if isinstance(b, tuple) else (b,))) for b in banks]
        st.at = {s: self.tick(s, n) for s, n in signals}
        if unit is not None:
            self.stream.append(unit)
        self.steps.append(st)
        if name is not None:
            self.named[name] = st
        return st

    def close(self):
        self.units = len(self.stream)
        assert self.units % SLOTS == 0
        self.place = {key: i for i, key in enumerate(self.stream)}
        assert len(self.place) == self.units
        self.low = []
        for i, key in enumerate(self.stream):
            by = "pool" if key[0] in self.by_pool and i % 2 else "vector"
            self.low.append((by, self.tick("low_by_" + by, 1)))
            self.tick("high_ready", 1)
            self.tick("slots_free", 1)
            self.tick(("slot", i % SLOTS), 16)
        used, split, begun = 0, 0, False
        for st in self.steps:
            begun = begun or st.kind == "xt"
            used += st.unit is not None
            upto = min(used + AHEAD - (used == 0), self.units) if begun else 0
            while split < upto:
                st.split.append(split)
                split += 1
        assert split == self.units


def plan_ffn(pl, s):
    def down(j2):
        pl.step("down", ("down", s, j2), s=s, j=j2, unit=("d", s, j2))

    for j in range(FB):
        pl.step("gu", ("gu", s, j), banks=["hi"], s=s, j=j, unit=("gu", s, j),
                signals=[("gate_silu_ready", 1), ("hidden_ready", 1)])
        if j >= 2 and j % 2 == 0:
            down(j // 2 - 1)
    down(FP - 1)


def weave(pl, chain, dense, every):
    dense = list(dense)
    for n, f in enumerate(chain):
        f()
        if n % every == every - 1 and dense:
            dense.pop(0)()
    for f in dense:
        f()


def plan_first():
    pl = Plan()
    acc_lo = [(b, 1, 1) for b in range(4)]
    acc_hi = [(b, 1, 1) for b in range(4, 8)]

    def norm_in(s):
        pl.step("norm", ("norm", s), s=s, signals=[("squares_summed", 1), ("rsqrt_ready", 1), ("normed_ready", 1)])
        pl.step("xt", ("xt", s), s=s, banks=["hi"] * 4, signals=[("activation_high_ready", 4)])

    def post(s, acc, root):
        pl.step("post", ("post", s), s=s, acc=acc, root=root, banks=[],
                signals=[("squares_summed", 2), ("rsqrt_ready", 2), ("residual_ready", 2)])

    pl.step("params", signals=[("params_loaded", 16)])

    def ffn(s):
        pl.step("feature", signals=[("feature_rows_loaded", 16)], s=s)
        norm_in(s)
        acc = pl.step("acc", ("acc", s), banks=acc_lo, s=s)
        plan_ffn(pl, s)
        post(s, acc, 2 * D ** -0.5)

    ffn(0)
    pl.step("feature", signals=[("feature_rows_loaded", 16)], s=1)
    norm_in(1)
    pl.step("lam", "lam", signals=[("lambda_dots", 1), ("lambda_exps", 1), ("lambda_ready", 1)])
    for p in range(4):
        pl.step("pb", ("pb", p), banks=["lo"], signals=[("branch_gate_ready", 1)], p=p, unit=("ba", p))
    taps = [(t, min(t + 5, 31)) for t in range(0, 31, 5)]

    def conv_b():
        if taps:
            a, b = taps.pop(0)
            pl.step("convb", ("convb", a), a=a, b=b, signals=[("conv_b_ready", 1 if b == 31 else 0)])

    for p in range(2):
        pl.step("pc", ("cq", p), banks=["lo"], what="cq", p=p, unit=("w", 10 + p))
    conv_b()
    for p in range(2):
        pl.step("pc", ("ck", p), banks=["lo"], what="ck", p=p, unit=("w", 12 + p))
    conv_b()
    for p in range(2):
        pl.step("pc", ("cv", p), banks=["lo"], what="cv", p=p, unit=("w", 14 + p))
    conv_b()
    pl.step("pf", "pf", banks=["lo"], signals=[("forget_log_ready", 1), ("log_forget_ready", 1)])
    for p in range(2):
        pl.step("pc", ("dq", p), banks=["lo"], what="dq", p=p, unit=("w", 16 + p))
    conv_b()
    pl.step("cum", "cum", banks=["s"])

    def chain_of(br, heads):
        steps = []
        per = 2 if br == "c" else 1

        def score(h):
            for m in range(per):
                e = h * per + m
                pl.step("score", ("score", br, e), banks=["s"], br=br, e=e, signals=[("probs_ready", 1)])
            if br == "c":
                pl.step("diff", ("diff", h), h=h, signals=[("probs_combined", 1)])

        def turn(h):
            pl.step("turn", ("turn", br, h), banks=["s"], br=br, h=h)

        def value(h):
            pl.step("value", ("value", br, h), br=br, h=h, signals=[("values_summed", 1)])

        for n in range(heads + 2):
            if n < heads:
                steps.append(lambda n=n: score(n))
            if 1 <= n <= heads:
                steps.append(lambda n=n: turn(n - 1))
            if n >= 2:
                steps.append(lambda n=n: value(n - 2))
        return steps

    dense = []
    for p in range(2):
        dense.append(lambda p=p: pl.step("pc", ("dk", p), banks=["lo"], what="dk", p=p, unit=("w", 18 + p)))
        dense.append(conv_b)
    for p in range(2):
        dense.append(lambda p=p: pl.step("pc", ("dv", p), banks=["lo"], what="dv", p=p, unit=("w", 20 + p)))
        dense.append(conv_b)
    for p in range(4):
        dense.append(lambda p=p: pl.step("pa", ("pa", p), banks=["lo"], signals=[("branch_gate_ready", 1)], p=p,
                                         unit=("aa", p)))
    for p in range(2):
        dense.append(lambda p=p: pl.step("conva", ("conva", p), banks=["lo"], p=p, unit=("w", p),
                                         signals=[("branch_a_ready", 1)]))
    pl.step("out_open", ("oo", "c"), banks=[(6, 0, 1), (7, 0, 1)], br="c")
    weave(pl, chain_of("c", NH_C), dense, 1)
    pl.step("out_norm", ("on", "c"), br="c", signals=[("out_squares_summed", 1), ("out_rsqrt_ready", 1)])
    gates = []
    for i in range(4):
        for k in range(KB):
            last = [("merged_ready", 1)] if i == 3 else []
            gates.append(lambda i=i, k=k, last=last: pl.step(
                "gy", ("gy", i, k), banks=["lo"], i=i, k=k, unit=("gy", i, k),
                signals=[("gate_tanh_ready", 1)] + last))
    gates[0]()
    pl.step("out_turn", ("ot", "c"), banks=["s", "s"], br="c", signals=[("activation_high_ready", 2)])
    pl.step("lnb1", "lnb1", banks=["s", "s"], signals=[("mean_var_ready", 2), ("branch_b_rsqrt_ready", 2)])
    gates[1]()
    pl.step("lnb3", "lnb3", banks=["s", "s"], signals=[("branch_b_ready", 1)])
    pl.step("out_open", ("oo", "d"), banks=[(6, 0, 1), (7, 0, 1)], br="d")
    weave(pl, chain_of("d", NH_D), gates[2:24], 1)
    pl.step("out_norm", ("on", "d"), br="d", signals=[("out_squares_summed", 0), ("out_rsqrt_ready", 0)])
    pl.step("out_turn", ("ot", "d"), banks=["s", "s"], br="d", signals=[("activation_high_ready", 2)])
    gates[24]()
    gates[25]()
    acc = pl.step("acc", ("acc", 1), banks=acc_hi, s=1)
    for k in range(2, KB + 1, 2):
        if k < KB:
            gates[24 + k]()
            gates[24 + k + 1]()
        pl.step("wo", ("wo", k // 2 - 1), k=k // 2 - 1, unit=("wo", k // 2 - 1), src=("gy", 3, k - 1))
    post(1, acc, D ** -0.5)
    ffn(2)
    pl.close()
    return pl


def plan_second():
    pl = Plan()
    acc_lo = [(b, 1, 1) for b in range(4)]
    acc_hi = [(b, 1, 1) for b in range(4, 8)]
    pl.step("params", signals=[("params_loaded", 16)])

    def begin(s):
        pl.step("feature", signals=[("feature_rows_loaded", 16)], s=s)
        if s == 0:
            pl.step("bias", signals=[("bias_loaded", 16)])
        pl.step("xt", ("xt", s), s=s, banks=["hi"] * 4, signals=[("activation_high_ready", 4)])
        pl.step("scale_h", ("sh", s), s=s)

    def post(s, acc):
        pl.step("post2", ("post", s), s=s, acc=acc, signals=[("mean_var_ready", 2), ("rsqrt_ready", 2), ("residual_ready", 2)])

    def ffn(s):
        begin(s)
        acc = pl.step("acc", ("acc", s), banks=acc_lo, s=s)
        plan_ffn(pl, s)
        post(s, acc)

    ffn(0)
    begin(1)

    def conv(hp, w):
        pl.step("pconv", ("pconv", hp, w), banks=["lo"], hp=hp, w=w, unit=("w", 6 + 4 * w + hp),
                signals=[("conv_ready", 1), ("conv_tanh_ready", 1), ("conv_silu_ready", 1)])

    pl.step("ps", "ps", banks=["lo"], signals=[("small_proj_ready", 1), ("small_logs_ready", 1), ("log_decay_ready", 1)])
    pl.step("pk", "pk", banks=["lo"], unit=("w", 4))
    for p in range(4):
        pl.step("pq", ("pq", p), banks=["lo"], p=p, unit=("w", p))
    pl.step("pv", "pv", banks=["lo"], unit=("w", 5))
    pl.step("cumg", "cumg", banks=["s"], signals=[("decay_diff_ready", 1), ("decay_exps_ready", 1), ("decay_scalars_ready", 1)])
    dense = [lambda p=p: pl.step("pz", ("pz", p), banks=["lo"], p=p, unit=("w", 18 + p), signals=[("z_tanh_ready", 1)])
             for p in range(4)]
    dense += [lambda w=w: conv(0, w) for w in range(3)]

    def chain_of(first):
        steps = []

        def score(h):
            pl.step("score", ("score", "a", h), banks=["s"], br="a", e=h, signals=[("probs_ready", 1), ("sink_exp_ready", 1)])

        def turn(h):
            pl.step("turn", ("turn", "a", h), banks=["s"], br="a", h=h)

        def value(h):
            pl.step("value", ("value", "a", h), br="a", h=h, signals=[("values_summed", 1)])

        for n in range(10):
            if n < 8:
                steps.append(lambda n=n: score(first + n))
            if 1 <= n <= 8:
                steps.append(lambda n=n: turn(first + n - 1))
            if n >= 2:
                steps.append(lambda n=n: value(first + n - 2))
        return steps

    for half in range(2):
        pl.step("out_open", ("oo", half), banks=[(6, 0, 1), (7, 0, 1)], br="a", half=half)
        weave(pl, chain_of(8 * half), dense[:4] if half == 0 else dense[4:], 4)
        pl.step("out_norm", ("on", half), br="a", half=half)
        pl.step("out_turn", ("ot", half), banks=["s", "s"], br="a", half=half,
                signals=[("activation_high_ready", 2)])

    gates = []
    for i in range(2):
        for k in range(KB):
            last = [("merged_ready", 1)] if i == 1 else []
            gates.append(lambda i=i, k=k, last=last: pl.step(
                "gy", ("gy", i, k), banks=["lo"], i=i, k=k, unit=("gy", i, k),
                signals=[("gate_tanh_ready", 1)] + last))

    for hp in range(NH_B // 2):
        chain = []
        hs = (2 * hp, 2 * hp + 1)

        def both(kind, banks, signals=(), **a):
            for h in hs:
                chain.append(lambda h=h: pl.step(kind, (kind, h) + tuple(a.values()), banks=banks, h=h,
                                                 signals=signals, **a))

        both("dtr", ["hi", "hi"], [("qk_squares_summed", 1), ("qk_rsqrt_ready", 1)])
        both("dte", [], [("head_scalars_ready", 1)])
        both("ddc", ["hi"], [("decay_ready", 1), ("strict_decay_ready", 1)])
        both("dtf", ["hi", "hi"])
        both("dkk", ["hi"])
        both("dl0", ["hi"], [("level_masked", 1)])
        for s in range(1, LEVELS):
            both("dla", ["hi"], [("level_masked", 1)], s=s)
            both("dlb", ["hi"], s=s)
        both("du1", ["hi"])
        both("du2", ["hi"])
        both("du3", ["hi"])
        both("du4", ["hi"], [("out_squares_summed", 1), ("out_rsqrt_ready", 1)])
        both("dot", ["hi"], [("delta_out_ready", 1)])
        dense = []
        if hp + 1 < NH_B // 2:
            dense += [lambda w=w, hp=hp: conv(hp + 1, w) for w in range(3)]
        dense += gates[2 * hp:2 * hp + 2]
        weave(pl, chain, dense, len(chain) // len(dense))
    gates[8]()
    gates[9]()
    acc = pl.step("acc", ("acc", 1), banks=acc_hi, s=1)
    for k in range(2, KB + 1, 2):
        if k < KB:
            gates[8 + k]()
            gates[8 + k + 1]()
        pl.step("wo", ("wo", k // 2 - 1), k=k // 2 - 1, unit=("wo", k // 2 - 1), src=("gy", 1, k - 1))
    post(1, acc)
    ffn(2)
    pl.close()
    return pl


PLANS = {1: plan_first(), 2: plan_second()}


def bias_table():
    m = np.arange(384)
    rel = 255 - m
    n = np.maximum(rel, 0)
    nf = np.maximum(n, 1).astype(np.float32)
    large = 16 + (np.log(nf / np.float32(16)) / np.float32(math.log(8)) * np.float32(16)).astype(np.int32)
    bucket = np.where(n < 16, n, np.minimum(large, 31))
    seen = (rel >= 0) & (rel < 128)
    onehot = (bucket[None, :] == np.arange(32)[:, None]) & seen[None, :]
    return onehot.astype(np.float32), np.where(seen, 0.0, MASKED).astype(np.float32)


def constants():
    i = np.arange(P)
    j256 = np.arange(S)
    ident = np.eye(P, dtype=np.float32)
    tri = np.stack([(i[:, None] + P * t <= j256[None, :]) for t in range(T)], 1).astype(np.float32)
    dist = (P + i[:, None] - j256[None, :]).astype(np.float32)
    causal = np.where(dist >= 0, 0.0, MASKED).astype(np.float32)
    alibi = np.stack([np.where(dist >= 0, -(2.0 ** (-8.0 / NH_C * (h + 1))) / QK_SCALE * dist, MASKED)
                      for h in range(NH_C)], 1).astype(np.float32)
    maskt = np.where(i[None, :] >= i[:, None], 0.0, MASKED).astype(np.float32)
    strict = (i[None, :] > i[:, None]).astype(np.float32)
    level = []
    for s in range(LEVELS):
        same = (i[None, :] >> (s + 1)) == (i[:, None] >> (s + 1))
        level.append(same & (((i[None, :] >> s) & 1) == 1) & (((i[:, None] >> s) & 1) == 0))
    level = np.stack(level, 1).astype(np.float32)
    c1 = np.concatenate([a.reshape(P, -1) for a in (ident, tri, causal, alibi)], 1)
    c2 = np.concatenate([a.reshape(P, -1) for a in (ident, tri[:, 0, :P], np.ones((P, P), np.float32),
                                                    maskt, strict, level)], 1)
    con = np.zeros((2, P, NCON), np.float32)
    con[0, :, :NCON1], con[1, :, :NCON2] = c1, c2
    return con


def build_kernel(nc, x, stream1, stream2, prm1, prm2, feat1, feat2, con, onehot, rowmask, relb, toep, out):
    with ExitStack() as ctx:
        def sb(name, shape):
            return ctx.enter_context(nc.sbuf_tensor(name, shape, F32))

        def sb_twice(name, parts, shape):
            with nc.sbuf_tensor(name, shape, F32) as whole:
                pass
            return whole, ctx.enter_context(nc.sbuf_tensor(parts, shape, F32R))

        def sem(name):
            return ctx.enter_context(nc.semaphore(name))

        H = sb("residual", [P, T, D])
        XTH = ctx.enter_context(nc.sbuf_tensor("normed_t_high", [P, KB, S], F32R))
        XTL = ctx.enter_context(nc.sbuf_tensor("normed_t_low", [P, KB, S], F32R))
        XT = (XTH, XTL)
        RING, LOW = sb_twice("weight_ring", "weights_low", [P, SLOTS, UNIT])
        HIGH = ctx.enter_context(nc.sbuf_tensor("weights_high", [P, SLOTS, UNIT], F32R))
        PG = sb("feature_rows", [P, 2, D])
        PRM = sb("params", [P, max(NCOL1, NCOL2)])
        CON = sb("constants", [P, NCON])
        PS = ctx.enter_context(nc.psum_tensor("psum", [P, 8, HALF], F32))
        SMALL = sb("small", [P, 524])
        ARENA = 25600
        W, WP = sb_twice("work", "work_parts", [P, ARENA])

        def small(a, *dims):
            n = int(np.prod(dims))
            v = SMALL[:, a:a + n]
            return v if len(dims) == 1 else v.rearrange("p (a b) -> p a b", a=dims[0])

        SS, RS = small(0, 4), small(4, 4)
        MX, NM = small(8, 4, 2), small(16, 4, 2)
        LS = small(24, 16, 2)
        RL = small(56, 16, 2)
        RC = small(88, 4)
        SSO, RSO = small(92, 16), small(108, 16)
        MV = small(124, 2, 2)
        RSB = small(128, 2)
        LAM, ELAM = small(130, 2), small(132, 2)
        NLAM, SUBG = small(134, 1), small(135, 1)
        ZF, ZA_, ZL, LF = (small(136 + 16 * n, 2, 8) for n in range(4))
        ES = small(200, 16, 2)
        HALFNEG = small(232, 16)
        ST = small(248, 4, 6)
        GDH = small(272, 1)
        SINK8 = small(273, 16)
        SBT = small(289, 2, 16)
        BETA, HB, GG = small(321, 2, 8), small(337, 2, 8), small(353, 2, 8)
        G, GL = small(369, 2, 8), small(385, 2, 8)
        EG, ET, BEG = small(401, 2, 8), small(417, 2, 8), small(433, 2, 8)
        EAL = small(449, 8)
        SSD, RD = small(457, 2, 4), small(465, 2, 4)
        SC = small(473, 2, 12)
        EPS_AT = {EPS: 0, 4 * EPS: 1, LN_EPS: 2}
        EPSES = small(498, 3, 8)
        TOUCH = small(522, 1)

        pos = [0]

        def arena(*dims, at=None):
            if at is not None:
                pos[0] = at
            n = int(np.prod(dims))
            v = W[:, pos[0]:pos[0] + n]
            pos[0] += n
            assert pos[0] <= ARENA, pos[0]
            if len(dims) == 2:
                v = v.rearrange("p (a b) -> p a b", a=dims[0])
            if len(dims) == 3:
                v = v.rearrange("p (a b c) -> p a b c", a=dims[0], b=dims[1])
            return v

        def parts(at, blocks):
            return WP[:, at:at + blocks * S].rearrange("p (a b) -> p a b", b=S)

        MG = arena(KB, S)
        XN = W[:, 0:T * D].rearrange("p (t d) -> p t d", t=T)
        EX = arena(4, 384)
        SG, HF = (W[:, at:at + 2 * S].rearrange("p (a b) -> p a b", b=S) for at in (T * D, T * D + 2 * S))
        HTH, HTL = parts(T * D + 4 * S, 4), parts(T * D + 8 * S, 4)
        PT = arena(3, 384)
        ON = arena(T, 512)
        TH = arena(2, 512)
        TMP = arena(2, S)
        common = pos[0]
        CQ, CK, CV = arena(4, S), arena(4, 2, S), arena(T, 512)
        merged_at = pos[0] - T * 512
        DQ, DK, DV = arena(4, S), arena(4, 2, S), arena(T, 512)
        dv_at = pos[0] - T * 512
        zb_at = pos[0]
        ZB, ACCB, ZA, ACCA = arena(4, S), arena(4, S), arena(4, S), arena(4, S)
        YB1, YC, YD = arena(4, S), arena(4, S), arena(4, S)
        NC = arena(S)
        JUNK = arena(P)
        BWH = arena(31, 4)
        za_at, acca_at, yb1_at, yc_at, yd_at = (zb_at + n * 4 * S for n in range(2, 7))
        Y1 = [tuple(parts(at, 4) for at in pair) for pair in
              ((za_at, acca_at), (zb_at, yb1_at), (common, yc_at), (dv_at, yd_at))]
        MGH1 = parts(merged_at, KB)
        MGL = parts(0, KB)
        BN = ACCB.rearrange("p a b -> p (a b)").rearrange("p (t n) -> p t n", t=T)
        YAH, YAL = parts(common, KB), parts(common + KB * S, KB)
        ZS = arena(KB, S, at=common + 2 * KB * S)
        YBH, YBL = parts(pos[0] - KB * S, KB), parts(pos[0], KB)
        CO = arena(6, S, at=pos[0] + KB * S)
        GTR = arena(S)
        TC = arena(2 * S)
        phase = pos[0]
        BIAS = arena(NH_A, S)
        QA, KA, VA = arena(KB, S), arena(4, S), arena(T, S)
        TM = arena(2, 11, P, at=phase)
        AL = arena(2, 4, P)
        TT = arena(2, 4, P)
        MT, DD = arena(2, 2, P), arena(2, 2, P)
        VW, VS, OD = arena(2, 2, P), arena(2, 2, P), DD
        MGH2 = parts(phase, KB)
        arena(0, at=2 * D)
        FA, FBM, DEC, P1S = arena(2, 4, P), arena(2, 3, P), arena(2, 4, P), arena(2, 2, P)
        assert pos[0] <= common - 3 * HALF

        def prm(name, blk, *dims):
            a, b = (COL1 if blk == 1 else COL2)[name]
            v = PRM[:, a:b]
            return v if not dims else v.rearrange("p (a b) -> p a b", a=dims[0])

        def cst(name, blk, *dims):
            a, b = (CON1 if blk == 1 else CON2)[name]
            v = CON[:, a:b]
            return v if not dims else v.rearrange("p (a b) -> p a b", a=dims[0])

        IDENT = CON[:, 0:P]

        bank_full = [sem(f"bank{b}_full") for b in range(8)]
        bank_taken = [sem(f"bank{b}_taken") for b in range(8)]
        slot_loaded = [sem(f"slot{s}_loaded") for s in range(SLOTS)]
        slots_free = sem("slots_free")
        x_loaded, con_loaded, out_stored = sem("x_loaded"), sem("constants_loaded"), sem("out_stored")
        prologue_done, toeplitz_stored, bias_loaded = sem("prologue_done"), sem("toeplitz_stored"), sem("bias_loaded")
        prologue_row, zeros_set = sem("prologue_row"), sem("zeros_set")
        gate_silu_ready = sem("gate_silu_ready")
        hidden_ready = sem("hidden_ready")
        merged_ready = sem("merged_ready")
        high_ready = sem("weights_high_ready")
        low_by_vector, low_by_pool = sem("weights_low_by_vector"), sem("weights_low_by_pool")
        activation_high_ready = sem("activation_high_ready")
        branch_b_ready = sem("branch_b_ready")
        delta_out_ready = sem("delta_out_ready")
        branch_gate_ready = sem("branch_gate_ready")
        squares_summed = sem("squares_summed")
        rsqrt_ready = sem("rsqrt_ready")
        normed_ready = sem("normed_ready")
        residual_ready = sem("residual_ready")
        params_loaded = sem("params_loaded")
        feature_rows_loaded = sem("feature_rows_loaded")
        lambda_dots = sem("lambda_dots")
        lambda_exps = sem("lambda_exps")
        lambda_ready = sem("lambda_ready")
        conv_b_ready = sem("conv_b_ready")
        forget_log_ready = sem("forget_log_ready")
        log_forget_ready = sem("log_forget_ready")
        probs_ready = sem("probs_ready")
        probs_combined = sem("probs_combined")
        values_summed = sem("values_summed")
        branch_a_ready = sem("branch_a_ready")
        out_squares_summed = sem("out_squares_summed")
        out_rsqrt_ready = sem("out_rsqrt_ready")
        gate_tanh_ready = sem("gate_tanh_ready")
        mean_var_ready = sem("mean_var_ready")
        branch_b_rsqrt_ready = sem("branch_b_rsqrt_ready")
        sink_exp_ready = sem("sink_exp_ready")
        small_proj_ready = sem("small_proj_ready")
        small_logs_ready = sem("small_logs_ready")
        log_decay_ready = sem("log_decay_ready")
        decay_diff_ready = sem("decay_diff_ready")
        decay_exps_ready = sem("decay_exps_ready")
        decay_scalars_ready = sem("decay_scalars_ready")
        z_tanh_ready = sem("z_tanh_ready")
        conv_ready = sem("conv_ready")
        conv_tanh_ready = sem("conv_tanh_ready")
        conv_silu_ready = sem("conv_silu_ready")
        qk_squares_summed = sem("qk_squares_summed")
        qk_rsqrt_ready = sem("qk_rsqrt_ready")
        head_scalars_ready = sem("head_scalars_ready")
        decay_ready = sem("decay_ready")
        strict_decay_ready = sem("strict_decay_ready")
        level_masked = sem("level_masked")
        CREDIT = {"residual_ready": 1, **{("taken", b): 1 for b in range(8)}}
        now = Now()

        def reach(key, k):
            per = [PLANS[b].count.get(key, 0) for b in (1, 2)]
            base = CREDIT.get(key, 0) + (L * per[0] if now.blk == 2 else 0) + k
            return now.l * per[now.blk - 1] + base

        def full_at(job):
            return reach(("full", job.bank), job.full)

        def taken_at(job):
            return reach(("taken", job.bank), job.taken)

        def turn_at(job):
            return reach(("taken", job.bank), job.turn)

        def loaded_at(i):
            return reach(("slot", i % SLOTS), 16 * (i // SLOTS + 1))

        def low_sem(i):
            return low_by_pool if PLANS[now.blk].low[i][0] == "pool" else low_by_vector

        def low_at(i):
            by, n = PLANS[now.blk].low[i]
            return reach("low_by_" + by, n)

        def width(i):
            return 12 * P if now.blk == 1 and PLANS[1].stream[i][0] == "gy" else UNIT

        def named(key):
            return PLANS[now.blk].named[key]

        def walk(eng, kinds, blk, split=None):
            now.blk = blk
            with eng.Fori(0, L) as l:
                now.l = l
                for st in PLANS[blk].steps:
                    if split is not None:
                        for i in st.split:
                            split(i)
                    if st.kind in kinds:
                        kinds[st.kind](st)

        block = ctx.enter_context(nc.Block())

        @block.sync
        def _(sp):
            sp.dma_start(H[:], x.rearrange("o (t p) d -> p (o t) d", p=P)).then_inc(x_loaded, 16)
            for blk, src in ((1, stream1), (2, stream2)):
                pl = PLANS[blk]
                now.blk = blk
                with sp.Fori(0, L) as l:
                    now.l = l
                    for i in range(pl.units):
                        n = width(i)
                        sp.wait_ge(slots_free, reach("slots_free", i + 1))
                        sp.dma_start(RING[:, i % SLOTS, 0:n], src[bass.ds(l, 1), i, :, 0:n]
                                     .rearrange("a p n -> (a p) n")).then_inc(slot_loaded[i % SLOTS], 16)
            now.blk, now.l = 2, L - 1
            sp.wait_ge(residual_ready, reach("residual_ready", 6))
            sp.dma_start(out.rearrange("o (t p) d -> p (o t) d", p=P), H[:]).then_inc(out_stored, 16)
            sp.wait_ge(out_stored, 16)

        @block.gpsimd
        def _(pool):
            def rsqrt(dst, src, eps, signal):
                n = dst.shape[1]
                pool.tensor_tensor(dst, src, EPSES[:, EPS_AT[eps], 0:n], ALU.add)
                pool.drain()
                pool.tensor_tensor(dst, dst, HALFNEG[:, 0:dst.shape[1]], ALU.pow).then_inc(signal, 1)

            def params(st):
                pool.wait_ge(residual_ready, reach("residual_ready", 0))
                src, n = (prm1, NCOL1) if now.blk == 1 else (prm2, NCOL2)
                pool.dma_start(PRM[:, 0:n], src[bass.ds(now.l, 1)].rearrange("a p n -> (a p) n")
                               ).then_inc(params_loaded, 16)

            def feature(st):
                pool.wait_ge(residual_ready, reach("residual_ready", 2 * st.s))
                if now.blk == 1:
                    row = feat1[bass.ds(now.l, 1), st.s:st.s + 1, :].rearrange("a b n -> (a b) n")
                    pool.dma_start(PG[:, 0, :], row.to_broadcast([P, D])).then_inc(feature_rows_loaded, 16)
                else:
                    row = feat2[bass.ds(now.l, 1), st.s].rearrange("a c n -> a (c n)")
                    pool.dma_start(PG[:].rearrange("p c n -> p (c n)"), row.to_broadcast([P, 2 * D])
                                   ).then_inc(feature_rows_loaded, 16)

            def bias(st):
                pool.dma_start(BIAS[:, :, :], bass.AP(toep.tensor, P - 1, [[383, P], [P * 384, NH_A], [1, S]])
                               ).then_inc(bias_loaded, 16)

            def split_low(i):
                if low_sem(i) is low_by_pool:
                    pool.wait_ge(high_ready, reach("high_ready", i + 1))
                    raw, high = RING[:, i % SLOTS, 0:width(i)], HIGH[:, i % SLOTS, 0:width(i)]
                    pool.tensor_tensor(LOW[:, i % SLOTS, 0:width(i)], raw, high.bitcast(F32), ALU.subtract
                                       ).then_inc(low_by_pool, 1)

            def norm(st):
                pool.wait_ge(squares_summed, reach("squares_summed", st.at["squares_summed"]))
                rsqrt(RS[:, 0:2], SS[:, 0:2], EPS, rsqrt_ready)

            def post(st):
                for t in range(T):
                    pool.wait_ge(squares_summed, reach("squares_summed", st.at["squares_summed"] - 1 + t))
                    rsqrt(RS[:, 2 + t:3 + t], SS[:, 2 + t:3 + t], 4 * EPS, rsqrt_ready)

            def post2(st):
                for t in range(T):
                    pool.wait_ge(mean_var_ready, reach("mean_var_ready", st.at["mean_var_ready"] - 1 + t))
                    rsqrt(RS[:, 2 + t:3 + t], MV[:, t, 1:2], LN_EPS, rsqrt_ready)

            def lnb1(st):
                for t in range(T):
                    pool.wait_ge(mean_var_ready, reach("mean_var_ready", st.at["mean_var_ready"] - 1 + t))
                    rsqrt(RSB[:, t:t + 1], MV[:, t, 1:2], EPS, branch_b_rsqrt_ready)

            def out_norm(st):
                if st.br == "c":
                    pool.wait_ge(out_squares_summed, reach("out_squares_summed", st.at["out_squares_summed"]))
                    rsqrt(RSO[:, 0:8], SSO[:, 0:8], EPS, out_rsqrt_ready)

            def dtr(st):
                i = st.h % 2
                pool.wait_ge(qk_squares_summed, reach("qk_squares_summed", st.at["qk_squares_summed"]))
                if st.h >= 2:
                    pool.wait_ge(head_scalars_ready, reach("head_scalars_ready", named(("dte", st.h - 2)).at["head_scalars_ready"]))
                rsqrt(RD[:, i, :], SSD[:, i, :], 4 * EPS, qk_rsqrt_ready)

            def ddc(st):
                i = st.h % 2
                dec = DEC[:, i].rearrange("p (t k) n -> p t k n", t=T)
                pool.wait_ge(decay_ready, reach("decay_ready", st.at["decay_ready"]))
                for t in range(T):
                    last = pool.tensor_tensor(dec[:, t, 0, :], dec[:, t, 1, :], cst("strict", 2), ALU.mult)
                last.then_inc(strict_decay_ready, 1)

            def level(st, s):
                i = st.h % 2
                al = AL[:, i].rearrange("p (t k) n -> p t k n", t=T)
                if s == 0:
                    ready = named(("dkk", st.h)).jobs[0]
                    pool.wait_ge(bank_taken[ready.bank], taken_at(ready))
                if s > 0:
                    done = named(("dla", st.h, s - 1) if s > 1 else ("dl0", st.h)).jobs[0]
                    pool.wait_ge(bank_full[done.bank], full_at(done))
                if s == 1:
                    ready = named(("dl0", st.h)).jobs[0]
                    pool.wait_ge(bank_taken[ready.bank], taken_at(ready))
                for t in range(T):
                    last = pool.tensor_tensor(MT[:, i, t, :], al[:, t, 0, :], cst("level", 2, LEVELS)[:, s, :],
                                              ALU.mult)
                last.then_inc(level_masked, 1)

            def du4(st):
                i = st.h % 2
                pool.wait_ge(out_squares_summed, reach("out_squares_summed", st.at["out_squares_summed"]))
                rsqrt(RSO[:, 2 * i:2 * i + 2], SSO[:, 2 * i:2 * i + 2], EPS, out_rsqrt_ready)

            pool.dma_start(CON[:, 0:NCON1], con[0, :, 0:NCON1]).then_inc(con_loaded, 16)
            pool.memset(HALFNEG[:, :], -0.5)
            for eps, at in EPS_AT.items():
                pool.drain()
                pool.memset(EPSES[:, at, :], eps)
            pool.drain()
            pool.memset(CK[64:128, :, 0, :], 0.0)
            pool.drain()
            pool.memset(CK[0:64, :, 1, :], 0.0)
            pool.drain()
            pool.memset(DK[64:128, :, 0, :], 0.0)
            pool.drain()
            pool.memset(DK[0:64, :, 1, :], 0.0)
            pool.drain()
            pool.memset(NC[:, :], 0.0).then_inc(zeros_set, 1)
            pool.drain()
            kinds = {"params": params, "feature": feature, "norm": norm, "post": post, "lnb1": lnb1,
                     "out_norm": out_norm}
            walk(pool, kinds, 1, split_low)
            now.blk, now.l = 2, 0
            pool.wait_ge(residual_ready, reach("residual_ready", 0))
            pool.dma_start(CON[:, 0:NCON2], con[1, :, 0:NCON2]).then_inc(con_loaded, 16)
            pool.dma_start(ZS[0:32, 0:2, :].rearrange("p a b -> p (a b)")[:, 0:384], onehot).then_inc(con_loaded, 16)
            pool.dma_start(ZS[0:32, 2, 0:NH_A], relb).then_inc(con_loaded, 16)
            pool.dma_start(ZS[0:NH_A, 4:6, :].rearrange("p a b -> p (a b)")[:, 0:384],
                           rowmask.to_broadcast([NH_A, 384])).then_inc(con_loaded, 16)
            pool.memset(GTR[:, :], 0.0)
            pool.wait_ge(prologue_done, 1)
            row = ZS[0:NH_A, 6:8, :].rearrange("p a b -> p (a b)")[:, 0:384]
            pool.dma_start(toep, row.unsqueeze(1).to_broadcast([NH_A, P, 384])).then_inc(toeplitz_stored, 16)
            pool.wait_ge(toeplitz_stored, 16)
            pool.drain().then_inc(zeros_set, 1)
            walk(pool, {"params": params, "feature": feature, "post2": post2, "dtr": dtr, "ddc": ddc,
                        "dl0": lambda st: level(st, 0), "dla": lambda st: level(st, st.s), "du4": du4,
                        "bias": bias}, 2, split_low)

        @block.tensor
        def _(pe):
            owed = [0]

            def mm(dst, lhsT, rhs, start=True, stop=True):
                return pe.matmul(dst, lhsT, rhs, start=start, stop=stop, skip_group_check=True)

            def transpose(dst, src):
                return pe.transpose(dst, src, IDENT)

            def pay(ins):
                if owed[0]:
                    ins.then_inc(slots_free, owed[0])
                    owed[0] = 0
                return ins

            def flush():
                if owed[0]:
                    pe.drain().then_inc(slots_free, owed[0])
                    owed[0] = 0

            def weights(st, a):
                i = PLANS[now.blk].place[st.unit]
                pe.wait_ge(low_sem(i), low_at(i))
                n = width(i)
                return [v.rearrange("p (a b) -> p a b", a=a)
                        for v in (HIGH[:, i % SLOTS, 0:n], LOW[:, i % SLOTS, 0:n])]

            PARTS = ((0, 0), (0, 1), (1, 0))

            def cols_product(bank, at, w, c, src, n, first=0):
                for k in range(n):
                    for m, (a, b) in enumerate(PARTS):
                        ins = mm(PS[:, bank, at:at + S], w[a][:, first + k, c * P:(c + 1) * P], src[b][:, k, :],
                                 (k, m) == (0, 0), (k, m) == (n - 1, 2))
                        if (k, m) == (0, 0):
                            pay(ins)
                return ins

            def xt(st):
                flush()
                blk, src = now.blk, (XN if now.blk == 1 else H)
                if blk == 1:
                    pe.wait_ge(normed_ready, reach("normed_ready", named(("norm", st.s)).at["normed_ready"]))
                else:
                    pe.wait_ge(residual_ready, reach("residual_ready", 2 * st.s))
                for k2, job in enumerate(st.jobs):
                    pe.wait_ge(bank_taken[job.bank], turn_at(job))
                    for kk in range(2):
                        for t in range(T):
                            k = 2 * k2 + kk
                            ins = transpose(PS[:, job.bank, (kk * T + t) * P:(kk * T + t + 1) * P],
                                            src[:, t, k * P:(k + 1) * P])
                            if (kk, t) == (1, T - 1):
                                ins.then_inc(bank_full[job.bank], 1)

            def acc(st):
                for job in st.jobs:
                    pe.wait_ge(bank_taken[job.bank], turn_at(job))

            def wait_xt(s):
                for job in named(("xt", s)).jobs:
                    pe.wait_ge(bank_taken[job.bank], taken_at(job))

            def gu(st):
                job = st.jobs[0]
                if st.j == 0:
                    wait_xt(st.s)
                w = weights(st, KB)
                pe.wait_ge(bank_taken[job.bank], turn_at(job))
                cols_product(job.bank, 0, w, 0, XT, KB)
                cols_product(job.bank, S, w, 1, XT, KB).then_inc(bank_full[job.bank], 1)
                owed[0] += 1

            def down(st):
                w = weights(st, 2)
                pe.wait_ge(hidden_ready, reach("hidden_ready", named(("gu", st.s, 2 * st.j + 1)).at["hidden_ready"]))
                src = [h[:, 2 * st.j % 4:2 * st.j % 4 + 2, :] for h in (HTH, HTL)]
                rows_product(st, w, src, named(("acc", st.s)).jobs, st.j == 0, st.j == FP - 1)

            def rows_product(st, w, src, jobs, start, stop):
                for t in range(T):
                    for n in range(2):
                        b = jobs[2 * t + n].bank
                        for r in range(2):
                            for m, (a, c) in enumerate(PARTS):
                                ins = mm(PS[:, b, :], src[c][:, r, t * P:(t + 1) * P],
                                         w[a][:, r, n * HALF:(n + 1) * HALF], start and (r, m) == (0, 0),
                                         stop and (r, m) == (1, 2))
                                if (t, n, r, m) == (0, 0, 0, 0):
                                    pay(ins)
                        if stop:
                            ins.then_inc(bank_full[b], 1)
                owed[0] += 1
                if stop:
                    flush()

            def pb(st):
                job = st.jobs[0]
                if st.p == 0 and st.kind == "pb":
                    wait_xt(1)
                w = weights(st, KB)
                pe.wait_ge(bank_taken[job.bank], turn_at(job))
                cols_product(job.bank, 0, w, 0, XT, KB)
                cols_product(job.bank, S, w, 1, XT, KB).then_inc(bank_full[job.bank], 1)
                owed[0] += 1

            def project(st, tokens=False):
                job = st.jobs[0]
                w = weights(st, KB)
                pe.wait_ge(bank_taken[job.bank], turn_at(job))
                b = job.bank
                if tokens:
                    for t in range(T):
                        for k in range(KB):
                            for m, (i, j) in enumerate(PARTS):
                                ins = mm(PS[:, b, t * S:(t + 1) * S], XT[j][:, k, t * P:(t + 1) * P], w[i][:, k, :],
                                         (k, m) == (0, 0), (k, m) == (KB - 1, 2))
                                if (t, k, m) == (0, 0, 0):
                                    pay(ins)
                    ins.then_inc(bank_full[b], 1)
                else:
                    cols_product(b, 0, w, 0, XT, KB)
                    cols_product(b, S, w, 1, XT, KB).then_inc(bank_full[b], 1)
                owed[0] += 1

            def pc(st):
                project(st, st.what[1] == "v")

            def small_project(st, w, n):
                flush()
                job = st.jobs[0]
                pe.wait_ge(params_loaded, reach("params_loaded", 16))
                pe.wait_ge(bank_taken[job.bank], turn_at(job))
                for t in range(T):
                    for k in range(KB):
                        for part in (0, 1):
                            ins = mm(PS[:, job.bank, t * n:(t + 1) * n],
                                     XT[part][:, k, t * P:(t + 1) * P].bitcast(F32), w[:, k, :],
                                     (k, part) == (0, 0), (k, part) == (KB - 1, 1))
                ins.then_inc(bank_full[job.bank], 1)

            def pf(st):
                small_project(st, prm("wf", 1, KB), 8)

            def cum(st):
                job = st.jobs[0]
                pe.wait_ge(log_forget_ready, reach("log_forget_ready", 1))
                pe.wait_ge(bank_taken[job.bank], turn_at(job))
                for t in range(T):
                    ins = mm(PS[0:8, job.bank, 0:S], LF[:, t, :], cst("tri", 1, T)[:, t, :], t == 0, t == T - 1)
                    if t == T - 1:
                        ins.then_inc(bank_full[job.bank], 1)

            def score(st):
                job, e = st.jobs[0], st.e
                b = job.bank
                if st.br == "c":
                    h = e // 2
                    q, k = CQ[:, h, :], CK[:, h, e % 2, :]
                    if e % 4 == 0:
                        ready = named(("cq", h // 2)).jobs[0]
                        pe.wait_ge(bank_taken[ready.bank], taken_at(ready))
                        ready = named(("ck", h // 2)).jobs[0]
                        pe.wait_ge(bank_taken[ready.bank], taken_at(ready))
                elif st.br == "d":
                    q, k = DQ[:, e // 2, :], DK[:, e // 2, e % 2, :]
                    if e % 4 == 0:
                        ready = named(("dq", e // 4)).jobs[0]
                        pe.wait_ge(bank_taken[ready.bank], taken_at(ready))
                        ready = named(("dk", e // 4)).jobs[0]
                        pe.wait_ge(bank_taken[ready.bank], taken_at(ready))
                    if e == 0:
                        ready = named("cum").jobs[0]
                        pe.wait_ge(bank_taken[ready.bank], taken_at(ready))
                else:
                    g = e // 4
                    blk_ = (g // 2) * 4 + e % 4
                    rows = slice(64 * (g % 2), 64 * (g % 2) + 64)
                    q, k = QA[rows, blk_, :], KA[rows, g, :]
                    if e % 2 == 0:
                        ready = named(("pq", blk_ // 2)).jobs[0]
                        pe.wait_ge(bank_taken[ready.bank], taken_at(ready))
                    if e == 0:
                        ready = named("pk").jobs[0]
                        pe.wait_ge(bank_taken[ready.bank], taken_at(ready))
                pe.wait_ge(bank_taken[job.bank], turn_at(job))
                for t in range(T):
                    dst = PS[:, b, 0:P] if t == 0 else PS[:, b, P:P + S]
                    keys = (t + 1) * P
                    extra = st.br == "d"
                    ins = mm(dst, q[:, t * P:(t + 1) * P], k[:, 0:keys], True, not extra)
                    if extra:
                        ins = mm(dst, IDENT[:, e:e + 1].to_broadcast([P, P]), NC[:, 0:keys], False, True)
                ins.then_inc(bank_full[b], 1)

            def turn_(st):
                job = st.jobs[0]
                b = job.bank
                e = 2 * st.h if st.br == "c" else st.h
                if st.br == "c":
                    pe.wait_ge(probs_combined, reach("probs_combined", named(("diff", st.h)).at["probs_combined"]))
                else:
                    pe.wait_ge(probs_ready, reach("probs_ready", named(("score", st.br, e)).at["probs_ready"]))
                pe.wait_ge(bank_taken[job.bank], turn_at(job))
                for n in range(3):
                    ins = transpose(PS[:, b, n * P:(n + 1) * P], EX[:, e % 4, n * P:(n + 1) * P])
                    if n == 2:
                        ins.then_inc(bank_full[b], 1)

            def out_open(st):
                for job in st.jobs:
                    pe.wait_ge(bank_taken[job.bank], turn_at(job))

            def value(st):
                h = st.h
                ready = named(("turn", st.br, h)).jobs[0]
                pe.wait_ge(bank_taken[ready.bank], taken_at(ready))
                pt = PT[:, st.at["values_summed"] % 3, :]
                if st.br == "c":
                    v, c, w = [CV[:, t, h * P:(h + 1) * P] for t in range(T)], h * P, P
                    if h % 2 == 0:
                        ready = named(("cv", h // 2)).jobs[0]
                        pe.wait_ge(bank_taken[ready.bank], taken_at(ready))
                elif st.br == "d":
                    v, c, w = [DV[:, t, h * 64:(h + 1) * 64] for t in range(T)], h * 64, 64
                    if h % 4 == 0:
                        ready = named(("dv", h // 4)).jobs[0]
                        pe.wait_ge(bank_taken[ready.bank], taken_at(ready))
                else:
                    g = h // 4
                    v, c, w = [VA[:, t, g * 64:(g + 1) * 64] for t in range(T)], (h % 8) * 64, 64
                    if h == 0:
                        ready = named("pv").jobs[0]
                        pe.wait_ge(bank_taken[ready.bank], taken_at(ready))
                mm(PS[:, 6, c:c + w], pt[:, 0:P], v[0])
                mm(PS[:, 7, c:c + w], pt[:, P:2 * P], v[0], True, False)
                mm(PS[:, 7, c:c + w], pt[:, 2 * P:3 * P], v[1], False, True).then_inc(values_summed, 1)

            def out_turn(st):
                for job in named(("oo", st.half if st.br == "a" else st.br)).jobs:
                    pe.wait_ge(bank_taken[job.bank], taken_at(job))
                for p, job in enumerate(st.jobs):
                    pe.wait_ge(bank_taken[job.bank], turn_at(job))
                    for n in range(4):
                        c, t = 2 * p + n // 2, n % 2
                        ins = transpose(PS[:, job.bank, n * P:(n + 1) * P], ON[:, t, c * P:(c + 1) * P])
                        if n == 3:
                            ins.then_inc(bank_full[job.bank], 1)

            def lnb1(st):
                pe.wait_ge(conv_b_ready, reach("conv_b_ready", 1))
                for t, job in enumerate(st.jobs):
                    pe.wait_ge(bank_taken[job.bank], turn_at(job))
                    for c in range(4):
                        ins = transpose(PS[:, job.bank, c * P:(c + 1) * P], ACCB[:, c, t * P:(t + 1) * P])
                        if c == 3:
                            ins.then_inc(bank_full[job.bank], 1)

            def lnb3(st):
                assert [job.bank for job in st.jobs] == [job.bank for job in named("lnb1").jobs]
                for job in st.jobs:
                    pe.wait_ge(bank_taken[job.bank], turn_at(job))
                for p, job in enumerate(st.jobs):
                    for n in range(4):
                        c, t = 2 * p + n // 2, n % 2
                        ins = transpose(PS[:, job.bank, n * P:(n + 1) * P], BN[:, t, c * P:(c + 1) * P])
                        if n == 3:
                            ins.then_inc(bank_full[job.bank], 1)

            def gy(st):
                job, i, k = st.jobs[0], st.i, st.k
                w = weights(st, 12 if now.blk == 1 else KB)
                pe.wait_ge(bank_taken[job.bank], turn_at(job))
                cols_product(job.bank, 0, w, 0, XT, KB)
                if k == 0:
                    if now.blk == 1 and i == 0:
                        pe.wait_ge(branch_a_ready, reach("branch_a_ready", 2))
                    elif now.blk == 1 and i == 1:
                        pe.wait_ge(branch_b_ready, reach("branch_b_ready", 1))
                    elif now.blk == 2 and i == 1:
                        pe.wait_ge(delta_out_ready, reach("delta_out_ready", NH_B))
                    else:
                        for j2 in named({2: ("ot", "c"), 3: ("ot", "d"), 0: ("ot", 1)}[i]).jobs:
                            pe.wait_ge(bank_taken[j2.bank], taken_at(j2))
                if now.blk == 1:
                    cols_product(job.bank, S, w, 0, Y1[i], 4, KB).then_inc(bank_full[job.bank], 1)
                else:
                    y = ((YAH, YAL), (YBH, YBL))[i]
                    cols_product(job.bank, S, w, 1, y, KB).then_inc(bank_full[job.bank], 1)
                owed[0] += 1

            def wo(st):
                w = weights(st, 2)
                pe.wait_ge(merged_ready, reach("merged_ready", named(st.src).at["merged_ready"]))
                src = [v[:, 2 * st.k:2 * st.k + 2, :] for v in (MGH1 if now.blk == 1 else MGH2, MGL)]
                rows_product(st, w, src, named(("acc", 1)).jobs, st.k == 0, st.k == KB // 2 - 1)

            def ps(st):
                wait_xt(1)
                small_project(st, prm("ws", 2, KB), 16)

            def cumg(st):
                job = st.jobs[0]
                b = job.bank
                pe.wait_ge(log_decay_ready, reach("log_decay_ready", 1))
                pe.wait_ge(bank_taken[job.bank], turn_at(job))
                tri = cst("tri", 2)
                gg = GG.rearrange("p a b -> p (a b)")
                mm(PS[:, b, 0:16], tri, gg)
                mm(PS[:, b, 16:32], cst("ones", 2), gg)
                for t in range(T):
                    ins = mm(PS[0:8, b, 64 + t * P:64 + (t + 1) * P], GG[:, t, :], tri)
                    if t == T - 1:
                        ins.then_inc(bank_full[b], 1)

            def dtr(st):
                h, i, j1, j2 = st.h, st.h % 2, st.jobs[0], st.jobs[1]
                hp, c = h // 2, h % 2
                pe.wait_ge(conv_silu_ready, reach("conv_silu_ready", named(("pconv", hp, 2)).at["conv_silu_ready"]))
                pe.wait_ge(bank_taken[j1.bank], turn_at(j1))
                pe.wait_ge(bank_taken[j2.bank], turn_at(j2))
                for w, job, at in ((0, j1, 0), (2, j1, 2), (1, j2, 0)):
                    for t in range(T):
                        ins = transpose(PS[:, job.bank, (at + t) * P:(at + t + 1) * P],
                                        CO[:, 2 * w + c, t * P:(t + 1) * P])
                        if t == 1 and w > 0:
                            ins.then_inc(bank_full[job.bank], 1)

            def dtf(st):
                h, i = st.h, st.h % 2
                tr = named(("dtr", h)).jobs
                j1, j2 = st.jobs
                ready = tr[0]
                pe.wait_ge(bank_taken[ready.bank], taken_at(ready))
                ready = tr[1]
                pe.wait_ge(bank_taken[ready.bank], taken_at(ready))
                pe.wait_ge(bank_taken[j1.bank], turn_at(j1))
                for n, src in enumerate((TM[:, i, 4, :], TM[:, i, 0, :], TM[:, i, 5, :], TM[:, i, 1, :])):
                    ins = transpose(PS[:, j1.bank, n * P:(n + 1) * P], src)
                    if n == 3:
                        ins.then_inc(bank_full[j1.bank], 1)
                pe.wait_ge(bank_taken[j2.bank], turn_at(j2))
                for n, src in enumerate((TM[:, i, 2, :], TM[:, i, 3, :], TM[:, i, 8, :])):
                    ins = transpose(PS[:, j2.bank, n * P:(n + 1) * P], src)
                    if n == 2:
                        ins.then_inc(bank_full[j2.bank], 1)

            def ddc(st):
                job = st.jobs[0]
                if st.h == 0:
                    ready = named("cumg").jobs[0]
                    pe.wait_ge(bank_taken[ready.bank], taken_at(ready))
                pe.wait_ge(bank_taken[job.bank], turn_at(job))
                mm(PS[:, job.bank, 0:S], IDENT[:, st.h:st.h + 1].to_broadcast([P, P]), GTR[:, :]).then_inc(bank_full[job.bank], 1)

            def dkk(st):
                job, i = st.jobs[0], st.h % 2
                for j2 in named(("dtf", st.h)).jobs:
                    if j2.bank != job.bank:
                        pe.wait_ge(bank_taken[j2.bank], taken_at(j2))
                pe.wait_ge(bank_taken[job.bank], turn_at(job))
                for t in range(T):
                    ins = mm(PS[:, job.bank, t * S:(t + 1) * S], FBM[:, i, t, :],
                             FA[:, i, 2 * t:2 * t + 2, :].rearrange("p a b -> p (a b)"))
                    if t == 1:
                        ins.then_inc(bank_full[job.bank], 1)

            def dl0(st):
                job, i = st.jobs[0], st.h % 2
                pe.wait_ge(level_masked, reach("level_masked", st.at["level_masked"]))
                pe.wait_ge(bank_taken[job.bank], turn_at(job))
                for t in range(T):
                    ins = mm(PS[:, job.bank, t * P:(t + 1) * P], MT[:, i, t, :], IDENT)
                    if t == 1:
                        ins.then_inc(bank_full[job.bank], 1)

            def dla(st):
                job, i, s = st.jobs[0], st.h % 2, st.s
                pe.wait_ge(level_masked, reach("level_masked", st.at["level_masked"]))
                ready = named(("dlb", st.h, s - 1) if s > 1 else ("dl0", st.h)).jobs[0]
                pe.wait_ge(bank_taken[ready.bank], taken_at(ready))
                pe.wait_ge(bank_taken[job.bank], turn_at(job))
                for t in range(T):
                    ins = mm(PS[:, job.bank, t * P:(t + 1) * P], MT[:, i, t, :], TT[:, i, t, :])
                    if t == 1:
                        ins.then_inc(bank_full[job.bank], 1)

            def dlb(st):
                job, i, s = st.jobs[0], st.h % 2, st.s
                ready = named(("dla", st.h, s)).jobs[0]
                pe.wait_ge(bank_taken[ready.bank], taken_at(ready))
                pe.wait_ge(bank_taken[job.bank], turn_at(job))
                b = job.bank
                if s < LEVELS - 1:
                    for t in range(T):
                        mm(PS[:, b, t * P:(t + 1) * P], TT[:, i, 2 + t, :], P1S[:, i, t, :])
                for t in range(T):
                    ins = mm(PS[:, b, S + t * P:S + (t + 1) * P], P1S[:, i, t, :], TT[:, i, 2 + t, :])
                    if t == 1:
                        ins.then_inc(bank_full[b], 1)

            def du1(st):
                job, i = st.jobs[0], st.h % 2
                b = job.bank
                ready = named(("dlb", st.h, LEVELS - 1)).jobs[0]
                pe.wait_ge(bank_taken[ready.bank], taken_at(ready))
                pe.wait_ge(bank_taken[job.bank], turn_at(job))
                mm(PS[:, b, 0:P], TT[:, i, 2, :], TM[:, i, 9, :])
                mm(PS[:, b, P:S], TM[:, i, 7, :], TT[:, i, 3, :]).then_inc(bank_full[b], 1)

            def du2(st):
                job, i = st.jobs[0], st.h % 2
                ready = named(("du1", st.h)).jobs[0]
                pe.wait_ge(bank_taken[ready.bank], taken_at(ready))
                pe.wait_ge(bank_taken[job.bank], turn_at(job))
                mm(PS[:, job.bank, 0:P], TM[:, i, 6, :], VW[:, i, 0, :]).then_inc(bank_full[job.bank], 1)

            def du3(st):
                job, i = st.jobs[0], st.h % 2
                ready = named(("du2", st.h)).jobs[0]
                pe.wait_ge(bank_taken[ready.bank], taken_at(ready))
                pe.wait_ge(bank_taken[job.bank], turn_at(job))
                mm(PS[:, job.bank, 0:P], TT[:, i, 3, :], TM[:, i, 10, :], True, False)
                mm(PS[:, job.bank, 0:P], VW[:, i, 1, :], VS[:, i, 0, :], False, True).then_inc(bank_full[job.bank], 1)

            def du4(st):
                job, i = st.jobs[0], st.h % 2
                b = job.bank
                ready = named(("du3", st.h)).jobs[0]
                pe.wait_ge(bank_taken[ready.bank], taken_at(ready))
                pe.wait_ge(bank_taken[job.bank], turn_at(job))
                mm(PS[:, b, 0:P], AL[:, i, 1, :], VW[:, i, 0, :])
                mm(PS[:, b, P:S], FBM[:, i, 2, :], VS[:, i, 0, :], True, False)
                mm(PS[:, b, P:S], AL[:, i, 3, :], VS[:, i, 1, :], False, True).then_inc(bank_full[b], 1)

            def dot(st):
                job, i = st.jobs[0], st.h % 2
                ready = named(("du4", st.h)).jobs[0]
                pe.wait_ge(bank_taken[ready.bank], taken_at(ready))
                pe.wait_ge(bank_taken[job.bank], turn_at(job))
                for t in range(T):
                    ins = transpose(PS[:, job.bank, t * P:(t + 1) * P], OD[:, i, t, :])
                    if t == 1:
                        ins.then_inc(bank_full[job.bank], 1)

            pe.drain().then_inc(slots_free, SLOTS)
            for b in range(8):
                pe.drain().then_inc(bank_taken[b], 1)
            pe.wait_ge(con_loaded, 16)
            pe.wait_ge(zeros_set, 1)
            walk(pe, {"xt": xt, "acc": acc, "gu": gu, "down": down, "pb": pb, "pc": pc, "pf": pf, "cum": cum,
                      "pa": pb, "conva": project, "score": score, "turn": turn_, "out_open": out_open,
                      "value": value, "out_turn": out_turn, "lnb1": lnb1, "lnb3": lnb3, "gy": gy, "wo": wo}, 1)
            pe.wait_ge(con_loaded, 16 * 5)
            now.blk, now.l = 2, 0
            pe.wait_ge(bank_taken[0], reach(("taken", 0), 0))
            pe.matmul(PS[0:NH_A, 0, 0:384], ZS[0:32, 2, 0:NH_A],
                      ZS[0:32, 0:2, :].rearrange("p a b -> p (a b)")[:, 0:384], start=True, stop=True
                      ).then_inc(prologue_row, 1)
            pe.wait_ge(prologue_done, 1)
            pe.wait_ge(zeros_set, 2)
            walk(pe, {"xt": xt, "acc": acc, "gu": gu, "down": down, "score": score, "turn": turn_,
                      "out_open": out_open, "value": value, "out_turn": out_turn, "gy": gy, "wo": wo, "ps": ps,
                      "pk": project, "pq": project, "pv": lambda st: project(st, True), "pz": project,
                      "pconv": project, "cumg": cumg, "dtr": dtr, "dtf": dtf, "ddc": ddc, "dkk": dkk, "dl0": dl0,
                      "dla": dla, "dlb": dlb, "du1": du1, "du2": du2, "du3": du3, "du4": du4, "dot": dot}, 2)

        @block.scalar
        def _(act):
            def copy(dst, src, scale=1.0):
                return act.activation(dst, src, ACT.Copy, scale=scale)

            def norm(st):
                act.wait_ge(residual_ready, reach("residual_ready", 2 * st.s))
                for t in range(T):
                    last = act.activation(XN[:, t, :], H[:, t, :], ACT.Square, scale=D ** -0.5,
                                          accum_out=SS[:, t:t + 1])
                last.then_inc(squares_summed, 1)

            def split_high(i):
                act.wait_ge(slot_loaded[i % SLOTS], loaded_at(i))
                copy(HIGH[:, i % SLOTS, 0:width(i)], RING[:, i % SLOTS, 0:width(i)]).then_inc(high_ready, 1)

            def xt(st):
                act.wait_ge(params_loaded, reach("params_loaded", 16))
                for k2, job in enumerate(st.jobs):
                    act.wait_ge(bank_full[job.bank], full_at(job))
                    b = job.bank
                    if now.blk == 1:
                        g = prm(f"g{st.s}", 1)
                        for kk in range(2):
                            k = 2 * k2 + kk
                            last = copy(XTH[:, k, :], PS[:, b, kk * S:(kk + 1) * S], g[:, k:k + 1])
                    else:
                        last = copy(XTH[:, 2 * k2:2 * k2 + 2, :].rearrange("p a b -> p (a b)"), PS[:, b, :])
                    last.then_inc(activation_high_ready, 1)

            def gu(st):
                job = st.jobs[0]
                act.wait_ge(bank_full[job.bank], full_at(job))
                if st.j >= 2:
                    ready = named(("gu", st.s, st.j - 2)).jobs[0]
                    act.wait_ge(bank_taken[ready.bank], taken_at(ready))
                act.activation(SG[:, st.j % 2, :], PS[:, job.bank, 0:S], ACT.Silu).then_inc(gate_silu_ready, 1)

            def post(st):
                for t in range(T):
                    j0, j1 = st.acc.jobs[2 * t], st.acc.jobs[2 * t + 1]
                    act.wait_ge(bank_full[j0.bank], full_at(j0))
                    act.wait_ge(bank_full[j1.bank], full_at(j1))
                    act.activation(XN[:, t, :], PS[:, j0.bank:j0.bank + 2, :].rearrange("p a b -> p (a b)"),
                                   ACT.Square, scale=st.root, accum_out=SS[:, 2 + t:3 + t]).then_inc(squares_summed, 1)

            def lam(st):
                act.wait_ge(lambda_dots, reach("lambda_dots", 1))
                act.activation(ELAM[:, :], LAM[:, :], ACT.Exp).then_inc(lambda_exps, 1)

            def pb(st):
                job = st.jobs[0]
                act.wait_ge(bank_full[job.bank], full_at(job))
                if st.p >= 2:
                    before = named(("pb", st.p - 2)).jobs[0]
                    act.wait_ge(bank_taken[before.bank], taken_at(before))
                act.activation(TH[:, st.p % 2, 0:S], PS[:, job.bank, S:2 * S], ACT.Tanh, scale=0.5
                               ).then_inc(branch_gate_ready, 1)

            def pc(st):
                job, p = st.jobs[0], st.p
                act.wait_ge(bank_full[job.bank], full_at(job))
                src = PS[:, job.bank, :].rearrange("p (a b) -> p a b", a=2)
                if st.what in ("cq", "dq"):
                    dst = CQ if st.what == "cq" else DQ
                    last = copy(dst[:, 2 * p:2 * p + 2, :], src)
                elif st.what in ("ck", "dk"):
                    dst = CK if st.what == "ck" else DK
                    for m in range(2):
                        rows = slice(64 * m, 64 * m + 64)
                        last = copy(dst[rows, 2 * p:2 * p + 2, m, :], src[rows])
                else:
                    dst = CV if st.what == "cv" else DV
                    last = copy(dst[:, :, p * S:(p + 1) * S], src)
                last.then_inc(bank_taken[job.bank], 1)

            def pf(st):
                ready = st.jobs[0]
                act.wait_ge(bank_taken[ready.bank], taken_at(ready))
                act.activation(ZA_[:, :, :], ZF[:, :, :], ACT.Abs)
                act.drain()
                act.activation(ZA_[:, :, :], ZA_[:, :, :], ACT.Exp, scale=-1.0)
                act.drain()
                act.activation(ZL[:, :, :], ZA_[:, :, :], ACT.Ln, bias=1.0).then_inc(forget_log_ready, 1)

            def cum(st):
                job = st.jobs[0]
                act.wait_ge(bank_full[job.bank], full_at(job))
                copy(NC[0:8, :], PS[0:8, job.bank, 0:S], -1.0 / QK_SCALE).then_inc(bank_taken[job.bank], 1)

            def pa(st):
                job = st.jobs[0]
                act.wait_ge(bank_full[job.bank], full_at(job))
                if st.p >= 2:
                    before = named(("pa", st.p - 2)).jobs[0]
                    act.wait_ge(bank_taken[before.bank], taken_at(before))
                copy(TH[:, st.p % 2, 0:S], PS[:, job.bank, 0:S]).then_inc(branch_gate_ready, 1)

            def score(st):
                e = st.e
                ready = st.jobs[0]
                act.wait_ge(bank_taken[ready.bank], taken_at(ready))
                ls = LS[:, e % 16, :]
                act.activation(EX[:, e % 4, 0:P], EX[:, e % 4, 0:P], ACT.Exp, bias=NM[:, e % 4, 0:1],
                               scale=QK_SCALE, accum_out=ls[:, 0:1])
                act.activation(EX[:, e % 4, P:384], EX[:, e % 4, P:384], ACT.Exp, bias=NM[:, e % 4, 1:2],
                               scale=QK_SCALE, accum_out=ls[:, 1:2]).then_inc(probs_ready, 1)
                if st.br == "a":
                    act.activation(ES[:, e, :], NM[:, e % 4, :], ACT.Exp, bias=prm("sink", 2)[:, e:e + 1]
                                   ).then_inc(sink_exp_ready, 1)

            def turn_(st):
                job = st.jobs[0]
                n = named(("value", st.br, st.h)).at["values_summed"]
                act.wait_ge(bank_full[job.bank], full_at(job))
                if n > 3:
                    act.wait_ge(values_summed, reach("values_summed", n - 3))
                copy(PT[:, n % 3, :], PS[:, job.bank, 0:384]).then_inc(bank_taken[job.bank], 1)

            def out_norm(st):
                if st.br != "c":
                    return
                act.wait_ge(values_summed, reach("values_summed", named(("value", "c", NH_C - 1)).at["values_summed"]))
                for t in range(T):
                    for h in range(NH_C):
                        last = act.activation(JUNK[:, :], PS[:, 6 + t, h * P:(h + 1) * P], ACT.Square,
                                              scale=P ** -0.5, accum_out=SSO[:, t * 4 + h:t * 4 + h + 1])
                        if (t, h) != (T - 1, NH_C - 1):
                            act.drain()
                last.then_inc(out_squares_summed, 1)

            def out_turn(st):
                for p, job in enumerate(st.jobs):
                    act.wait_ge(bank_full[job.bank], full_at(job))
                    c = 2 * p + (4 * st.half if st.br == "a" else 0)
                    dst = {"a": YAH, "c": Y1[2][0], "d": Y1[3][0]}[st.br][:, c:c + 2, :].rearrange("p a b -> p (a b)")
                    copy(dst, PS[:, job.bank, :], SUBG[:, 0:1] if st.br == "c" else 1.0
                         ).then_inc(activation_high_ready, 1)

            def lnb3(st):
                for p, job in enumerate(st.jobs):
                    act.wait_ge(bank_full[job.bank], full_at(job))
                    for n in range(2):
                        c = 2 * p + n
                        last = act.activation(YB1[:, c, :], PS[:, job.bank, n * S:(n + 1) * S], ACT.Silu,
                                              bias=prm("blb", 1)[:, c:c + 1], scale=prm("blg", 1)[:, c:c + 1])
                    last.then_inc(bank_taken[job.bank], 1)

            def gy(st):
                job, k = st.jobs[0], st.k
                act.wait_ge(bank_full[job.bank], full_at(job))
                n = st.i * KB + k
                if n >= 2:
                    ready = named(("gy", (n - 2) // KB, (n - 2) % KB)).jobs[0]
                    act.wait_ge(bank_taken[ready.bank], taken_at(ready))
                act.activation(TH[:, n % 2, 0:S], PS[:, job.bank, 0:S], ACT.Tanh, scale=0.5).then_inc(gate_tanh_ready, 1)

            def ps(st):
                ready = st.jobs[0]
                act.wait_ge(bank_taken[ready.bank], taken_at(ready))
                act.activation(BETA[:, :, :], SBT[:, :, 0:8], ACT.Tanh, scale=0.5)
                act.activation(EAL[:, :], prm("alog", 2), ACT.Exp)
                act.activation(ZA_[:, :, :], SBT[:, :, 8:16], ACT.Abs)
                act.drain()
                act.activation(ZA_[:, :, :], ZA_[:, :, :], ACT.Exp, scale=-1.0)
                act.drain()
                act.activation(ZL[:, :, :], ZA_[:, :, :], ACT.Ln, bias=1.0).then_inc(small_logs_ready, 1)

            def pk(st):
                job = st.jobs[0]
                act.wait_ge(bank_full[job.bank], full_at(job))
                src = PS[:, job.bank, :].rearrange("p (a b) -> p a b", a=2)
                for m in range(2):
                    rows = slice(64 * m, 64 * m + 64)
                    for c in range(2):
                        last = copy(KA[rows, 2 * c + m, :], src[rows, c, :])
                last.then_inc(bank_taken[job.bank], 1)

            def pq(st):
                job = st.jobs[0]
                act.wait_ge(bank_full[job.bank], full_at(job))
                copy(QA[:, 2 * st.p:2 * st.p + 2, :].rearrange("p a b -> p (a b)"), PS[:, job.bank, :]
                     ).then_inc(bank_taken[job.bank], 1)

            def pv(st):
                job = st.jobs[0]
                act.wait_ge(bank_full[job.bank], full_at(job))
                copy(VA[:, :, :].rearrange("p a b -> p (a b)"), PS[:, job.bank, :]).then_inc(bank_taken[job.bank], 1)

            def cumg(st):
                act.wait_ge(decay_diff_ready, reach("decay_diff_ready", 1))
                act.activation(ET[:, :, :], ET[:, :, :], ACT.Exp)
                act.activation(EG[:, :, :], G[:, :, :], ACT.Exp).then_inc(decay_exps_ready, 1)

            def pz(st):
                job = st.jobs[0]
                act.wait_ge(bank_full[job.bank], full_at(job))
                if st.p >= 2:
                    ready = named(("pz", st.p - 2)).jobs[0]
                    act.wait_ge(bank_taken[ready.bank], taken_at(ready))
                act.activation(TH[:, st.p % 2, :], PS[:, job.bank, :], ACT.Tanh, scale=0.5).then_inc(z_tanh_ready, 1)

            def pconv(st):
                act.wait_ge(conv_ready, reach("conv_ready", st.at["conv_ready"]))
                if st.at["conv_silu_ready"] > 1:
                    act.wait_ge(conv_silu_ready, reach("conv_silu_ready", st.at["conv_silu_ready"] - 1))
                co = CO[:, 2 * st.w:2 * st.w + 2, :].rearrange("p a b -> p (a b)")
                act.activation(TC[:, :], co, ACT.Tanh, scale=0.5).then_inc(conv_tanh_ready, 1)

            def dtr(st):
                i = st.h % 2
                done = st.jobs[0]
                act.wait_ge(bank_full[done.bank], full_at(done))
                done = st.jobs[1]
                act.wait_ge(bank_full[done.bank], full_at(done))
                if st.h >= 2:
                    act.wait_ge(qk_rsqrt_ready, reach("qk_rsqrt_ready", named(("dtr", st.h - 2)).at["qk_rsqrt_ready"]))
                for n in range(4):
                    b = st.jobs[n // 2].bank
                    last = act.activation(P1S[:, i, 0, :], PS[:, b, n % 2 * P:(n % 2 + 1) * P], ACT.Square,
                                          accum_out=SSD[:, i, n:n + 1])
                    if n < 3:
                        act.drain()
                last.then_inc(qk_squares_summed, 1)

            def dte(st):
                i, h = st.h % 2, st.h
                b = named(("dtr", h)).jobs[0].bank
                act.wait_ge(head_scalars_ready, reach("head_scalars_ready", st.at["head_scalars_ready"]))
                sc = SC[:, i, :]
                for n, src, scale in ((0, 0, sc[:, 0:1]), (1, 1, sc[:, 1:2]), (8, 1, sc[:, 8:9]),
                                      (9, 2, HB[:, 0, h:h + 1]), (10, 3, HB[:, 1, h:h + 1])):
                    last = copy(TM[:, i, n, :], PS[:, b, src * P:(src + 1) * P], scale)
                last.then_inc(bank_taken[b], 1)

            def dtf(st):
                job = st.jobs[0]
                act.wait_ge(bank_full[job.bank], full_at(job))
                copy(FA[:, st.h % 2].rearrange("p a b -> p (a b)"), PS[:, job.bank, :]
                     ).then_inc(bank_taken[job.bank], 1)

            def ddc(st):
                i = st.h % 2
                ready = st.jobs[0]
                act.wait_ge(bank_taken[ready.bank], taken_at(ready))
                if st.h >= 2:
                    ready = named(("dkk", st.h - 2)).jobs[0]
                    act.wait_ge(bank_taken[ready.bank], taken_at(ready))
                act.activation(DEC[:, i].rearrange("p (t k) n -> p t k n", t=T)[:, :, 1, :], DD[:, i], ACT.Exp
                               ).then_inc(decay_ready, 1)

            def dla(st):
                job = st.jobs[0]
                act.wait_ge(bank_full[job.bank], full_at(job))
                copy(P1S[:, st.h % 2].rearrange("p a b -> p (a b)"), PS[:, job.bank, 0:S]
                     ).then_inc(bank_taken[job.bank], 1)

            def evac(dst, n):
                def run(st):
                    job, i = st.jobs[0], st.h % 2
                    act.wait_ge(bank_full[job.bank], full_at(job))
                    copy(dst(i), PS[:, job.bank, 0:n]).then_inc(bank_taken[job.bank], 1)
                return run

            def du4(st):
                job, i = st.jobs[0], st.h % 2
                act.wait_ge(bank_full[job.bank], full_at(job))
                for t in range(T):
                    last = act.activation(P1S[:, i, t, :], PS[:, job.bank, t * P:(t + 1) * P], ACT.Square,
                                          scale=P ** -0.5, accum_out=SSO[:, 2 * i + t:2 * i + t + 1])
                last.then_inc(out_squares_summed, 1)

            act.wait_ge(x_loaded, 16)
            act.wait_ge(zeros_set, 1)
            walk(act, {"norm": norm, "xt": xt, "gu": gu, "post": post, "lam": lam, "pb": pb, "pc": pc, "pf": pf,
                       "cum": cum, "pa": pa, "score": score, "turn": turn_, "out_norm": out_norm,
                       "out_turn": out_turn, "lnb3": lnb3, "gy": gy}, 1, split_high)
            now.blk, now.l = 2, 0
            act.wait_ge(residual_ready, reach("residual_ready", 0))
            act.wait_ge(zeros_set, 2)
            walk(act, {"xt": xt, "gu": gu, "score": score, "turn": turn_, "out_turn": out_turn, "gy": gy, "ps": ps,
                       "pk": pk, "pq": pq, "pv": pv, "cumg": cumg, "pz": pz, "pconv": pconv, "dtr": dtr, "dte": dte,
                       "dtf": dtf, "ddc": ddc, "dla": dla,
                       "du1": evac(lambda i: VW[:, i].rearrange("p a b -> p (a b)"), S),
                       "du2": evac(lambda i: VS[:, i, 0, :], P), "du3": evac(lambda i: VS[:, i, 1, :], P),
                       "du4": du4}, 2, split_high)

        @block.vector
        def _(dve):
            def norm(st):
                dve.wait_ge(rsqrt_ready, reach("rsqrt_ready", st.at["rsqrt_ready"]))
                for t in range(T):
                    last = dve.tensor_scalar(XN[:, t, :], H[:, t, :], RS[:, t:t + 1], None, ALU.mult)
                last.then_inc(normed_ready, 1)

            def split_low(i):
                if low_sem(i) is low_by_vector:
                    dve.wait_ge(high_ready, reach("high_ready", i + 1))
                    raw, high = RING[:, i % SLOTS, 0:width(i)], HIGH[:, i % SLOTS, 0:width(i)]
                    dve.tensor_tensor(LOW[:, i % SLOTS, 0:width(i)], raw, high.bitcast(F32), ALU.subtract
                                      ).then_inc(low_by_vector, 1)

            def split_here(high, low, whole):
                dve.drain()
                dve.tensor_copy(high, whole)
                dve.drain()
                return dve.tensor_tensor(low, whole, high.bitcast(F32), ALU.subtract)

            def xt(st):
                for k2, job in enumerate(st.jobs):
                    b = job.bank
                    dve.wait_ge(activation_high_ready,
                                reach("activation_high_ready", st.at["activation_high_ready"] - 3 + k2))
                    if now.blk == 1:
                        g = prm(f"g{st.s}", 1)
                        for kk in range(2):
                            k = 2 * k2 + kk
                            last = dve.scalar_tensor_tensor(out=XTL[:, k, :], in0=PS[:, b, kk * S:(kk + 1) * S],
                                                            scalar=g[:, k:k + 1], in1=XTH[:, k, :].bitcast(F32),
                                                            op0=ALU.mult, op1=ALU.subtract)
                    else:
                        last = dve.tensor_tensor(
                            XTL[:, 2 * k2:2 * k2 + 2, :].rearrange("p a b -> p (a b)"), PS[:, b, :],
                            XTH[:, 2 * k2:2 * k2 + 2, :].rearrange("p a b -> p (a b)").bitcast(F32), ALU.subtract)
                    last.then_inc(bank_taken[b], 1)

            def gu(st):
                job = st.jobs[0]
                dve.wait_ge(gate_silu_ready, reach("gate_silu_ready", st.at["gate_silu_ready"]))
                hidden = HF[:, st.j % 2, :]
                dve.tensor_tensor(hidden, SG[:, st.j % 2, :], PS[:, job.bank, S:2 * S], ALU.mult
                                  ).then_inc(bank_taken[job.bank], 1)
                split_here(HTH[:, st.j % 4, :], HTL[:, st.j % 4, :], hidden).then_inc(hidden_ready, 1)

            def out_turn(st):
                for p, job in enumerate(st.jobs):
                    c = 2 * p + (4 * st.half if st.br == "a" else 0)
                    high, low = (v[:, c:c + 2, :].rearrange("p a b -> p (a b)")
                                 for v in {"a": (YAH, YAL), "c": Y1[2], "d": Y1[3]}[st.br])
                    dve.wait_ge(activation_high_ready,
                                reach("activation_high_ready", st.at["activation_high_ready"] - 1 + p))
                    if st.br == "c":
                        ins = dve.scalar_tensor_tensor(out=low, in0=PS[:, job.bank, :], scalar=SUBG[:, 0:1],
                                                       in1=high.bitcast(F32), op0=ALU.mult, op1=ALU.subtract)
                    else:
                        ins = dve.tensor_tensor(low, PS[:, job.bank, :], high.bitcast(F32), ALU.subtract)
                    ins.then_inc(bank_taken[job.bank], 1)

            def lnb3(st):
                for job in st.jobs:
                    dve.wait_ge(bank_taken[job.bank], taken_at(job))
                dve.tensor_copy(Y1[1][0], YB1)
                dve.drain()
                dve.tensor_tensor(Y1[1][1], YB1, Y1[1][0].bitcast(F32), ALU.subtract).then_inc(branch_b_ready, 1)

            def post(st):
                dve.wait_ge(feature_rows_loaded, reach("feature_rows_loaded", 16 * (st.s + 1)))
                for t in range(T):
                    dve.wait_ge(rsqrt_ready, reach("rsqrt_ready", st.at["rsqrt_ready"] - 1 + t))
                    for n in range(2):
                        b = st.acc.jobs[2 * t + n].bank
                        cols = slice(n * HALF, (n + 1) * HALF)
                        dve.scalar_tensor_tensor(out=XN[:, t, cols], in0=PS[:, b, :], scalar=RS[:, 2 + t:3 + t],
                                                 in1=PG[:, 0, cols], op0=ALU.mult, op1=ALU.mult
                                                 ).then_inc(bank_taken[b], 1)
                    dve.drain()
                    dve.tensor_tensor(H[:, t, :], H[:, t, :], XN[:, t, :], ALU.add).then_inc(residual_ready, 1)

            def lam(st):
                lv = prm("lam", 1, 4)
                for n in range(2):
                    last = dve.tensor_tensor_reduce(TMP[:, n, 0:64], lv[:, 2 * n, :], lv[:, 2 * n + 1, :], 1.0, 0.0,
                                                    ALU.mult, ALU.add, LAM[:, n:n + 1])
                last.then_inc(lambda_dots, 1)
                dve.tensor_scalar(BWH.rearrange("p a b -> p (a b)"), prm("bw", 1), 0.5, None, ALU.mult)
                dve.tensor_tensor(SUBG[:, :], prm("sub", 1), prm("lami", 1)[:, 1:2], ALU.mult)
                dve.wait_ge(lambda_exps, reach("lambda_exps", 1))
                dve.tensor_tensor(NLAM[:, :], ELAM[:, 1:2], ELAM[:, 0:1], ALU.subtract)
                dve.drain()
                dve.tensor_tensor(NLAM[:, :], NLAM[:, :], prm("lami", 1)[:, 0:1], ALU.subtract
                                  ).then_inc(lambda_ready, 1)
                dve.drain()

            def pb(st):
                job = st.jobs[0]
                dve.wait_ge(branch_gate_ready, reach("branch_gate_ready", st.at["branch_gate_ready"]))
                dve.scalar_tensor_tensor(out=ZB[:, st.p, :], in0=TH[:, st.p % 2, 0:S], scalar=1.0,
                                         in1=PS[:, job.bank, 0:S], op0=ALU.add, op1=ALU.mult
                                         ).then_inc(bank_taken[job.bank], 1)

            def convb(st):
                for n in range(st.a, st.b):
                    tap = 30 - n
                    dve.drain()
                    for c in range(4):
                        w = BWH[:, tap, c:c + 1]
                        if n == 0:
                            last = dve.tensor_scalar(ACCB[:, c, :], ZB[:, c, :], w, prm("bb", 1)[:, c:c + 1],
                                                     ALU.mult, ALU.add)
                        else:
                            last = dve.scalar_tensor_tensor(out=ACCB[:, c, n:S], in0=ZB[:, c, 0:S - n], scalar=w,
                                                            in1=ACCB[:, c, n:S], op0=ALU.mult, op1=ALU.add)
                if st.b == 31:
                    last.then_inc(conv_b_ready, 1)

            def pf(st):
                job = st.jobs[0]
                dve.wait_ge(bank_full[job.bank], full_at(job))
                for t in range(T):
                    last = dve.tensor_tensor(ZF[:, t, :], PS[:, job.bank, t * 8:(t + 1) * 8], prm("fb", 1), ALU.add)
                last.then_inc(bank_taken[job.bank], 1)
                dve.drain()
                dve.tensor_scalar(LF[:, :, :], ZF[:, :, :], 0.0, None, ALU.min)
                dve.drain()
                dve.wait_ge(forget_log_ready, reach("forget_log_ready", 1))
                dve.tensor_tensor(LF[:, :, :], LF[:, :, :], ZL[:, :, :], ALU.subtract).then_inc(log_forget_ready, 1)

            def pa(st):
                job = st.jobs[0]
                dve.wait_ge(branch_gate_ready, reach("branch_gate_ready", st.at["branch_gate_ready"]))
                dve.tensor_tensor(ZA[:, st.p, :], TH[:, st.p % 2, 0:S], PS[:, job.bank, S:2 * S], ALU.mult
                                  ).then_inc(bank_taken[job.bank], 1)

            def conva(st):
                job, c2 = st.jobs[0], 2 * st.p
                aw = prm("aw", 1, 3)
                for n in range(3):
                    dve.drain()
                    for c in (c2, c2 + 1):
                        w = aw[:, 2 - n, c:c + 1]
                        if n == 0:
                            dve.tensor_scalar(ACCA[:, c, :], ZA[:, c, :], w, None, ALU.mult)
                        else:
                            dve.scalar_tensor_tensor(out=ACCA[:, c, n:S], in0=ZA[:, c, 0:S - n], scalar=w,
                                                     in1=ACCA[:, c, n:S], op0=ALU.mult, op1=ALU.add)
                dve.drain()
                dve.wait_ge(bank_full[job.bank], full_at(job))
                dst = ACCA[:, c2:c2 + 2, :]
                dve.tensor_tensor(dst.rearrange("p a b -> p (a b)"), dst.rearrange("p a b -> p (a b)"),
                                  PS[:, job.bank, :], ALU.mult).then_inc(bank_taken[job.bank], 1)
                split_here(Y1[0][0][:, c2:c2 + 2, :], Y1[0][1][:, c2:c2 + 2, :], dst).then_inc(branch_a_ready, 1)

            def score(st):
                job, e = st.jobs[0], st.e
                b = job.bank
                dve.wait_ge(bank_full[job.bank], full_at(job))
                if e >= 4:
                    done = named(("turn", st.br, (e - 4) // (2 if st.br == "c" else 1))).jobs[0]
                    dve.wait_ge(bank_full[done.bank], full_at(done))
                    if st.br == "a":
                        dve.wait_ge(sink_exp_ready, reach("sink_exp_ready", named(("score", "a", e - 4)).at["sink_exp_ready"]))
                elif st.br == "d":
                    done = named(("turn", "c", NH_C - 1)).jobs[0]
                    dve.wait_ge(bank_full[done.bank], full_at(done))
                if st.br == "a" and e == 0:
                    dve.wait_ge(bias_loaded, reach("bias_loaded", 16))
                bias = {"c": lambda: cst("alibi", 1, NH_C)[:, e // 2, :], "d": lambda: cst("causal", 1),
                        "a": lambda: BIAS[:, e, :]}[st.br]()
                dve.memset(TOUCH[:, :], 0.0)
                dve.tensor_tensor_reduce(EX[:, e % 4, 0:P], PS[:, b, 0:P], bias[:, P:S], 1.0, -3e38, ALU.add,
                                         ALU.max, MX[:, e % 4, 0:1])
                dve.tensor_tensor_reduce(EX[:, e % 4, P:384], PS[:, b, P:384], bias, 1.0, -3e38, ALU.add,
                                         ALU.max, MX[:, e % 4, 1:2])
                dve.drain()
                if st.br == "a":
                    last = dve.tensor_scalar(NM[:, e % 4, :], MX[:, e % 4, :], SINK8[:, e:e + 1], -QK_SCALE,
                                             ALU.max, ALU.mult)
                else:
                    last = dve.tensor_scalar(NM[:, e % 4, :], MX[:, e % 4, :], -QK_SCALE, None, ALU.mult)
                last.then_inc(bank_taken[b], 1)

            def diff(st):
                h = st.h
                e0, e1 = 2 * h % 4, (2 * h + 1) % 4
                dve.drain()
                dve.wait_ge(probs_ready, reach("probs_ready", named(("score", "c", 2 * h + 1)).at["probs_ready"]))
                if h == 0:
                    dve.wait_ge(lambda_ready, reach("lambda_ready", 1))
                dve.reciprocal(RC[:, 0:4], LS[:, 2 * h:2 * h + 2, :].rearrange("p a b -> p (a b)"))
                dve.drain()
                dve.tensor_scalar(RC[:, 2:4], RC[:, 2:4], NLAM[:, 0:1], None, ALU.mult)
                parts = ((0, slice(0, P)), (1, slice(P, 384)))
                for t, c in parts:
                    dve.tensor_scalar(EX[:, e0, c], EX[:, e0, c], RC[:, t:t + 1], None, ALU.mult)
                dve.drain()
                for t, c in parts:
                    last = dve.scalar_tensor_tensor(out=EX[:, e0, c], in0=EX[:, e1, c], scalar=RC[:, 2 + t:3 + t],
                                                    in1=EX[:, e0, c], op0=ALU.mult, op1=ALU.add)
                last.then_inc(probs_combined, 1)

            def out_norm(st):
                key = st.half if st.br == "a" else st.br
                jobs = named(("oo", key)).jobs
                if st.br == "c":
                    dve.wait_ge(out_rsqrt_ready, reach("out_rsqrt_ready", st.at["out_rsqrt_ready"]))
                    n, w = 4, P
                else:
                    n, w = 8, 64
                    first = 8 * st.half if st.br == "a" else 0
                    dve.wait_ge(values_summed, reach("values_summed", named(("value", st.br, first + 7)).at["values_summed"]))
                    if st.br == "a":
                        dve.wait_ge(sink_exp_ready, reach("sink_exp_ready", named(("score", "a", first + 7)).at["sink_exp_ready"]))
                        ls = LS[:, first:first + 8, :]
                        dve.tensor_tensor(ls, ls, ES[:, first:first + 8, :], ALU.add)
                        dve.drain()
                    dve.reciprocal(RL[:, first:first + 8, :], LS[:, first:first + 8, :])
                    dve.drain()
                    before = {"d": ("ot", "c"), "a": ("ot", 0)}[st.br]
                    if not (st.br == "a" and st.half == 0):
                        for job in named(before).jobs:
                            dve.wait_ge(bank_full[job.bank], full_at(job))
                for t in range(T):
                    if st.br == "c":
                        r = RSO[:, t * 4:t * 4 + 4].unsqueeze(2)
                    else:
                        r = RL[:, first:first + 8, t].unsqueeze(2)
                    dve.tensor_tensor(ON[:, t, :].rearrange("p (a b) -> p a b", a=n),
                                      PS[:, 6 + t, :].rearrange("p (a b) -> p a b", a=n),
                                      r.to_broadcast([P, n, w]), ALU.mult).then_inc(bank_taken[6 + t], 1)

            def lnb1(st):
                for t, job in enumerate(st.jobs):
                    dve.wait_ge(bank_full[job.bank], full_at(job))
                    dve.bn_stats(ST[:, t, :], PS[:, job.bank, :])
                    dve.drain()
                    dve.bn_aggr(MV[:, t, :], ST[:, t, :]).then_inc(mean_var_ready, 1)
                dve.drain()
                for t, job in enumerate(st.jobs):
                    dve.wait_ge(branch_b_rsqrt_ready, reach("branch_b_rsqrt_ready", st.at["branch_b_rsqrt_ready"] - 1 + t))
                    dve.tensor_scalar(BN[:, t, :], PS[:, job.bank, :], MV[:, t, 0:1], RSB[:, t:t + 1],
                                      ALU.subtract, ALU.mult).then_inc(bank_taken[job.bank], 1)

            def gy(st):
                job, k, i = st.jobs[0], st.k, st.i
                n = i * KB + k
                dve.wait_ge(gate_tanh_ready, reach("gate_tanh_ready", st.at["gate_tanh_ready"]))
                dst = MG[:, k, :] if i == 0 else TMP[:, n % 2, :]
                dve.scalar_tensor_tensor(out=dst, in0=TH[:, n % 2, 0:S], scalar=1.0,
                                         in1=PS[:, job.bank, S:2 * S], op0=ALU.add, op1=ALU.mult
                                         ).then_inc(bank_taken[job.bank], 1)
                if i:
                    dve.drain()
                    dve.tensor_tensor(MG[:, k, :], MG[:, k, :], TMP[:, n % 2, :], ALU.add)
                if i == (3 if now.blk == 1 else 1):
                    high = (MGH1 if now.blk == 1 else MGH2)[:, k, :]
                    split_here(high, MGL[:, k, :], MG[:, k, :]).then_inc(merged_ready, 1)

            def scale_h(st):
                for job in named(("xt", st.s)).jobs:
                    dve.wait_ge(bank_full[job.bank], full_at(job))
                dve.tensor_scalar(H[:, :, :], H[:, :, :], ALPHA, None, ALU.mult)
                if st.s == 1:
                    dve.tensor_scalar(GDH[:, :], prm("dng", 2), 0.5, None, ALU.mult)
                    dve.tensor_scalar(SINK8[:, :], prm("sink", 2), 1.0 / QK_SCALE, None, ALU.mult)
                dve.drain()

            def post2(st):
                dve.wait_ge(feature_rows_loaded, reach("feature_rows_loaded", 16 * (st.s + 1)))
                for t in range(T):
                    for n in range(2):
                        job = st.acc.jobs[2 * t + n]
                        cols = slice(n * HALF, (n + 1) * HALF)
                        dve.wait_ge(bank_full[job.bank], full_at(job))
                        dve.scalar_tensor_tensor(out=XN[:, t, cols], in0=PS[:, job.bank, :], scalar=0.5,
                                                 in1=H[:, t, cols], op0=ALU.mult, op1=ALU.add
                                                 ).then_inc(bank_taken[job.bank], 1)
                    dve.drain()
                    for n in range(2):
                        dve.bn_stats(ST[:, 2 * t + n, :], XN[:, t, n * HALF:(n + 1) * HALF])
                    dve.drain()
                    dve.bn_aggr(MV[:, t, :], ST[:, 2 * t:2 * t + 2, :]).then_inc(mean_var_ready, 1)
                dve.drain()
                for t in range(T):
                    dve.wait_ge(rsqrt_ready, reach("rsqrt_ready", st.at["rsqrt_ready"] - 1 + t))
                    dve.tensor_scalar(XN[:, t, :], XN[:, t, :], MV[:, t, 0:1], RS[:, 2 + t:3 + t],
                                      ALU.subtract, ALU.mult)
                    dve.drain()
                    dve.tensor_tensor(XN[:, t, :], XN[:, t, :], PG[:, 0, :], ALU.mult)
                    dve.drain()
                    dve.tensor_tensor(H[:, t, :], XN[:, t, :], PG[:, 1, :], ALU.add).then_inc(residual_ready, 1)

            def ps(st):
                job = st.jobs[0]
                dve.wait_ge(bank_full[job.bank], full_at(job))
                for t in range(T):
                    c = t * 16
                    dve.tensor_copy(SBT[:, t, 0:8], PS[:, job.bank, c:c + 8])
                    last = dve.tensor_tensor(SBT[:, t, 8:16], PS[:, job.bank, c + 8:c + 16], prm("dtb", 2), ALU.add)
                last.then_inc(bank_taken[job.bank], 1)
                dve.drain()
                dve.tensor_scalar(GG[:, :, :], SBT[:, :, 8:16], 0.0, None, ALU.max)
                dve.drain()
                dve.wait_ge(small_logs_ready, reach("small_logs_ready", 1))
                dve.tensor_tensor(GG[:, :, :], GG[:, :, :], ZL[:, :, :], ALU.add)
                dve.tensor_scalar(BETA[:, :, :], BETA[:, :, :], 0.5, 0.5, ALU.mult, ALU.add)
                dve.drain()
                for t in range(T):
                    last = dve.scalar_tensor_tensor(out=GG[:, t, :], in0=GG[:, t, :], scalar=-1.0, in1=EAL[:, :],
                                                    op0=ALU.mult, op1=ALU.mult)
                last.then_inc(log_decay_ready, 1)
                dve.tensor_scalar(HB[:, :, :], BETA[:, :, :], 0.5, None, ALU.mult)
                dve.drain()

            def cumg(st):
                job = st.jobs[0]
                dve.wait_ge(bank_full[job.bank], full_at(job))
                dve.tensor_copy(G[:, :, :].rearrange("p a b -> p (a b)"), PS[:, job.bank, 0:16])
                dve.tensor_copy(GL[:, :, :].rearrange("p a b -> p (a b)"), PS[:, job.bank, 16:32])
                dve.tensor_copy(GTR[0:8, :], PS[0:8, job.bank, 64:64 + S]
                                ).then_inc(bank_taken[job.bank], 1)
                dve.drain()
                dve.tensor_tensor(ET[:, :, :], GL[:, :, :], G[:, :, :], ALU.subtract).then_inc(decay_diff_ready, 1)
                dve.wait_ge(decay_exps_ready, reach("decay_exps_ready", 1))
                dve.tensor_tensor(BEG[:, :, :], BETA[:, :, :], EG[:, :, :], ALU.mult).then_inc(decay_scalars_ready, 1)
                dve.drain()

            def pz(st):
                job = st.jobs[0]
                dve.wait_ge(z_tanh_ready, reach("z_tanh_ready", st.at["z_tanh_ready"]))
                dve.scalar_tensor_tensor(out=ZS[:, 2 * st.p:2 * st.p + 2, :].rearrange("p a b -> p (a b)"),
                                         in0=TH[:, st.p % 2, :], scalar=1.0, in1=PS[:, job.bank, :],
                                         op0=ALU.add, op1=ALU.mult).then_inc(bank_taken[job.bank], 1)

            def pconv(st):
                job, w = st.jobs[0], st.w
                b = job.bank
                cw = prm("cw", 2, 4)
                co = CO[:, 2 * w:2 * w + 2, :]
                dve.wait_ge(bank_full[job.bank], full_at(job))
                if st.hp >= 1:
                    for h in (2 * st.hp - 2, 2 * st.hp - 1):
                        done = named(("dtr", h)).jobs[1]
                        dve.wait_ge(bank_full[done.bank], full_at(done))
                for n in range(4):
                    for c in range(2):
                        tap = cw[:, 3 - n, 8 * w + 2 * st.hp + c:8 * w + 2 * st.hp + c + 1]
                        src = PS[:, b, c * S:(c + 1) * S - n]
                        if n == 0:
                            last = dve.tensor_scalar(co[:, c, :], src, tap, None, ALU.mult)
                        else:
                            last = dve.scalar_tensor_tensor(out=co[:, c, n:S], in0=src, scalar=tap,
                                                            in1=co[:, c, n:S], op0=ALU.mult, op1=ALU.add)
                    if n < 3:
                        dve.drain()
                last.then_inc(bank_taken[b], 1)
                dve.drain().then_inc(conv_ready, 1)
                dve.wait_ge(conv_tanh_ready, reach("conv_tanh_ready", st.at["conv_tanh_ready"]))
                flat = co.rearrange("p a b -> p (a b)")
                dve.scalar_tensor_tensor(out=flat, in0=TC[:, :], scalar=1.0, in1=flat, op0=ALU.add, op1=ALU.mult
                                         ).then_inc(conv_silu_ready, 1)

            def dte(st):
                i, h = st.h % 2, st.h
                b = named(("dtr", h)).jobs[1].bank
                sc, rd = SC[:, i, :], RD[:, i, :]
                dve.wait_ge(qk_rsqrt_ready, reach("qk_rsqrt_ready", named(("dtr", h)).at["qk_rsqrt_ready"]))
                dve.tensor_scalar(sc[:, 0:2], rd[:, 0:2], 128.0 ** -0.5, None, ALU.mult)
                dve.tensor_copy(sc[:, 2:4], rd[:, 2:4])
                dve.tensor_tensor(sc[:, 4:6], rd[:, 2:4], BETA[:, :, h], ALU.mult)
                dve.tensor_tensor(sc[:, 6:7], rd[:, 2:3], ET[:, 0, h:h + 1], ALU.mult)
                dve.tensor_scalar(sc[:, 7:8], rd[:, 3:4], BEG[:, 1, h:h + 1], -1.0, ALU.mult, ALU.mult)
                dve.tensor_scalar(sc[:, 8:9], rd[:, 1:2], EG[:, 1, h:h + 1], 128.0 ** -0.5, ALU.mult, ALU.mult
                                  ).then_inc(head_scalars_ready, 1)
                dve.drain()
                for n, src, s in ((2, 0, 2), (3, 1, 3), (4, 0, 4), (5, 1, 5), (6, 0, 6), (7, 1, 7)):
                    last = dve.tensor_scalar(TM[:, i, n, :], PS[:, b, src * P:(src + 1) * P], sc[:, s:s + 1], None,
                                             ALU.mult)
                last.then_inc(bank_taken[b], 1)

            def ddc(st):
                job, i, h = st.jobs[0], st.h % 2, st.h
                dve.wait_ge(bank_full[job.bank], full_at(job))
                for t in range(T):
                    last = dve.scalar_tensor_tensor(out=DD[:, i, t, :], in0=PS[:, job.bank, t * P:(t + 1) * P],
                                                    scalar=G[:, t, h:h + 1], in1=cst("maskt", 2),
                                                    op0=ALU.subtract, op1=ALU.add)
                last.then_inc(bank_taken[job.bank], 1)

            def dtf(st):
                job = st.jobs[1]
                dve.wait_ge(bank_full[job.bank], full_at(job))
                dve.tensor_copy(FBM[:, st.h % 2].rearrange("p a b -> p (a b)"), PS[:, job.bank, 0:384]
                                ).then_inc(bank_taken[job.bank], 1)

            def dkk(st):
                job, i = st.jobs[0], st.h % 2
                dve.wait_ge(bank_full[job.bank], full_at(job))
                dve.wait_ge(strict_decay_ready, reach("strict_decay_ready", named(("ddc", st.h)).at["strict_decay_ready"]))
                dve.tensor_tensor(AL[:, i].rearrange("p a b -> p (a b)"), PS[:, job.bank, :],
                                  DEC[:, i].rearrange("p a b -> p (a b)"), ALU.mult
                                  ).then_inc(bank_taken[job.bank], 1)

            def dl0(st):
                job, i = st.jobs[0], st.h % 2
                dve.wait_ge(bank_full[job.bank], full_at(job))
                for t in range(T):
                    dve.tensor_tensor(TT[:, i, t, :], IDENT, PS[:, job.bank, t * P:(t + 1) * P], ALU.subtract)
                for t in range(T):
                    last = dve.tensor_tensor(TT[:, i, 2 + t, :], IDENT, MT[:, i, t, :], ALU.subtract)
                last.then_inc(bank_taken[job.bank], 1)

            def dlb(st):
                job, i = st.jobs[0], st.h % 2
                dve.wait_ge(bank_full[job.bank], full_at(job))
                tt = TT[:, i].rearrange("p a b -> p (a b)")
                c = slice(0, 2 * S) if st.s < LEVELS - 1 else slice(S, 2 * S)
                dve.tensor_tensor(tt[:, c], tt[:, c], PS[:, job.bank, c], ALU.subtract
                                  ).then_inc(bank_taken[job.bank], 1)

            def du4(st):
                job, i = st.jobs[0], st.h % 2
                dve.wait_ge(out_rsqrt_ready, reach("out_rsqrt_ready", st.at["out_rsqrt_ready"]))
                for t in range(T):
                    last = dve.tensor_scalar(OD[:, i, t, :], PS[:, job.bank, t * P:(t + 1) * P],
                                             RSO[:, 2 * i + t:2 * i + t + 1], None, ALU.mult)
                last.then_inc(bank_taken[job.bank], 1)

            def dot(st):
                job, i, h = st.jobs[0], st.h % 2, st.h
                dve.wait_ge(bank_full[job.bank], full_at(job))
                dve.scalar_tensor_tensor(out=TMP[:, h % 2, :], in0=PS[:, job.bank, 0:S], scalar=GDH[:, 0:1],
                                         in1=ZS[:, h, :], op0=ALU.mult, op1=ALU.mult
                                         ).then_inc(bank_taken[job.bank], 1)
                split_here(YBH[:, h, :], YBL[:, h, :], TMP[:, h % 2, :]).then_inc(delta_out_ready, 1)

            dve.wait_ge(x_loaded, 16)
            dve.drain().then_inc(residual_ready, 1)
            dve.wait_ge(con_loaded, 16)
            walk(dve, {"norm": norm, "xt": xt, "gu": gu, "post": post, "lam": lam, "pb": pb, "convb": convb,
                       "pf": pf, "pa": pa, "conva": conva, "score": score, "diff": diff, "out_norm": out_norm,
                       "lnb1": lnb1, "lnb3": lnb3, "out_turn": out_turn, "gy": gy}, 1, split_low)
            dve.wait_ge(prologue_row, 1)
            dve.scalar_tensor_tensor(out=ZS[0:NH_A, 6:8, :].rearrange("p a b -> p (a b)")[:, 0:384],
                                     in0=PS[0:NH_A, 0, 0:384], scalar=1.0 / QK_SCALE,
                                     in1=ZS[0:NH_A, 4:6, :].rearrange("p a b -> p (a b)")[:, 0:384],
                                     op0=ALU.mult, op1=ALU.add).then_inc(prologue_done, 1)
            walk(dve, {"xt": xt, "gu": gu, "score": score, "out_norm": out_norm, "gy": gy, "scale_h": scale_h,
                       "post2": post2, "ps": ps, "cumg": cumg, "pz": pz, "pconv": pconv, "dte": dte, "ddc": ddc,
                       "dtf": dtf, "dkk": dkk, "dl0": dl0, "dlb": dlb, "du4": du4, "dot": dot,
                       "out_turn": out_turn}, 2, split_low)


def _cols_unit(w, c):
    return w[:, c * 256:(c + 1) * 256].reshape(-1, P, 256).transpose(1, 0, 2).reshape(P, UNIT)


def _pair_unit(v, i, w, j):
    return _cols_unit(np.concatenate([v[:, i * P:(i + 1) * P], w[:, j * P:(j + 1) * P]], 1), 0)


def _rows_unit(w, r):
    return w[r * 256:(r + 1) * 256].reshape(2, P, D).transpose(1, 0, 2).reshape(P, UNIT)


def _by_feature(v):
    v = v.reshape(-1, v.shape[-1] // P, P)
    return v.transpose(2, 0, 1).reshape(P, -1)


def _rows(v):
    return np.broadcast_to(v.reshape(1, -1), (P, v.size))


def lay_out(a):
    s1 = np.zeros((L, PLANS[1].units, P, UNIT), np.float32)
    s2 = np.empty((L, PLANS[2].units, P, UNIT), np.float32)
    prm1, prm2 = np.empty((L, P, NCOL1), np.float32), np.empty((L, P, NCOL2), np.float32)
    order = [8 * (b // 4) + b % 4 + 4 * u for b in range(8) for u in range(2)]
    for l in range(L):
        w_in = a["w_in"][l]
        w_main = np.concatenate([w_in[:, :5632], w_in[:, 5640:]], 1)
        outs = [a[n][l] for n in ("a_w_out", "b_w_out", "c_w_out", "d_w_out")]
        for i, key in enumerate(PLANS[1].stream):
            f = "ffn1" if key[0] in ("gu", "d") and key[1] == 0 else "ffn2"
            if key[0] == "gu":
                u = _pair_unit(a[f + "_w_gate"][l], key[2], a[f + "_w_up"][l], key[2])
            elif key[0] == "d":
                u = _rows_unit(a[f + "_w_down"][l], key[2])
            elif key[0] == "ba":
                u = _pair_unit(w_main, 12 + key[1], w_main, 16 + key[1])
            elif key[0] == "aa":
                u = _pair_unit(w_main, 4 + key[1], w_main, 8 + key[1])
            elif key[0] == "w":
                u = _cols_unit(w_main, key[1])
            elif key[0] == "gy":
                k, g = key[2], 44 + 8 * key[1] + key[2]
                u = np.zeros((P, UNIT), np.float32)
                rows = np.concatenate([w_main[:, g * P:(g + 1) * P], outs[key[1]][:, k * P:(k + 1) * P]])
                u[:, :12 * P] = rows.reshape(12, P, P).transpose(1, 0, 2).reshape(P, 12 * P)
            else:
                u = _rows_unit(a["w_o"][l], key[1])
            s1[l, i] = u
        lam_init = 0.8 - 0.6 * math.exp(-0.3 * l)
        parts = {"g0": _by_feature(a["ffn1_pre_g"][l]), "g1": _by_feature(a["mix_pre_g"][l]),
                 "g2": _by_feature(a["ffn2_pre_g"][l]), "aw": _by_feature(a["a_conv_w"][l]),
                 "bw": _by_feature(a["b_conv_w"][l]), "bb": _by_feature(a["b_conv_b"][l]),
                 "blg": _by_feature(a["b_ln_g"][l]), "blb": _by_feature(a["b_ln_b"][l]),
                 "sub": _by_feature(a["c_subln_g"][l]),
                 "lami": _rows(np.array([lam_init, 1.0 - lam_init], np.float32)),
                 "fb": _rows(a["d_forget_b"][l]),
                 "lam": _rows(np.concatenate([a[n][l] for n in ("c_lam_q1", "c_lam_k1", "c_lam_q2", "c_lam_k2")])),
                 "wf": w_in[:, 5632:5640].reshape(KB, P, 8).transpose(1, 0, 2).reshape(P, 64)}
        for name, (c0, c1) in COL1.items():
            prm1[l, :, c0:c1] = parts[name]
        w_in = a["w_in_2"][l]
        qa = w_in[:, :1024].reshape(D, NH_A, 64)[:, order].reshape(D, 1024)
        w_main = np.concatenate([qa, w_in[:, 1024:4608], w_in[:, 4624:]], 1)
        for i, key in enumerate(PLANS[2].stream):
            f = 0 if key[0] in ("gu", "d") and key[1] == 0 else 1
            if key[0] == "gu":
                w13 = a["ffn_w13_2"][l, f]
                u = _pair_unit(w13, key[2], w13, FB + key[2])
            elif key[0] == "d":
                u = _rows_unit(a["ffn_w2_2"][l, f], key[2])
            elif key[0] == "w":
                u = _cols_unit(w_main, key[1])
            elif key[0] == "gy":
                out = a["w_branch_a_2" if key[1] == 0 else "w_branch_b_2"][l]
                u = _pair_unit(w_main, 44 + 8 * key[1] + key[2], out, key[2])
            else:
                u = _rows_unit(a["w_out_2"][l], key[1])
            s2[l, i] = u
        parts = {"cw": _by_feature(a["conv_w_2"][l]), "dng": _by_feature(a["dn_norm_g_2"][l]),
                 "sink": _rows(a["sinks_2"][l]), "dtb": _rows(a["dt_bias_2"][l]), "alog": _rows(a["a_log_2"][l]),
                 "ws": w_in[:, 4608:4624].reshape(KB, P, 16).transpose(1, 0, 2).reshape(P, 128)}
        for name, (c0, c1) in COL2.items():
            prm2[l, :, c0:c1] = parts[name]
    feat1 = np.stack([a["ffn1_post_g"], a["mix_post_g"], a["ffn2_post_g"]], 1)
    feat2 = np.stack([a["ln_g_2"], a["ln_b_2"]], 2)
    onehot, rowmask = bias_table()
    return {"x": a["x"], "stream1": s1, "stream2": s2, "prm1": prm1, "prm2": prm2, "feat1": feat1, "feat2": feat2,
            "con": constants(), "onehot": onehot, "rowmask": rowmask.reshape(1, 384), "relb": a["rel_bias_2"]}


def kernel(**inputs):
    import concourse.bacc as _bacc
    from concourse.bass_utils import run_bass_kernel_spmd as _run

    a = {k: np.asarray(v) for k, v in inputs.items()}
    arrays = {k: np.ascontiguousarray(v) for k, v in lay_out(a).items()}
    nc = _bacc.Bacc("TRN2", target_bir_lowering=False, num_devices=1)
    aps = {n: nc.dram_tensor(n, v.shape, F32, kind="ExternalInput").ap() for n, v in arrays.items()}
    aps["toep"] = nc.dram_tensor("toeplitz_rows", (NH_A, P, 384), F32, kind="Internal").ap()
    aps["out"] = nc.dram_tensor("out", (1, S, D), F32, kind="ExternalOutput").ap()
    build_kernel(nc, **aps)
    r = _run(nc, [arrays], core_ids=[0])
    return r.results[0]["out"]
```

```python
import math
from contextlib import ExitStack

import numpy as np

import concourse.bass as bass
import concourse.mybir as mybir
from concourse.alu_op_type import AluOpType as ALU

ACT = mybir.ActivationFunctionType
F32 = mybir.dt.float32
F32R = mybir.dt.float32r

P = 128
D = 1024
KB = D // P
S = 256
T = S // P
L = 2
FF = 2816
FB = FF // P
FP = FF // 256
EPS = 1e-6
LN_EPS = 1e-5
SLOTS = 4
AHEAD = 3
UNIT = 2048
ALPHA = (2 * L) ** 0.25
RES_EPS = LN_EPS / ALPHA ** 2
MASKED = -1e30
HALF = 512
NH_C, NH_D, NH_A, NH_B = 4, 8, 16, 8
QK_SCALE = 0.125
LEVELS = 7

_c = 0


def _cols(table):
    out, at = {}, 0
    for name, n in table:
        out[name] = (at, at + n)
        at += n
    return out, at


COL1, NCOL1 = _cols([("g0", 8), ("g1", 8), ("g2", 8), ("aw", 12), ("bw", 124), ("bb", 4), ("blg", 4),
                     ("blb", 4), ("sub", 1), ("lami", 2), ("fb", 8), ("lam", 256), ("wf", 64)])
COL2, NCOL2 = _cols([("cw", 96), ("dng", 1), ("sink", 16), ("dtb", 8), ("alog", 8), ("ws", 128),
                     ("ing", 24), ("inb", 24)])
CON1, NCON1 = _cols([("ident", 128), ("tri", 512), ("causal", 256), ("alibi", 1024)])
CON2, NCON2 = _cols([("ident", 128), ("tri", 128), ("ones", 128), ("maskt", 128), ("strict", 128),
                     ("level", P), ("masks", (LEVELS - 1) * 2 * P // 4)])
NCON = max(NCON1, NCON2)


class Job:

    def __init__(self, bank, turn, full, taken):
        self.bank, self.turn, self.full, self.taken = bank, turn, full, taken


class Step:

    def __init__(self, kind, unit, a=None, acc=None, b=None, br=None, e=None, h=None, half=None, hp=None,
                 i=None, j=None, k=None, p=None, root=None, s=None, src=None, w=None, what=None):
        self.kind, self.unit = kind, unit
        self.jobs, self.at, self.split = [], {}, []
        self.s, self.j, self.k, self.a, self.b, self.p, self.w = s, j, k, a, b, p, w
        self.h, self.e, self.hp, self.i, self.br, self.half, self.what = h, e, hp, i, br, half, what
        self.acc, self.root, self.src = acc, root, src


class Now:

    def __init__(self):
        self.blk, self.l = 1, 0


class Plan:

    def __init__(self):
        self.steps, self.count, self.stream, self.named = [], {}, [], {}
        self.by_pool = ("w", "ba", "aa", "gy")
        self.rot = {"lo": 0, "hi": 0, "s": 0}

    def tick(self, name, n):
        self.count[name] = self.count.get(name, 0) + n
        return self.count[name]

    def job(self, bank, fulls=1, takes=1):
        if isinstance(bank, str):
            pool = {"lo": (0, 1, 2, 3), "hi": (4, 5, 6, 7), "s": (4, 5)}[bank]
            self.rot[bank] += 1
            bank = pool[(self.rot[bank] - 1) % len(pool)]
        turn = self.count.get(("taken", bank), 0)
        return Job(bank, turn, self.tick(("full", bank), fulls), self.tick(("taken", bank), takes))

    def step(self, kind, name=None, banks=(), signals=(), unit=None, **args):
        st = Step(kind, unit, **args)
        st.jobs = [self.job(*(b if isinstance(b, tuple) else (b,))) for b in banks]
        st.at = {s: self.tick(s, n) for s, n in signals}
        if unit is not None:
            self.stream.append(unit)
        self.steps.append(st)
        if name is not None:
            self.named[name] = st
        return st

    def close(self):
        self.units = len(self.stream)
        assert self.units % SLOTS == 0
        self.place = {key: i for i, key in enumerate(self.stream)}
        assert len(self.place) == self.units
        self.low = []
        for i, key in enumerate(self.stream):
            after_ffn = any(k[0] in ("gu", "d") for k in self.stream[max(0, i - 3):i])
            by = "pool" if key[0] in self.by_pool and not after_ffn else "vector"
            self.low.append((by, self.tick("low_by_" + by, 1)))
            self.tick("high_ready", 1)
            self.tick("slots_free", 1)
            self.tick(("slot", i % SLOTS), 16)
        used, split, short = 0, 0, True
        for n, st in enumerate(self.steps):
            used += st.unit is not None
            if st.unit is not None:
                short = any(x.kind in ("post", "post2") for x in self.steps[n + 1:n + 3])
            upto = min(used + AHEAD - short, self.units) if used or st.kind in ("norm", "xt") else 0
            while split < upto:
                st.split.append(split)
                split += 1
        assert split == self.units


def plan_ffn(pl, s, after=()):
    def down(j2):
        pl.step("down", ("down", s, j2), s=s, j=j2, unit=("d", s, j2))

    for j in range(FB):
        pl.step("gu", ("gu", s, j), banks=["hi"], s=s, j=j, unit=("gu", s, j),
                signals=[("gate_silu_ready", 1), ("hidden_ready", 1)])
        if j >= 2 and j % 2 == 0:
            down(j // 2 - 1)
        for kind, signals, args in after:
            if j in args["j"]:
                pl.step(kind, signals=signals, s=s, j=j, p=args["j"].index(j))
    down(FP - 1)


def weave(pl, chain, dense):
    later = []
    for n, f in enumerate(chain):
        f()
        if later:
            later.pop(0)()
        for g in dense.get(n, ()):
            rest = g()
            later += rest if isinstance(rest, list) else []
    for g in later:
        g()


def evenly(chain, dense):
    every = max(1, len(chain) // len(dense))
    at = {}
    for m, g in enumerate(dense):
        at.setdefault(min((m + 1) * every, len(chain)) - 1, []).append(g)
    return at


def plan_first():
    pl = Plan()
    acc_lo = [(b, 1, 1) for b in range(4)]
    acc_hi = [(b, 1, 1) for b in range(4, 8)]

    def norm_in(s):
        pl.step("norm", ("norm", s), s=s,
                signals=[("squares_summed", 2), ("rsqrt_ready", 2), ("normed_ready", 2)])
        pl.step("xt", ("xt", s), s=s, banks=["hi"] * 4, signals=[("activation_high_ready", 4)])

    def post(s, acc, root):
        pl.step("post", ("post", s), s=s, acc=acc, root=root, banks=[],
                signals=[("squares_summed", 2), ("rsqrt_ready", 2), ("residual_ready", 2)])

    def ffn(s):
        norm_in(s)
        if s == 2:
            pl.step("params", signals=[("params_loaded", 16)])
        pl.step("feature", signals=[("feature_rows_loaded", 16)], s=s)
        acc = pl.step("acc", ("acc", s), banks=acc_lo, s=s)
        plan_ffn(pl, s)
        post(s, acc, 2 * D ** -0.5)

    ffn(0)
    norm_in(1)
    pl.step("feature", signals=[("feature_rows_loaded", 16)], s=1)
    pl.step("small_split", signals=[("small_weights_ready", 1)])
    pl.step("lam", "lam", signals=[("lambda_dots", 1), ("lambda_exps", 1), ("lambda_ready", 1)])
    for p in range(4):
        pl.step("pb", ("pb", p), banks=["lo"], signals=[("branch_gate_ready", 1)], p=p, unit=("ba", p))
    taps = [(t, min(t + 2, 31)) for t in range(0, 31, 2)]

    def conv_b():
        if taps:
            a, b = taps.pop(0)
            pl.step("convb", ("convb", a), a=a, b=b, signals=[("conv_b_ready", 1 if b == 31 else 0)])

    for p in range(2):
        pl.step("pc", ("cq", p), banks=["lo"], what="cq", p=p, unit=("w", 10 + p))
        conv_b()
    for p in range(2):
        pl.step("pc", ("ck", p), banks=["lo"], what="ck", p=p, unit=("w", 12 + p))
        conv_b()
    for p in range(2):
        pl.step("pc", ("cv", p), banks=["lo"], what="cv", p=p, unit=("w", 14 + p))
        conv_b()
    pl.step("pf", "pf", banks=["lo"], signals=[("forget_log_ready", 1), ("log_forget_ready", 1)])
    for p in range(2):
        pl.step("pc", ("dq", p), banks=["lo"], what="dq", p=p, unit=("w", 16 + p))
        conv_b()
    pl.step("cum", "cum", banks=["s"])

    def chain_of(br, heads):
        steps = []
        per = 2 if br == "c" else 1

        def score(h):
            for m in range(per):
                e = h * per + m
                pl.step("score", ("score", br, e), banks=["s"], br=br, e=e, signals=[("probs_ready", 1)])
            if br == "c":
                pl.step("diff", ("diff", h), h=h, signals=[("probs_combined", 1)])

        def turn(h):
            pl.step("turn", ("turn", br, h), banks=["s"], br=br, h=h)

        def value(h):
            pl.step("value", ("value", br, h), br=br, h=h, signals=[("values_summed", 1)])

        for n in range(heads + 2):
            if n < heads:
                steps.append(lambda n=n: score(n))
            if 1 <= n <= heads:
                steps.append(lambda n=n: turn(n - 1))
            if n >= 2:
                steps.append(lambda n=n: value(n - 2))
        return steps

    dense = []
    for p in range(2):
        dense.append(lambda p=p: pl.step("pc", ("dk", p), banks=["lo"], what="dk", p=p, unit=("w", 18 + p)))
        dense.append(conv_b)
    for p in range(2):
        dense.append(lambda p=p: pl.step("pc", ("dv", p), banks=["lo"], what="dv", p=p, unit=("w", 20 + p)))
        dense.append(conv_b)
    for p in range(4):
        dense.append(lambda p=p: pl.step("pa", ("pa", p), banks=["lo"], signals=[("branch_gate_ready", 1)], p=p,
                                         unit=("aa", p)))
        dense.append(conv_b)
    for p in range(2):
        dense.append(lambda p=p: pl.step("conva", ("conva", p), banks=["lo"], p=p, unit=("w", p),
                                         signals=[("branch_a_ready", 1)]))
    pl.step("out_open", ("oo", "c"), banks=[(6, 0, 1), (7, 0, 1)], br="c")
    chain = chain_of("c", NH_C)
    weave(pl, chain, evenly(chain, dense))
    pl.step("out_norm", ("on", "c"), br="c", signals=[("out_squares_summed", 1), ("out_rsqrt_ready", 1)])
    gates = []
    for i in range(4):
        for k in range(KB):
            last = [("merged_ready", 1)] if i == 3 else []
            gates.append(lambda i=i, k=k, last=last: pl.step(
                "gy", ("gy", i, k), banks=["lo"], i=i, k=k, unit=("gy", i, k),
                signals=[("gate_tanh_ready", 1)] + last))
    gates[0]()
    pl.step("out_turn", ("ot", "c"), banks=["s", "s"], br="c", signals=[("activation_high_ready", 2)])
    pl.step("lnb1", "lnb1", banks=["s", "s"], signals=[("mean_var_ready", 2), ("branch_b_rsqrt_ready", 2)])
    gates[1]()
    pl.step("lnb3", "lnb3", banks=["s", "s"], signals=[("branch_b_ready", 1)])
    pl.step("out_open", ("oo", "d"), banks=[(6, 0, 1), (7, 0, 1)], br="d")
    chain = chain_of("d", NH_D)
    weave(pl, chain, evenly(chain, gates[2:24]))
    pl.step("out_norm", ("on", "d"), br="d", signals=[("out_squares_summed", 0), ("out_rsqrt_ready", 0)])
    pl.step("out_turn", ("ot", "d"), banks=["s", "s"], br="d", signals=[("activation_high_ready", 2)])
    gates[24]()
    gates[25]()
    acc = pl.step("acc", ("acc", 1), banks=acc_hi, s=1)
    for k in range(2, KB + 1, 2):
        if k < KB:
            gates[24 + k]()
            gates[24 + k + 1]()
        pl.step("wo", ("wo", k // 2 - 1), k=k // 2 - 1, unit=("wo", k // 2 - 1), src=("gy", 3, k - 1))
    post(1, acc, D ** -0.5)
    ffn(2)
    pl.close()
    return pl


def plan_second():
    pl = Plan()
    acc_lo = [(b, 1, 1) for b in range(4)]
    acc_hi = [(b, 1, 1) for b in range(4, 8)]
    def begin(s):
        pl.step("xt", ("xt", s), s=s, banks=["hi"] * 4, signals=[("activation_high_ready", 4)])
        if s == 2:
            pl.step("params", signals=[("params_loaded", 16)])
        pl.step("feature", signals=[("feature_rows_loaded", 16)], s=s)
        if s == 1:
            pl.step("small_split", signals=[("small_weights_ready", 1)])
            pl.step("factors")

    def post(s, acc):
        pl.step("post2", ("post", s), s=s, acc=acc,
                signals=[("mean_var_ready", 2), ("rsqrt_ready", 2), ("normed_ready", 2), ("residual_ready", 2)])

    def ffn(s):
        begin(s)
        acc = pl.step("acc", ("acc", s), banks=acc_lo, s=s)
        plan_ffn(pl, s, [("bias", [("bias_loaded", 16)], {"j": (3, 7, 11, 15)})] if s == 0 else [])
        post(s, acc)

    ffn(0)
    begin(1)

    def conv(hp, w):
        pl.step("pconv", ("pconv", hp, w), banks=["lo"], hp=hp, w=w, unit=("w", 6 + 4 * w + hp))
        return [lambda: pl.step("taps", ("taps", hp, w, 0), hp=hp, w=w, p=0,
                                signals=[("conv_ready", 1), ("conv_tanh_ready", 1)]),
                lambda: pl.step("taps", ("taps", hp, w, 1), hp=hp, w=w, p=1,
                                signals=[("conv_ready", 1), ("conv_tanh_ready", 1)]),
                lambda: pl.step("silu", ("silu", hp, w), hp=hp, w=w, signals=[("conv_silu_ready", 1)])]

    pl.step("pk", "pk", banks=["lo"], unit=("w", 4))
    pl.step("ps", "ps", banks=["lo"],
            signals=[("small_proj_ready", 1), ("small_logs_ready", 1), ("log_decay_ready", 1)])
    project_q = [lambda p=p: pl.step("pq", ("pq", p), banks=["lo"], p=p, unit=("w", p)) for p in range(4)]
    project_q[0]()
    project_q[1]()
    pl.step("pv", "pv", banks=["lo"], unit=("w", 5))
    pl.step("cumg", "cumg", banks=["s"],
            signals=[("decay_diff_ready", 1), ("decay_exps_ready", 1), ("decay_scalars_ready", 1)])
    project_z = [lambda p=p: pl.step("pz", ("pz", p), banks=["lo"], p=p, unit=("w", 18 + p),
                                     signals=[("z_tanh_ready", 1)]) for p in range(4)]
    dense = [project_q[2:4] + project_z[0:2], project_z[2:4] + [lambda w=w: conv(0, w) for w in range(3)]]

    def chain_of(first):
        steps = []

        def score(h):
            pl.step("score", ("score", "a", h), banks=["s"], br="a", e=h,
                    signals=[("probs_ready", 1), ("sink_exp_ready", 1)])

        def turn(h):
            pl.step("turn", ("turn", "a", h), banks=["s"], br="a", h=h)

        def value(h):
            pl.step("value", ("value", "a", h), br="a", h=h, signals=[("values_summed", 1)])

        for n in range(10):
            if n < 8:
                steps.append(lambda n=n: score(first + n))
            if 1 <= n <= 8:
                steps.append(lambda n=n: turn(first + n - 1))
            if n >= 2:
                steps.append(lambda n=n: value(first + n - 2))
        return steps

    for half in range(2):
        pl.step("out_open", ("oo", half), banks=[(6, 0, 1), (7, 0, 1)], br="a", half=half)
        chain = chain_of(8 * half)
        weave(pl, chain, evenly(chain, dense[half]))
        pl.step("out_norm", ("on", half), br="a", half=half)
        pl.step("out_turn", ("ot", half), banks=["s", "s"], br="a", half=half,
                signals=[("activation_high_ready", 2)])

    gates = []
    for i in range(2):
        for k in range(KB):
            last = [("merged_ready", 1)] if i == 1 else []
            gates.append(lambda i=i, k=k, last=last: pl.step(
                "gy", ("gy", i, k), banks=["lo"], i=i, k=k, unit=("gy", i, k),
                signals=[("gate_tanh_ready", 1)] + last))

    for hp in range(NH_B // 2):
        chain = []
        hs = (2 * hp, 2 * hp + 1)

        def both(kind, banks, signals=(), **a):
            for h in hs:
                chain.append(lambda h=h: pl.step(kind, (kind, h) + tuple(a.values()), banks=banks, h=h,
                                                 signals=signals, **a))

        both("dtr", ["hi", "hi"], [("qk_squares_summed", 1), ("qk_rsqrt_ready", 1)])
        both("dte", [], [("head_scalars_ready", 1)])
        both("ddc", ["hi"], [("decay_ready", 1), ("strict_decay_ready", 1)])
        both("dtf", ["hi", "hi"])
        both("dkk", ["hi"])
        both("dl0", ["hi"], [("level_masked", 1)])
        for s in range(1, LEVELS):
            both("dla", ["hi"], s=s)
            both("dlb", ["hi"], s=s)
        both("du1", ["hi"])
        both("du2", ["hi"])
        both("du3", ["hi"])
        both("du4", ["hi"], [("out_squares_summed", 1), ("out_rsqrt_ready", 1)])
        both("dot", ["hi"], [("delta_out_ready", 1)])
        convs = [lambda w=w, hp=hp: conv(hp + 1, w) for w in range(3)] if hp + 1 < NH_B // 2 else []
        dense = {1: gates[2 * hp:2 * hp + 1], 3: gates[2 * hp + 1:2 * hp + 2]}
        dense.update({pos: [g] for pos, g in zip((15, 23, 31), convs)})
        weave(pl, chain, dense)
    gates[8]()
    gates[9]()
    acc = pl.step("acc", ("acc", 1), banks=acc_hi, s=1)
    for k in range(2, KB + 1, 2):
        if k < KB:
            gates[8 + k]()
            gates[8 + k + 1]()
        pl.step("wo", ("wo", k // 2 - 1), k=k // 2 - 1, unit=("wo", k // 2 - 1), src=("gy", 1, k - 1))
    post(1, acc)
    ffn(2)
    pl.close()
    return pl


PLANS = {1: plan_first(), 2: plan_second()}


def bias_table():
    m = np.arange(384)
    rel = 255 - m
    n = np.maximum(rel, 0)
    nf = np.maximum(n, 1).astype(np.float32)
    large = 16 + (np.log(nf / np.float32(16)) / np.float32(math.log(8)) * np.float32(16)).astype(np.int32)
    bucket = np.where(n < 16, n, np.minimum(large, 31))
    seen = (rel >= 0) & (rel < 128)
    onehot = (bucket[None, :] == np.arange(32)[:, None]) & seen[None, :]
    return onehot.astype(np.float32), np.where(seen, 0.0, MASKED).astype(np.float32)


def constants():
    i = np.arange(P)
    j256 = np.arange(S)
    ident = np.eye(P, dtype=np.float32)
    tri = np.stack([(i[:, None] + P * t <= j256[None, :]) for t in range(T)], 1).astype(np.float32)
    dist = (P + i[:, None] - j256[None, :]).astype(np.float32)
    causal = np.where(dist >= 0, 0.0, MASKED).astype(np.float32)
    alibi = np.stack([np.where(dist >= 0, -(2.0 ** (-8.0 / NH_C * (h + 1))) / QK_SCALE * dist, MASKED)
                      for h in range(NH_C)], 1).astype(np.float32)
    maskt = np.where(i[None, :] >= i[:, None], 0.0, MASKED).astype(np.float32)
    strict = (i[None, :] > i[:, None]).astype(np.float32)
    level = []
    for s in range(LEVELS):
        same = (i[None, :] >> (s + 1)) == (i[:, None] >> (s + 1))
        level.append(same & (((i[None, :] >> s) & 1) == 1) & (((i[:, None] >> s) & 1) == 0))
    masks = np.stack([m.T if o == 0 else m for m in level[1:] for o in range(2)], 1).astype(np.uint8)
    masks = np.ascontiguousarray(masks.reshape(P, -1)).view(np.float32)
    level = level[0].astype(np.float32)
    c1 = np.concatenate([a.reshape(P, -1) for a in (ident, tri, causal, alibi)], 1)
    c2 = np.concatenate([a.reshape(P, -1) for a in (ident, tri[:, 0, :P], np.ones((P, P), np.float32),
                                                    maskt, strict, level, masks)], 1)
    con = np.zeros((2, P, NCON), np.float32)
    con[0, :, :NCON1], con[1, :, :NCON2] = c1, c2
    return con


def build_kernel(nc, x, stream1, stream2, prms, feat1, feat2, con, onehot, rowmask, relb, toep, out):
    with ExitStack() as ctx:
        def sb(name, shape):
            return ctx.enter_context(nc.sbuf_tensor(name, shape, F32))

        def sb_twice(name, parts, shape):
            with nc.sbuf_tensor(name, shape, F32) as whole:
                pass
            return whole, ctx.enter_context(nc.sbuf_tensor(parts, shape, F32R))

        def sem(name):
            return ctx.enter_context(nc.semaphore(name))

        H = sb("residual", [P, T, D])
        XTH = ctx.enter_context(nc.sbuf_tensor("normed_t_high", [P, KB, S], F32R))
        XTL = ctx.enter_context(nc.sbuf_tensor("normed_t_low", [P, KB, S], F32R))
        XT = (XTH, XTL)
        RING, LOW = sb_twice("weight_ring", "weights_low", [P, SLOTS, UNIT])
        HIGH = ctx.enter_context(nc.sbuf_tensor("weights_high", [P, SLOTS, UNIT], F32R))
        PG = sb("feature_rows", [P, 2, D])
        PRM = sb("params", [P, max(NCOL1, NCOL2)])
        CON = sb("constants", [P, NCON])
        PS = ctx.enter_context(nc.psum_tensor("psum", [P, 8, HALF], F32))
        SMALL = sb("small", [P, 524])
        ARENA = 25600
        W, WP = sb_twice("work", "work_parts", [P, ARENA])

        def small(a, *dims):
            n = int(np.prod(dims))
            v = SMALL[:, a:a + n]
            return v if len(dims) == 1 else v.rearrange("p (a b) -> p a b", a=dims[0])

        SS, RS = small(0, 4), small(4, 4)
        MX, NM = small(8, 4, 2), small(16, 4, 2)
        LS = small(24, 16, 2)
        RL = small(56, 16, 2)
        RC = small(88, 4)
        SSO, RSO = small(92, 16), small(108, 16)
        MV = small(124, 2, 2)
        RSB = small(128, 2)
        LAM, ELAM = small(130, 2), small(132, 2)
        NLAM, SUBG = small(134, 1), small(135, 1)
        ZF, ZA_, ZL, LF = (small(136 + 16 * n, 2, 8) for n in range(4))
        ES = small(200, 16, 2)
        HALFNEG = small(232, 16)
        ST = small(248, 4, 6)
        GDH = small(272, 1)
        SINK8 = small(273, 16)
        SBT = small(289, 2, 16)
        BETA, HB, GG = small(321, 2, 8), small(337, 2, 8), small(353, 2, 8)
        G, GL = small(369, 2, 8), small(385, 2, 8)
        EG, ET, BEG = small(401, 2, 8), small(417, 2, 8), small(433, 2, 8)
        EAL = small(449, 8)
        SSD, RD = small(457, 2, 4), small(465, 2, 4)
        SC = small(473, 2, 12)
        EPS_AT = {EPS: 0, 4 * EPS: 1, RES_EPS: 2}
        EPSES = small(498, 3, 8)
        TOUCH = small(522, 2)

        pos = [0]

        def arena(*dims, at=None):
            if at is not None:
                pos[0] = at
            n = int(np.prod(dims))
            v = W[:, pos[0]:pos[0] + n]
            pos[0] += n
            assert pos[0] <= ARENA, pos[0]
            if len(dims) == 2:
                v = v.rearrange("p (a b) -> p a b", a=dims[0])
            if len(dims) == 3:
                v = v.rearrange("p (a b c) -> p a b c", a=dims[0], b=dims[1])
            return v

        def parts(at, blocks):
            return WP[:, at:at + blocks * S].rearrange("p (a b) -> p a b", b=S)

        MG = arena(KB, S)
        XN = W[:, 0:T * D].rearrange("p (t d) -> p t d", t=T)
        EX = arena(4, 384)
        SG, HF = (W[:, at:at + 2 * S].rearrange("p (a b) -> p a b", b=S) for at in (T * D, T * D + 2 * S))
        DG = W[:, T * D:T * D + S].rearrange("p (t n) -> p t n", t=T)
        XTF = W[:, T * D:T * D + 4 * S].rearrange("p (a b) -> p a b", b=2 * S)
        HTH, HTL = parts(T * D + 4 * S, 4), parts(T * D + 8 * S, 4)
        NARROW = parts(T * D + 4 * S, 1)[:, 0, :].rearrange("p (a b) -> p a b", a=2)
        PT = arena(3, 384)
        ON = arena(T, 512)
        TH = arena(2, 512)
        TMP = arena(2, S)
        common = pos[0]
        CQ, CK, CV = arena(4, S), arena(4, 2, S), arena(T, 512)
        merged_at = pos[0] - T * 512
        DQ, DK, DV = arena(4, S), arena(4, 2, S), arena(T, 512)
        dv_at = pos[0] - T * 512
        zb_at = pos[0]
        ZB, ACCB, ZA, ACCA = arena(4, S), arena(4, S), arena(4, S), arena(4, S)
        YB1, YC, YD = arena(4, S), arena(4, S), arena(4, S)
        NC = arena(S)
        JUNK = arena(P)
        BWH = arena(31, 4)
        ROWS = arena(4, 384)
        za_at, acca_at, yb1_at, yc_at, yd_at = (zb_at + n * 4 * S for n in range(2, 7))
        Y1 = [tuple(parts(at, 4) for at in pair) for pair in
              ((za_at, acca_at), (zb_at, yb1_at), (common, yc_at), (dv_at, yd_at))]
        MGH1 = parts(merged_at, KB)
        MGL = parts(0, KB)
        BN = ACCB.rearrange("p a b -> p (a b)").rearrange("p (t n) -> p t n", t=T)
        YAH, YAL = parts(common, KB), parts(common + KB * S, KB)
        ZS = arena(KB, S, at=common + 2 * KB * S)
        YBH, YBL = parts(pos[0] - KB * S, KB), parts(pos[0], KB)
        CO = arena(6, S, at=pos[0] + KB * S)
        GTR = arena(S)
        TC = arena(2 * S)
        phase = pos[0]
        BIAS = arena(NH_A, S)
        QA, KA, VA = arena(KB, S), arena(4, S), arena(T, S)
        TM = arena(2, 11, P, at=phase)
        AL = arena(2, 4, P)
        TT = arena(2, 4, P)
        MT, DD = arena(2, 2, P), arena(2, 2, P)
        VW, VS, OD = arena(2, 2, P), arena(2, 2, P), DD
        MGH2 = parts(phase, KB)
        arena(0, at=2 * D)
        FA, FBM, DEC, P1S = arena(2, 4, P), arena(2, 3, P), arena(2, 4, P), arena(2, 2, P)
        assert pos[0] <= common - 3 * HALF

        def prm(name, blk, *dims):
            a, b = (COL1 if blk == 1 else COL2)[name]
            v = PRM[:, a:b]
            return v if not dims else v.rearrange("p (a b) -> p a b", a=dims[0])

        def cst(name, blk, *dims):
            a, b = (CON1 if blk == 1 else CON2)[name]
            v = CON[:, a:b]
            return v if not dims else v.rearrange("p (a b) -> p a b", a=dims[0])

        IDENT = CON[:, 0:P]

        bank_full = [sem(f"bank{b}_full") for b in range(8)]
        bank_taken = [sem(f"bank{b}_taken") for b in range(8)]
        slot_loaded = [sem(f"slot{s}_loaded") for s in range(SLOTS)]
        slots_free = sem("slots_free")
        x_loaded, con_loaded, out_stored = sem("x_loaded"), sem("constants_loaded"), sem("out_stored")
        prologue_done, toeplitz_stored, bias_loaded = sem("prologue_done"), sem("toeplitz_stored"), sem("bias_loaded")
        con2_loaded = sem("second_constants_loaded")
        ident_loaded, table_loaded = sem("identity_loaded"), sem("bias_table_loaded")
        prologue_row, zeros_set = sem("prologue_row"), sem("zeros_set")
        gate_silu_ready = sem("gate_silu_ready")
        hidden_ready = sem("hidden_ready")
        merged_ready = sem("merged_ready")
        small_weights_ready = sem("small_weights_ready")
        high_ready = sem("weights_high_ready")
        low_by_vector, low_by_pool = sem("weights_low_by_vector"), sem("weights_low_by_pool")
        activation_high_ready = sem("activation_high_ready")
        branch_b_ready = sem("branch_b_ready")
        delta_out_ready = sem("delta_out_ready")
        branch_gate_ready = sem("branch_gate_ready")
        squares_summed = sem("squares_summed")
        rsqrt_ready = sem("rsqrt_ready")
        normed_ready = sem("normed_ready")
        residual_ready = sem("residual_ready")
        params_loaded = sem("params_loaded")
        feature_rows_loaded = sem("feature_rows_loaded")
        lambda_dots = sem("lambda_dots")
        lambda_exps = sem("lambda_exps")
        lambda_ready = sem("lambda_ready")
        conv_b_ready = sem("conv_b_ready")
        forget_log_ready = sem("forget_log_ready")
        log_forget_ready = sem("log_forget_ready")
        probs_ready = sem("probs_ready")
        probs_combined = sem("probs_combined")
        values_summed = sem("values_summed")
        branch_a_ready = sem("branch_a_ready")
        out_squares_summed = sem("out_squares_summed")
        out_rsqrt_ready = sem("out_rsqrt_ready")
        gate_tanh_ready = sem("gate_tanh_ready")
        mean_var_ready = sem("mean_var_ready")
        branch_b_rsqrt_ready = sem("branch_b_rsqrt_ready")
        sink_exp_ready = sem("sink_exp_ready")
        small_proj_ready = sem("small_proj_ready")
        small_logs_ready = sem("small_logs_ready")
        log_decay_ready = sem("log_decay_ready")
        decay_diff_ready = sem("decay_diff_ready")
        decay_exps_ready = sem("decay_exps_ready")
        decay_scalars_ready = sem("decay_scalars_ready")
        z_tanh_ready = sem("z_tanh_ready")
        conv_ready = sem("conv_ready")
        conv_tanh_ready = sem("conv_tanh_ready")
        conv_silu_ready = sem("conv_silu_ready")
        qk_squares_summed = sem("qk_squares_summed")
        qk_rsqrt_ready = sem("qk_rsqrt_ready")
        head_scalars_ready = sem("head_scalars_ready")
        decay_ready = sem("decay_ready")
        strict_decay_ready = sem("strict_decay_ready")
        level_masked = sem("level_masked")
        CREDIT = {"residual_ready": 2, "params_loaded": 16, **{("taken", b): 1 for b in range(8)}}
        BETWEEN = {"normed_ready": T}
        now = Now()

        def reach(key, k):
            per = [PLANS[b].count.get(key, 0) for b in (1, 2)]
            base = CREDIT.get(key, 0) + (L * per[0] + BETWEEN.get(key, 0) if now.blk == 2 else 0) + k
            return now.l * per[now.blk - 1] + base

        def full_at(job):
            return reach(("full", job.bank), job.full)

        def taken_at(job):
            return reach(("taken", job.bank), job.taken)

        def turn_at(job):
            return reach(("taken", job.bank), job.turn)

        def loaded_at(i):
            return reach(("slot", i % SLOTS), 16 * (i // SLOTS + 1))

        def low_sem(i):
            return low_by_pool if PLANS[now.blk].low[i][0] == "pool" else low_by_vector

        def low_at(i):
            by, n = PLANS[now.blk].low[i]
            return reach("low_by_" + by, n)

        def width(i):
            return 12 * P if now.blk == 1 and PLANS[1].stream[i][0] == "gy" else UNIT

        def named(key):
            return PLANS[now.blk].named[key]

        def walk(eng, kinds, blk, split=None):
            now.blk = blk
            with eng.Fori(0, L) as l:
                now.l = l
                for st in PLANS[blk].steps:
                    if split is not None:
                        for i in st.split:
                            split(i)
                    if st.kind in kinds:
                        kinds[st.kind](st)

        block = ctx.enter_context(nc.Block())

        @block.sync
        def _(sp):
            sp.dma_start(IDENT, con[0, :, 0:P]).then_inc(ident_loaded, 16)
            sp.dma_start(H[:], x.rearrange("o (t p) d -> p (o t) d", p=P)).then_inc(x_loaded, 16)
            for blk, src in ((1, stream1), (2, stream2)):
                pl = PLANS[blk]
                now.blk = blk
                with sp.Fori(0, L) as l:
                    now.l = l
                    for i in range(pl.units):
                        n = width(i)
                        sp.wait_ge(slots_free, reach("slots_free", i + 1))
                        sp.dma_start(RING[:, i % SLOTS, 0:n], src[bass.ds(l, 1), i, :, 0:n]
                                     .rearrange("a p n -> (a p) n")).then_inc(slot_loaded[i % SLOTS], 16)
            now.blk, now.l = 2, L - 1
            sp.wait_ge(residual_ready, reach("residual_ready", 6))
            sp.dma_start(out.rearrange("o (t p) d -> p (o t) d", p=P), H[:]).then_inc(out_stored, 16)
            sp.wait_ge(out_stored, 16)

        @block.gpsimd
        def _(pool):
            def rsqrt(dst, src, eps, signal):
                n = dst.shape[1]
                pool.tensor_tensor(dst, src, EPSES[:, EPS_AT[eps], 0:n], ALU.add)
                pool.drain()
                pool.tensor_tensor(dst, dst, HALFNEG[:, 0:dst.shape[1]], ALU.pow).then_inc(signal, 1)

            def params(st):
                for ready in named(("xt", 2)).jobs:
                    pool.wait_ge(bank_taken[ready.bank], taken_at(ready))
                pool.dma_start(PRM[:, :], prms[bass.ds(now.l + (1 if now.blk == 1 else L + 1), 1)]
                               .rearrange("a p n -> (a p) n")).then_inc(params_loaded, 16)

            def feature(st):
                pool.wait_ge(residual_ready, reach("residual_ready", 2 * st.s))
                if now.blk == 1:
                    row = feat1[bass.ds(now.l, 1), st.s:st.s + 1, :].rearrange("a b n -> (a b) n")
                    pool.dma_start(PG[:, 0, :], row.to_broadcast([P, D])).then_inc(feature_rows_loaded, 16)
                else:
                    row = feat2[bass.ds(now.l, 1), st.s].rearrange("a c n -> a (c n)")
                    pool.dma_start(PG[:].rearrange("p c n -> p (c n)"), row.to_broadcast([P, 2 * D])
                                   ).then_inc(feature_rows_loaded, 16)

            def bias(st):
                pool.wait_ge(hidden_ready, reach("hidden_ready", named(("gu", st.s, st.j)).at["hidden_ready"]))
                pool.tensor_tensor(TOUCH[:, 1:2], HALFNEG[:, 0:1], HALFNEG[:, 0:1], ALU.add)
                pool.drain()
                pool.wait_ge(toeplitz_stored, 16)
                heads = NH_A // 4
                pool.dma_start(BIAS[:, st.p * heads:(st.p + 1) * heads, :],
                               bass.AP(toep.tensor, P - 1 + st.p * heads * P * 384,
                                       [[383, P], [P * 384, heads], [1, S]])
                               ).then_inc(bias_loaded, 16)

            def split_low(i):
                if low_sem(i) is low_by_pool:
                    pool.wait_ge(high_ready, reach("high_ready", i + 1))
                    raw, high = RING[:, i % SLOTS, 0:width(i)], HIGH[:, i % SLOTS, 0:width(i)]
                    pool.tensor_tensor(LOW[:, i % SLOTS, 0:width(i)], raw, high.bitcast(F32), ALU.subtract
                                       ).then_inc(low_by_pool, 1)

            def norm(st):
                for t in range(T):
                    pool.wait_ge(squares_summed, reach("squares_summed", st.at["squares_summed"] - 1 + t))
                    rsqrt(RS[:, t:t + 1], SS[:, t:t + 1], EPS, rsqrt_ready)

            def post(st):
                for t in range(T):
                    pool.wait_ge(squares_summed, reach("squares_summed", st.at["squares_summed"] - 1 + t))
                    rsqrt(RS[:, 2 + t:3 + t], SS[:, 2 + t:3 + t], 4 * EPS, rsqrt_ready)

            def post2(st):
                for t in range(T):
                    pool.wait_ge(mean_var_ready, reach("mean_var_ready", st.at["mean_var_ready"] - 1 + t))
                    rsqrt(RS[:, 2 + t:3 + t], MV[:, t, 1:2], RES_EPS, rsqrt_ready)
                pool.wait_ge(feature_rows_loaded, reach("feature_rows_loaded", 16 * (st.s + 1)))
                for t in range(T):
                    pool.wait_ge(normed_ready, reach("normed_ready", st.at["normed_ready"] - 1 + t))
                    pool.tensor_tensor(H[:, t, :], XN[:, t, :], PG[:, 0, :], ALU.mult)
                    pool.drain()
                    pool.tensor_tensor(H[:, t, :], H[:, t, :], PG[:, 1, :], ALU.add).then_inc(residual_ready, 1)

            def lnb1(st):
                for t in range(T):
                    pool.wait_ge(mean_var_ready, reach("mean_var_ready", st.at["mean_var_ready"] - 1 + t))
                    rsqrt(RSB[:, t:t + 1], MV[:, t, 1:2], EPS, branch_b_rsqrt_ready)

            def out_norm(st):
                if st.br == "c":
                    pool.wait_ge(out_squares_summed, reach("out_squares_summed", st.at["out_squares_summed"]))
                    rsqrt(RSO[:, 0:8], SSO[:, 0:8], EPS, out_rsqrt_ready)

            def dtr(st):
                i = st.h % 2
                pool.wait_ge(qk_squares_summed, reach("qk_squares_summed", st.at["qk_squares_summed"]))
                if st.h >= 2:
                    pool.wait_ge(head_scalars_ready,
                                 reach("head_scalars_ready", named(("dte", st.h - 2)).at["head_scalars_ready"]))
                rsqrt(RD[:, i, :], SSD[:, i, :], 4 * EPS, qk_rsqrt_ready)

            def ddc(st):
                i = st.h % 2
                dec = DEC[:, i].rearrange("p (t k) n -> p t k n", t=T)
                pool.wait_ge(decay_ready, reach("decay_ready", st.at["decay_ready"]))
                for t in range(T):
                    last = pool.tensor_tensor(dec[:, t, 0, :], dec[:, t, 1, :], cst("strict", 2), ALU.mult)
                last.then_inc(strict_decay_ready, 1)

            def du4(st):
                i = st.h % 2
                pool.wait_ge(out_squares_summed, reach("out_squares_summed", st.at["out_squares_summed"]))
                rsqrt(RSO[:, 2 * i:2 * i + 2], SSO[:, 2 * i:2 * i + 2], EPS, out_rsqrt_ready)

            pool.memset(HALFNEG[:, :], -0.5)
            for eps, at in EPS_AT.items():
                pool.drain()
                pool.memset(EPSES[:, at, :], eps)
            pool.drain()
            pool.memset(CK[64:128, :, 0, :], 0.0)
            pool.drain()
            pool.memset(CK[0:64, :, 1, :], 0.0)
            pool.drain()
            pool.memset(DK[64:128, :, 0, :], 0.0)
            pool.drain()
            pool.memset(DK[0:64, :, 1, :], 0.0)
            pool.drain()
            pool.memset(NC[:, :], 0.0).then_inc(zeros_set, 1)
            pool.drain()
            pool.dma_start(PRM[:, :], prms[0]).then_inc(params_loaded, 16)
            kinds = {"params": params, "feature": feature, "norm": norm, "post": post, "lnb1": lnb1,
                     "out_norm": out_norm}
            walk(pool, kinds, 1, split_low)
            now.blk, now.l = 2, 0
            pool.wait_ge(residual_ready, reach("residual_ready", 0))
            pool.memset(GTR[:, :], 0.0).then_inc(zeros_set, 1)
            pool.drain()
            pool.dma_start(CON[:, P:NCON2], con[1, :, P:NCON2]).then_inc(con2_loaded, 16)
            pool.wait_ge(prologue_done, 1)
            pool.dma_start(toep, ROWS[0:NH_A, 3:4, :].to_broadcast([NH_A, P, 384])).then_inc(toeplitz_stored, 16)
            walk(pool, {"params": params, "feature": feature, "post2": post2, "dtr": dtr, "ddc": ddc,
                        "du4": du4,
                        "bias": bias}, 2, split_low)

        @block.tensor
        def _(pe):
            owed = [0]

            def mm(dst, lhsT, rhs, start=True, stop=True):
                return pe.matmul(dst, lhsT, rhs, start=start, stop=stop, skip_group_check=True)

            def transpose(dst, src):
                return pe.transpose(dst, src, IDENT)

            def pay(ins):
                if owed[0]:
                    ins.then_inc(slots_free, owed[0])
                    owed[0] = 0
                return ins

            def flush():
                if owed[0]:
                    pe.drain().then_inc(slots_free, owed[0])
                    owed[0] = 0

            def weights(st, a):
                i = PLANS[now.blk].place[st.unit]
                pe.wait_ge(low_sem(i), low_at(i))
                n = width(i)
                return [v.rearrange("p (a b) -> p a b", a=a)
                        for v in (HIGH[:, i % SLOTS, 0:n], LOW[:, i % SLOTS, 0:n])]

            PARTS = ((0, 0), (0, 1), (1, 0))

            def cols_product(bank, at, w, c, src, n, first=0, fresh=None):
                for k in range(n):
                    if fresh is not None and k % 2 == 0:
                        ready = named(("xt", fresh)).jobs[k // 2]
                        pe.wait_ge(bank_taken[ready.bank], taken_at(ready))
                    for m, (a, b) in enumerate(PARTS):
                        ins = mm(PS[:, bank, at:at + S], w[a][:, first + k, c * P:(c + 1) * P], src[b][:, k, :],
                                 (k, m) == (0, 0), (k, m) == (n - 1, 2))
                        if (k, m) == (0, 0):
                            pay(ins)
                return ins

            def xt(st):
                flush()
                n = named(("norm", st.s)).at["normed_ready"] if now.blk == 1 else 2 * st.s
                for t in range(T):
                    pe.wait_ge(normed_ready, reach("normed_ready", n - 1 + t))
                    for k in range(KB):
                        job = st.jobs[k // 2]
                        if t == 0 and k % 2 == 0:
                            pe.wait_ge(bank_taken[job.bank], turn_at(job))
                        dst = PS[:, job.bank, (k % 2 * T + t) * P:(k % 2 * T + t + 1) * P]
                        if now.blk == 1:
                            ins = mm(dst, H[:, t, k * P:(k + 1) * P], DG[:, t, :])
                        else:
                            ins = transpose(dst, XN[:, t, k * P:(k + 1) * P])
                        if t == T - 1 and k % 2:
                            ins.then_inc(bank_full[job.bank], 1)

            def acc(st):
                for job in st.jobs:
                    pe.wait_ge(bank_taken[job.bank], turn_at(job))

            def gu(st):
                job = st.jobs[0]
                w = weights(st, KB)
                pe.wait_ge(bank_taken[job.bank], turn_at(job))
                cols_product(job.bank, 0, w, 0, XT, KB, fresh=st.s if st.j == 0 else None)
                cols_product(job.bank, S, w, 1, XT, KB).then_inc(bank_full[job.bank], 1)
                owed[0] += 1

            def down(st):
                w = weights(st, 2)
                src = [h[:, 2 * st.j % 4:2 * st.j % 4 + 2, :] for h in (HTH, HTL)]
                for r in range(2):
                    pe.wait_ge(hidden_ready,
                               reach("hidden_ready", named(("gu", st.s, 2 * st.j + r)).at["hidden_ready"]))
                    rows_product(r, w, src, named(("acc", st.s)).jobs, st.j == 0 and r == 0, st.j == FP - 1 and r == 1)
                owed[0] += 1
                if st.j == FP - 1:
                    flush()

            def rows_product(r, w, src, jobs, start, stop):
                for t in range(T):
                    for n in range(2):
                        b = jobs[2 * t + n].bank
                        for m, (a, c) in enumerate(PARTS):
                            ins = mm(PS[:, b, :], src[c][:, r, t * P:(t + 1) * P],
                                     w[a][:, r, n * HALF:(n + 1) * HALF], start and m == 0, stop and m == 2)
                            if (t, n, m) == (0, 0, 0):
                                pay(ins)
                        if stop:
                            ins.then_inc(bank_full[b], 1)

            def pb(st):
                job = st.jobs[0]
                w = weights(st, KB)
                pe.wait_ge(bank_taken[job.bank], turn_at(job))
                cols_product(job.bank, 0, w, 0, XT, KB, fresh=1 if st.p == 0 and st.kind == "pb" else None)
                cols_product(job.bank, S, w, 1, XT, KB).then_inc(bank_full[job.bank], 1)
                owed[0] += 1

            def project(st, tokens=False, fresh=None):
                job = st.jobs[0]
                w = weights(st, KB)
                pe.wait_ge(bank_taken[job.bank], turn_at(job))
                b = job.bank
                if tokens:
                    for t in range(T):
                        for k in range(KB):
                            for m, (i, j) in enumerate(PARTS):
                                ins = mm(PS[:, b, t * S:(t + 1) * S], XT[j][:, k, t * P:(t + 1) * P], w[i][:, k, :],
                                         (k, m) == (0, 0), (k, m) == (KB - 1, 2))
                                if (t, k, m) == (0, 0, 0):
                                    pay(ins)
                    ins.then_inc(bank_full[b], 1)
                else:
                    cols_product(b, 0, w, 0, XT, KB, fresh=fresh)
                    cols_product(b, S, w, 1, XT, KB).then_inc(bank_full[b], 1)
                owed[0] += 1

            def pc(st):
                project(st, st.what[1] == "v")

            def small_project(st, n):
                flush()
                job = st.jobs[0]
                w = [NARROW[:, part, 0:KB * n].rearrange("p (a b) -> p a b", a=KB) for part in range(2)]
                pe.wait_ge(small_weights_ready, reach("small_weights_ready", 1))
                pe.wait_ge(bank_taken[job.bank], turn_at(job))
                for t in range(T):
                    for k in range(KB):
                        for m, (a, b) in enumerate(PARTS):
                            ins = mm(PS[:, job.bank, t * n:(t + 1) * n], XT[b][:, k, t * P:(t + 1) * P],
                                     w[a][:, k, :], (k, m) == (0, 0), (k, m) == (KB - 1, 2))
                ins.then_inc(bank_full[job.bank], 1)

            def pf(st):
                small_project(st, 8)

            def cum(st):
                job = st.jobs[0]
                pe.wait_ge(con_loaded, 16)
                pe.wait_ge(log_forget_ready, reach("log_forget_ready", 1))
                pe.wait_ge(bank_taken[job.bank], turn_at(job))
                for t in range(T):
                    ins = mm(PS[0:8, job.bank, 0:S], LF[:, t, :], cst("tri", 1, T)[:, t, :], t == 0, t == T - 1)
                    if t == T - 1:
                        ins.then_inc(bank_full[job.bank], 1)

            def score(st):
                job, e = st.jobs[0], st.e
                b = job.bank
                if st.br == "c":
                    h = e // 2
                    q, k = CQ[:, h, :], CK[:, h, e % 2, :]
                    if e % 4 == 0:
                        ready = named(("cq", h // 2)).jobs[0]
                        pe.wait_ge(bank_taken[ready.bank], taken_at(ready))
                        ready = named(("ck", h // 2)).jobs[0]
                        pe.wait_ge(bank_taken[ready.bank], taken_at(ready))
                elif st.br == "d":
                    q, k = DQ[:, e // 2, :], DK[:, e // 2, e % 2, :]
                    if e % 4 == 0:
                        ready = named(("dq", e // 4)).jobs[0]
                        pe.wait_ge(bank_taken[ready.bank], taken_at(ready))
                        ready = named(("dk", e // 4)).jobs[0]
                        pe.wait_ge(bank_taken[ready.bank], taken_at(ready))
                    if e == 0:
                        ready = named("cum").jobs[0]
                        pe.wait_ge(bank_taken[ready.bank], taken_at(ready))
                else:
                    g = e // 4
                    blk_ = (g // 2) * 4 + e % 4
                    rows = slice(64 * (g % 2), 64 * (g % 2) + 64)
                    q, k = QA[rows, blk_, :], KA[rows, g, :]
                    if e % 2 == 0:
                        ready = named(("pq", blk_ // 2)).jobs[0]
                        pe.wait_ge(bank_taken[ready.bank], taken_at(ready))
                    if e == 0:
                        ready = named("pk").jobs[0]
                        pe.wait_ge(bank_taken[ready.bank], taken_at(ready))
                pe.wait_ge(bank_taken[job.bank], turn_at(job))
                for t in range(T):
                    dst = PS[:, b, 0:P] if t == 0 else PS[:, b, P:P + S]
                    keys = (t + 1) * P
                    extra = st.br == "d"
                    ins = mm(dst, q[:, t * P:(t + 1) * P], k[:, 0:keys], True, not extra)
                    if extra:
                        ins = mm(dst, IDENT[:, e:e + 1].to_broadcast([P, P]), NC[:, 0:keys], False, True)
                ins.then_inc(bank_full[b], 1)

            def turn_(st):
                job = st.jobs[0]
                b = job.bank
                e = 2 * st.h if st.br == "c" else st.h
                if st.br == "c":
                    pe.wait_ge(probs_combined, reach("probs_combined", named(("diff", st.h)).at["probs_combined"]))
                else:
                    pe.wait_ge(probs_ready, reach("probs_ready", named(("score", st.br, e)).at["probs_ready"]))
                pe.wait_ge(bank_taken[job.bank], turn_at(job))
                for n in range(3):
                    ins = transpose(PS[:, b, n * P:(n + 1) * P], EX[:, e % 4, n * P:(n + 1) * P])
                    if n == 2:
                        ins.then_inc(bank_full[b], 1)

            def out_open(st):
                for job in st.jobs:
                    pe.wait_ge(bank_taken[job.bank], turn_at(job))

            def value(st):
                h = st.h
                ready = named(("turn", st.br, h)).jobs[0]
                pe.wait_ge(bank_taken[ready.bank], taken_at(ready))
                pt = PT[:, st.at["values_summed"] % 3, :]
                if st.br == "c":
                    v, c, w = [CV[:, t, h * P:(h + 1) * P] for t in range(T)], h * P, P
                    if h % 2 == 0:
                        ready = named(("cv", h // 2)).jobs[0]
                        pe.wait_ge(bank_taken[ready.bank], taken_at(ready))
                elif st.br == "d":
                    v, c, w = [DV[:, t, h * 64:(h + 1) * 64] for t in range(T)], h * 64, 64
                    if h % 4 == 0:
                        ready = named(("dv", h // 4)).jobs[0]
                        pe.wait_ge(bank_taken[ready.bank], taken_at(ready))
                else:
                    g = h // 4
                    v, c, w = [VA[:, t, g * 64:(g + 1) * 64] for t in range(T)], (h % 8) * 64, 64
                    if h == 0:
                        ready = named("pv").jobs[0]
                        pe.wait_ge(bank_taken[ready.bank], taken_at(ready))
                mm(PS[:, 6, c:c + w], pt[:, 0:P], v[0])
                mm(PS[:, 7, c:c + w], pt[:, P:2 * P], v[0], True, False)
                mm(PS[:, 7, c:c + w], pt[:, 2 * P:3 * P], v[1], False, True).then_inc(values_summed, 1)

            def out_turn(st):
                for job in named(("oo", st.half if st.br == "a" else st.br)).jobs:
                    pe.wait_ge(bank_taken[job.bank], taken_at(job))
                for p, job in enumerate(st.jobs):
                    pe.wait_ge(bank_taken[job.bank], turn_at(job))
                    for n in range(4):
                        c, t = 2 * p + n // 2, n % 2
                        ins = transpose(PS[:, job.bank, n * P:(n + 1) * P], ON[:, t, c * P:(c + 1) * P])
                        if n == 3:
                            ins.then_inc(bank_full[job.bank], 1)

            def lnb1(st):
                pe.wait_ge(conv_b_ready, reach("conv_b_ready", 1))
                for t, job in enumerate(st.jobs):
                    pe.wait_ge(bank_taken[job.bank], turn_at(job))
                    for c in range(4):
                        ins = transpose(PS[:, job.bank, c * P:(c + 1) * P], ACCB[:, c, t * P:(t + 1) * P])
                        if c == 3:
                            ins.then_inc(bank_full[job.bank], 1)

            def lnb3(st):
                assert [job.bank for job in st.jobs] == [job.bank for job in named("lnb1").jobs]
                for job in st.jobs:
                    pe.wait_ge(bank_taken[job.bank], turn_at(job))
                for p, job in enumerate(st.jobs):
                    for n in range(4):
                        c, t = 2 * p + n // 2, n % 2
                        ins = transpose(PS[:, job.bank, n * P:(n + 1) * P], BN[:, t, c * P:(c + 1) * P])
                        if n == 3:
                            ins.then_inc(bank_full[job.bank], 1)

            def gy(st):
                job, i, k = st.jobs[0], st.i, st.k
                w = weights(st, 12 if now.blk == 1 else KB)
                pe.wait_ge(bank_taken[job.bank], turn_at(job))
                cols_product(job.bank, 0, w, 0, XT, KB)
                if k == 0:
                    if now.blk == 1 and i == 0:
                        pe.wait_ge(branch_a_ready, reach("branch_a_ready", 2))
                    elif now.blk == 1 and i == 1:
                        pe.wait_ge(branch_b_ready, reach("branch_b_ready", 1))
                    elif now.blk == 2 and i == 1:
                        pe.wait_ge(delta_out_ready, reach("delta_out_ready", NH_B))
                    else:
                        for j2 in named({2: ("ot", "c"), 3: ("ot", "d"), 0: ("ot", 1)}[i]).jobs:
                            pe.wait_ge(bank_taken[j2.bank], taken_at(j2))
                if now.blk == 1:
                    cols_product(job.bank, S, w, 0, Y1[i], 4, KB).then_inc(bank_full[job.bank], 1)
                else:
                    y = ((YAH, YAL), (YBH, YBL))[i]
                    cols_product(job.bank, S, w, 1, y, KB).then_inc(bank_full[job.bank], 1)
                owed[0] += 1

            def wo(st):
                w = weights(st, 2)
                src = [v[:, 2 * st.k:2 * st.k + 2, :] for v in (MGH1 if now.blk == 1 else MGH2, MGL)]
                for r in range(2):
                    n = named((st.src[0], st.src[1], 2 * st.k + r)).at["merged_ready"]
                    pe.wait_ge(merged_ready, reach("merged_ready", n))
                    rows_product(r, w, src, named(("acc", 1)).jobs, st.k == 0 and r == 0,
                                 st.k == KB // 2 - 1 and r == 1)
                owed[0] += 1
                if st.k == KB // 2 - 1:
                    flush()

            def ps(st):
                small_project(st, 16)

            def cumg(st):
                job = st.jobs[0]
                b = job.bank
                pe.wait_ge(con2_loaded, 16)
                pe.wait_ge(zeros_set, 2)
                pe.wait_ge(log_decay_ready, reach("log_decay_ready", 1))
                pe.wait_ge(bank_taken[job.bank], turn_at(job))
                tri = cst("tri", 2)
                gg = GG.rearrange("p a b -> p (a b)")
                mm(PS[:, b, 0:16], tri, gg)
                mm(PS[:, b, 16:32], cst("ones", 2), gg)
                for t in range(T):
                    ins = mm(PS[0:8, b, 64 + t * P:64 + (t + 1) * P], GG[:, t, :], tri)
                    if t == T - 1:
                        ins.then_inc(bank_full[b], 1)

            def dtr(st):
                h, i, j1, j2 = st.h, st.h % 2, st.jobs[0], st.jobs[1]
                hp, c = h // 2, h % 2
                pe.wait_ge(conv_silu_ready, reach("conv_silu_ready", named(("silu", hp, 2)).at["conv_silu_ready"]))
                pe.wait_ge(bank_taken[j1.bank], turn_at(j1))
                pe.wait_ge(bank_taken[j2.bank], turn_at(j2))
                for w, job, at in ((0, j1, 0), (2, j1, 2), (1, j2, 0)):
                    for t in range(T):
                        ins = transpose(PS[:, job.bank, (at + t) * P:(at + t + 1) * P],
                                        CO[:, 2 * w + c, t * P:(t + 1) * P])
                        if t == 1 and w > 0:
                            ins.then_inc(bank_full[job.bank], 1)

            def dtf(st):
                h, i = st.h, st.h % 2
                tr = named(("dtr", h)).jobs
                j1, j2 = st.jobs
                ready = tr[0]
                pe.wait_ge(bank_taken[ready.bank], taken_at(ready))
                ready = tr[1]
                pe.wait_ge(bank_taken[ready.bank], taken_at(ready))
                pe.wait_ge(bank_taken[j1.bank], turn_at(j1))
                for n, src in enumerate((TM[:, i, 4, :], TM[:, i, 0, :], TM[:, i, 5, :], TM[:, i, 1, :])):
                    ins = transpose(PS[:, j1.bank, n * P:(n + 1) * P], src)
                    if n == 3:
                        ins.then_inc(bank_full[j1.bank], 1)
                pe.wait_ge(bank_taken[j2.bank], turn_at(j2))
                for n, src in enumerate((TM[:, i, 2, :], TM[:, i, 3, :], TM[:, i, 8, :])):
                    ins = transpose(PS[:, j2.bank, n * P:(n + 1) * P], src)
                    if n == 2:
                        ins.then_inc(bank_full[j2.bank], 1)

            def ddc(st):
                job = st.jobs[0]
                if st.h == 0:
                    ready = named("cumg").jobs[0]
                    pe.wait_ge(bank_taken[ready.bank], taken_at(ready))
                pe.wait_ge(bank_taken[job.bank], turn_at(job))
                mm(PS[:, job.bank, 0:S], IDENT[:, st.h:st.h + 1].to_broadcast([P, P]), GTR[:, :]
                   ).then_inc(bank_full[job.bank], 1)

            def dkk(st):
                job, i = st.jobs[0], st.h % 2
                for j2 in named(("dtf", st.h)).jobs:
                    if j2.bank != job.bank:
                        pe.wait_ge(bank_taken[j2.bank], taken_at(j2))
                pe.wait_ge(bank_taken[job.bank], turn_at(job))
                for t in range(T):
                    ins = mm(PS[:, job.bank, t * S:(t + 1) * S], FBM[:, i, t, :],
                             FA[:, i, 2 * t:2 * t + 2, :].rearrange("p a b -> p (a b)"))
                    if t == 1:
                        ins.then_inc(bank_full[job.bank], 1)

            def dl0(st):
                job, i = st.jobs[0], st.h % 2
                pe.wait_ge(level_masked, reach("level_masked", st.at["level_masked"]))
                pe.wait_ge(bank_taken[job.bank], turn_at(job))
                for t in range(T):
                    ins = mm(PS[:, job.bank, t * P:(t + 1) * P], MT[:, i, t, :], IDENT)
                    if t == 1:
                        ins.then_inc(bank_full[job.bank], 1)

            def dla(st):
                job, i, s = st.jobs[0], st.h % 2, st.s
                ready = named(("dlb", st.h, s - 1) if s > 1 else ("dl0", st.h)).jobs[0]
                pe.wait_ge(bank_taken[ready.bank], taken_at(ready))
                pe.wait_ge(bank_taken[job.bank], turn_at(job))
                for t in range(T):
                    ins = mm(PS[:, job.bank, t * P:(t + 1) * P], AL[:, i, 2 * t, :], TT[:, i, t, :])
                ins.then_inc(bank_full[job.bank], 1)

            def dlb(st):
                job, i, s = st.jobs[0], st.h % 2, st.s
                ready = named(("dla", st.h, s)).jobs[0]
                pe.wait_ge(bank_taken[ready.bank], taken_at(ready))
                pe.wait_ge(bank_taken[job.bank], turn_at(job))
                b = job.bank
                if s < LEVELS - 1:
                    for t in range(T):
                        mm(PS[:, b, t * P:(t + 1) * P], TT[:, i, 2 + t, :], P1S[:, i, t, :])
                for t in range(T):
                    ins = mm(PS[:, b, S + t * P:S + (t + 1) * P], P1S[:, i, t, :], TT[:, i, 2 + t, :])
                    if t == 1:
                        ins.then_inc(bank_full[b], 1)

            def du1(st):
                job, i = st.jobs[0], st.h % 2
                b = job.bank
                ready = named(("dlb", st.h, LEVELS - 1)).jobs[0]
                pe.wait_ge(bank_taken[ready.bank], taken_at(ready))
                pe.wait_ge(bank_taken[job.bank], turn_at(job))
                mm(PS[:, b, 0:P], TT[:, i, 2, :], TM[:, i, 9, :])
                mm(PS[:, b, P:S], TM[:, i, 7, :], TT[:, i, 3, :]).then_inc(bank_full[b], 1)

            def du2(st):
                job, i = st.jobs[0], st.h % 2
                ready = named(("du1", st.h)).jobs[0]
                pe.wait_ge(bank_taken[ready.bank], taken_at(ready))
                pe.wait_ge(bank_taken[job.bank], turn_at(job))
                mm(PS[:, job.bank, 0:P], TM[:, i, 6, :], VW[:, i, 0, :]).then_inc(bank_full[job.bank], 1)

            def du3(st):
                job, i = st.jobs[0], st.h % 2
                ready = named(("du2", st.h)).jobs[0]
                pe.wait_ge(bank_taken[ready.bank], taken_at(ready))
                pe.wait_ge(bank_taken[job.bank], turn_at(job))
                mm(PS[:, job.bank, 0:P], TT[:, i, 3, :], TM[:, i, 10, :], True, False)
                mm(PS[:, job.bank, 0:P], VW[:, i, 1, :], VS[:, i, 0, :], False, True).then_inc(bank_full[job.bank], 1)

            def du4(st):
                job, i = st.jobs[0], st.h % 2
                b = job.bank
                ready = named(("du3", st.h)).jobs[0]
                pe.wait_ge(bank_taken[ready.bank], taken_at(ready))
                pe.wait_ge(bank_taken[job.bank], turn_at(job))
                mm(PS[:, b, 0:P], AL[:, i, 1, :], VW[:, i, 0, :])
                mm(PS[:, b, P:S], FBM[:, i, 2, :], VS[:, i, 0, :], True, False)
                mm(PS[:, b, P:S], AL[:, i, 3, :], VS[:, i, 1, :], False, True).then_inc(bank_full[b], 1)

            def dot(st):
                job, i = st.jobs[0], st.h % 2
                ready = named(("du4", st.h)).jobs[0]
                pe.wait_ge(bank_taken[ready.bank], taken_at(ready))
                pe.wait_ge(bank_taken[job.bank], turn_at(job))
                for t in range(T):
                    ins = transpose(PS[:, job.bank, t * P:(t + 1) * P], OD[:, i, t, :])
                    if t == 1:
                        ins.then_inc(bank_full[job.bank], 1)

            pe.drain().then_inc(slots_free, SLOTS)
            for b in range(8):
                pe.drain().then_inc(bank_taken[b], 1)
            pe.wait_ge(ident_loaded, 16)
            pe.wait_ge(zeros_set, 1)
            walk(pe, {"xt": xt, "acc": acc, "gu": gu, "down": down, "pb": pb, "pc": pc, "pf": pf, "cum": cum,
                      "pa": pb, "conva": project, "score": score, "turn": turn_, "out_open": out_open,
                      "value": value, "out_turn": out_turn, "lnb1": lnb1, "lnb3": lnb3, "gy": gy, "wo": wo}, 1)
            now.blk, now.l = 2, 0
            pe.wait_ge(table_loaded, 3 * 16)
            pe.wait_ge(bank_taken[0], reach(("taken", 0), 0))
            pe.matmul(PS[0:NH_A, 0, 0:384], ROWS[0:32, 1, 0:NH_A], ROWS[0:32, 0, :], start=True, stop=True
                      ).then_inc(prologue_row, 1)
            pe.wait_ge(prologue_done, 1)
            walk(pe, {"xt": xt, "acc": acc, "gu": gu, "down": down, "score": score, "turn": turn_,
                      "out_open": out_open, "value": value, "out_turn": out_turn, "gy": gy, "wo": wo, "ps": ps,
                      "pk": lambda st: project(st, fresh=1), "pq": project, "pv": lambda st: project(st, True), "pz": project,
                      "pconv": project, "cumg": cumg, "dtr": dtr, "dtf": dtf, "ddc": ddc, "dkk": dkk, "dl0": dl0,
                      "dla": dla, "dlb": dlb, "du1": du1, "du2": du2, "du3": du3, "du4": du4, "dot": dot}, 2)

        @block.scalar
        def _(act):
            def copy(dst, src, scale=1.0):
                return act.activation(dst, src, ACT.Copy, scale=scale)

            def norm(st):
                for t in range(T):
                    act.wait_ge(residual_ready, reach("residual_ready", 2 * st.s - 1 + t))
                    act.activation(XN[:, t, :], H[:, t, :], ACT.Square, scale=D ** -0.5,
                                   accum_out=SS[:, t:t + 1]).then_inc(squares_summed, 1)

            def split_high(i):
                act.wait_ge(slot_loaded[i % SLOTS], loaded_at(i))
                copy(HIGH[:, i % SLOTS, 0:width(i)], RING[:, i % SLOTS, 0:width(i)]).then_inc(high_ready, 1)

            def xt(st):
                act.wait_ge(params_loaded, reach("params_loaded", 0))
                for k2, job in enumerate(st.jobs):
                    act.wait_ge(bank_full[job.bank], full_at(job))
                    b = job.bank
                    if now.blk == 1:
                        g = prm(f"g{st.s}", 1)
                        for kk in range(2):
                            k = 2 * k2 + kk
                            last = copy(XTH[:, k, :], PS[:, b, kk * S:(kk + 1) * S], g[:, k:k + 1])
                        last.then_inc(activation_high_ready, 1)
                    else:
                        if k2 >= 2:
                            before = st.jobs[k2 - 2]
                            act.wait_ge(bank_taken[before.bank], taken_at(before))
                        for kk in range(2):
                            k = 8 * st.s + 2 * k2 + kk
                            last = act.activation(XTF[:, k2 % 2, kk * S:(kk + 1) * S], PS[:, b, kk * S:(kk + 1) * S],
                                                  ACT.Identity, scale=prm("ing", 2)[:, k:k + 1],
                                                  bias=prm("inb", 2)[:, k:k + 1])
                        last.then_inc(activation_high_ready, 1)

            def gu(st):
                job = st.jobs[0]
                act.wait_ge(bank_full[job.bank], full_at(job))
                if st.j >= 2:
                    ready = named(("gu", st.s, st.j - 2)).jobs[0]
                    act.wait_ge(bank_taken[ready.bank], taken_at(ready))
                act.activation(SG[:, st.j % 2, :], PS[:, job.bank, 0:S], ACT.Silu).then_inc(gate_silu_ready, 1)

            def post(st):
                for t in range(T):
                    j0, j1 = st.acc.jobs[2 * t], st.acc.jobs[2 * t + 1]
                    act.wait_ge(bank_full[j0.bank], full_at(j0))
                    act.wait_ge(bank_full[j1.bank], full_at(j1))
                    act.activation(XN[:, t, :], PS[:, j0.bank:j0.bank + 2, :].rearrange("p a b -> p (a b)"),
                                   ACT.Square, scale=st.root, accum_out=SS[:, 2 + t:3 + t]
                                      ).then_inc(squares_summed, 1)

            def lam(st):
                act.wait_ge(lambda_dots, reach("lambda_dots", 1))
                act.activation(ELAM[:, :], LAM[:, :], ACT.Exp).then_inc(lambda_exps, 1)

            def pb(st):
                job = st.jobs[0]
                act.wait_ge(bank_full[job.bank], full_at(job))
                if st.p >= 2:
                    before = named(("pb", st.p - 2)).jobs[0]
                    act.wait_ge(bank_taken[before.bank], taken_at(before))
                act.activation(TH[:, st.p % 2, 0:S], PS[:, job.bank, S:2 * S], ACT.Tanh, scale=0.5
                               ).then_inc(branch_gate_ready, 1)

            def pc(st):
                job, p = st.jobs[0], st.p
                act.wait_ge(bank_full[job.bank], full_at(job))
                src = PS[:, job.bank, :].rearrange("p (a b) -> p a b", a=2)
                if st.what in ("cq", "dq"):
                    dst = CQ if st.what == "cq" else DQ
                    last = copy(dst[:, 2 * p:2 * p + 2, :], src)
                elif st.what in ("ck", "dk"):
                    dst = CK if st.what == "ck" else DK
                    for m in range(2):
                        rows = slice(64 * m, 64 * m + 64)
                        last = copy(dst[rows, 2 * p:2 * p + 2, m, :], src[rows])
                else:
                    dst = CV if st.what == "cv" else DV
                    last = copy(dst[:, :, p * S:(p + 1) * S], src)
                last.then_inc(bank_taken[job.bank], 1)

            def pf(st):
                ready = st.jobs[0]
                act.wait_ge(bank_taken[ready.bank], taken_at(ready))
                act.activation(ZA_[:, :, :], ZF[:, :, :], ACT.Abs)
                act.drain()
                act.activation(ZA_[:, :, :], ZA_[:, :, :], ACT.Exp, scale=-1.0)
                act.drain()
                act.activation(ZL[:, :, :], ZA_[:, :, :], ACT.Ln, bias=1.0).then_inc(forget_log_ready, 1)

            def cum(st):
                job = st.jobs[0]
                act.wait_ge(bank_full[job.bank], full_at(job))
                copy(NC[0:8, :], PS[0:8, job.bank, 0:S], -1.0 / QK_SCALE).then_inc(bank_taken[job.bank], 1)

            def pa(st):
                job = st.jobs[0]
                act.wait_ge(bank_full[job.bank], full_at(job))
                if st.p >= 2:
                    before = named(("pa", st.p - 2)).jobs[0]
                    act.wait_ge(bank_taken[before.bank], taken_at(before))
                copy(TH[:, st.p % 2, 0:S], PS[:, job.bank, 0:S]).then_inc(branch_gate_ready, 1)

            def score(st):
                e = st.e
                ready = st.jobs[0]
                act.wait_ge(bank_taken[ready.bank], taken_at(ready))
                ls = LS[:, e % 16, :]
                act.activation(EX[:, e % 4, 0:P], EX[:, e % 4, 0:P], ACT.Exp, bias=NM[:, e % 4, 0:1],
                               scale=QK_SCALE, accum_out=ls[:, 0:1])
                act.activation(EX[:, e % 4, P:384], EX[:, e % 4, P:384], ACT.Exp, bias=NM[:, e % 4, 1:2],
                               scale=QK_SCALE, accum_out=ls[:, 1:2]).then_inc(probs_ready, 1)
                if st.br == "a":
                    act.activation(ES[:, e, :], NM[:, e % 4, :], ACT.Exp, bias=prm("sink", 2)[:, e:e + 1]
                                   ).then_inc(sink_exp_ready, 1)

            def turn_(st):
                job = st.jobs[0]
                n = named(("value", st.br, st.h)).at["values_summed"]
                act.wait_ge(bank_full[job.bank], full_at(job))
                if n > 3:
                    act.wait_ge(values_summed, reach("values_summed", n - 3))
                copy(PT[:, n % 3, :], PS[:, job.bank, 0:384]).then_inc(bank_taken[job.bank], 1)

            def out_norm(st):
                if st.br != "c":
                    return
                act.wait_ge(values_summed,
                            reach("values_summed", named(("value", "c", NH_C - 1)).at["values_summed"]))
                for t in range(T):
                    for h in range(NH_C):
                        last = act.activation(JUNK[:, :], PS[:, 6 + t, h * P:(h + 1) * P], ACT.Square,
                                              scale=P ** -0.5, accum_out=SSO[:, t * 4 + h:t * 4 + h + 1])
                        if (t, h) != (T - 1, NH_C - 1):
                            act.drain()
                last.then_inc(out_squares_summed, 1)

            def out_turn(st):
                for p, job in enumerate(st.jobs):
                    act.wait_ge(bank_full[job.bank], full_at(job))
                    c = 2 * p + (4 * st.half if st.br == "a" else 0)
                    dst = {"a": YAH, "c": Y1[2][0], "d": Y1[3][0]}[st.br][:, c:c + 2, :].rearrange("p a b -> p (a b)")
                    copy(dst, PS[:, job.bank, :], SUBG[:, 0:1] if st.br == "c" else 1.0
                         ).then_inc(activation_high_ready, 1)

            def lnb3(st):
                for p, job in enumerate(st.jobs):
                    act.wait_ge(bank_full[job.bank], full_at(job))
                    for n in range(2):
                        c = 2 * p + n
                        last = act.activation(YB1[:, c, :], PS[:, job.bank, n * S:(n + 1) * S], ACT.Silu,
                                              bias=prm("blb", 1)[:, c:c + 1], scale=prm("blg", 1)[:, c:c + 1])
                    last.then_inc(bank_taken[job.bank], 1)

            def gy(st):
                job, k = st.jobs[0], st.k
                act.wait_ge(bank_full[job.bank], full_at(job))
                n = st.i * KB + k
                if n >= 2:
                    ready = named(("gy", (n - 2) // KB, (n - 2) % KB)).jobs[0]
                    act.wait_ge(bank_taken[ready.bank], taken_at(ready))
                act.activation(TH[:, n % 2, 0:S], PS[:, job.bank, 0:S], ACT.Tanh, scale=0.5
                   ).then_inc(gate_tanh_ready, 1)

            def ps(st):
                ready = st.jobs[0]
                act.wait_ge(bank_taken[ready.bank], taken_at(ready))
                act.activation(BETA[:, :, :], SBT[:, :, 0:8], ACT.Tanh, scale=0.5)
                act.activation(EAL[:, :], prm("alog", 2), ACT.Exp)
                act.activation(ZA_[:, :, :], SBT[:, :, 8:16], ACT.Abs)
                act.drain()
                act.activation(ZA_[:, :, :], ZA_[:, :, :], ACT.Exp, scale=-1.0)
                act.drain()
                act.activation(ZL[:, :, :], ZA_[:, :, :], ACT.Ln, bias=1.0).then_inc(small_logs_ready, 1)

            def pk(st):
                job = st.jobs[0]
                act.wait_ge(bank_full[job.bank], full_at(job))
                src = PS[:, job.bank, :].rearrange("p (a b) -> p a b", a=2)
                for m in range(2):
                    rows = slice(64 * m, 64 * m + 64)
                    for c in range(2):
                        last = copy(KA[rows, 2 * c + m, :], src[rows, c, :])
                last.then_inc(bank_taken[job.bank], 1)

            def pq(st):
                job = st.jobs[0]
                act.wait_ge(bank_full[job.bank], full_at(job))
                copy(QA[:, 2 * st.p:2 * st.p + 2, :].rearrange("p a b -> p (a b)"), PS[:, job.bank, :]
                     ).then_inc(bank_taken[job.bank], 1)

            def pv(st):
                job = st.jobs[0]
                act.wait_ge(bank_full[job.bank], full_at(job))
                copy(VA[:, :, :].rearrange("p a b -> p (a b)"), PS[:, job.bank, :]).then_inc(bank_taken[job.bank], 1)

            def cumg(st):
                act.wait_ge(decay_diff_ready, reach("decay_diff_ready", 1))
                act.activation(ET[:, :, :], ET[:, :, :], ACT.Exp)
                act.activation(EG[:, :, :], G[:, :, :], ACT.Exp).then_inc(decay_exps_ready, 1)

            def pz(st):
                job = st.jobs[0]
                act.wait_ge(bank_full[job.bank], full_at(job))
                if st.p >= 2:
                    ready = named(("pz", st.p - 2)).jobs[0]
                    act.wait_ge(bank_taken[ready.bank], taken_at(ready))
                act.activation(TH[:, st.p % 2, :], PS[:, job.bank, :], ACT.Tanh, scale=0.5).then_inc(z_tanh_ready, 1)

            def taps(st):
                c, n = st.p, named(("silu", st.hp, st.w)).at["conv_silu_ready"]
                if n > 1:
                    act.wait_ge(conv_silu_ready, reach("conv_silu_ready", n - 1))
                act.wait_ge(conv_ready, reach("conv_ready", st.at["conv_ready"]))
                act.activation(TC[:, c * S:(c + 1) * S], CO[:, 2 * st.w + c, :], ACT.Tanh, scale=0.5
                               ).then_inc(conv_tanh_ready, 1)

            def dtr(st):
                i = st.h % 2
                done = st.jobs[0]
                act.wait_ge(bank_full[done.bank], full_at(done))
                done = st.jobs[1]
                act.wait_ge(bank_full[done.bank], full_at(done))
                if st.h >= 2:
                    act.wait_ge(qk_rsqrt_ready,
                                reach("qk_rsqrt_ready", named(("dtr", st.h - 2)).at["qk_rsqrt_ready"]))
                for n in range(4):
                    b = st.jobs[n // 2].bank
                    last = act.activation(P1S[:, i, 0, :], PS[:, b, n % 2 * P:(n % 2 + 1) * P], ACT.Square,
                                          accum_out=SSD[:, i, n:n + 1])
                    if n < 3:
                        act.drain()
                last.then_inc(qk_squares_summed, 1)

            def dte(st):
                i, h = st.h % 2, st.h
                b = named(("dtr", h)).jobs[0].bank
                act.wait_ge(head_scalars_ready, reach("head_scalars_ready", st.at["head_scalars_ready"]))
                sc = SC[:, i, :]
                for n, src, scale in ((0, 0, sc[:, 0:1]), (1, 1, sc[:, 1:2]), (8, 1, sc[:, 8:9]),
                                      (9, 2, HB[:, 0, h:h + 1]), (10, 3, HB[:, 1, h:h + 1])):
                    last = copy(TM[:, i, n, :], PS[:, b, src * P:(src + 1) * P], scale)
                last.then_inc(bank_taken[b], 1)

            def dtf(st):
                job = st.jobs[0]
                act.wait_ge(bank_full[job.bank], full_at(job))
                copy(FA[:, st.h % 2].rearrange("p a b -> p (a b)"), PS[:, job.bank, :]
                     ).then_inc(bank_taken[job.bank], 1)

            def ddc(st):
                i = st.h % 2
                ready = st.jobs[0]
                act.wait_ge(bank_taken[ready.bank], taken_at(ready))
                if st.h >= 2:
                    ready = named(("dkk", st.h - 2)).jobs[0]
                    act.wait_ge(bank_taken[ready.bank], taken_at(ready))
                act.activation(DEC[:, i].rearrange("p (t k) n -> p t k n", t=T)[:, :, 1, :], DD[:, i], ACT.Exp
                               ).then_inc(decay_ready, 1)

            def dla(st):
                job = st.jobs[0]
                act.wait_ge(bank_full[job.bank], full_at(job))
                copy(P1S[:, st.h % 2].rearrange("p a b -> p (a b)"), PS[:, job.bank, 0:S], -1.0
                     ).then_inc(bank_taken[job.bank], 1)

            def evac(dst, n):
                def run(st):
                    job, i = st.jobs[0], st.h % 2
                    act.wait_ge(bank_full[job.bank], full_at(job))
                    copy(dst(i), PS[:, job.bank, 0:n]).then_inc(bank_taken[job.bank], 1)
                return run

            def du4(st):
                job, i = st.jobs[0], st.h % 2
                act.wait_ge(bank_full[job.bank], full_at(job))
                for t in range(T):
                    last = act.activation(P1S[:, i, t, :], PS[:, job.bank, t * P:(t + 1) * P], ACT.Square,
                                          scale=P ** -0.5, accum_out=SSO[:, 2 * i + t:2 * i + t + 1])
                last.then_inc(out_squares_summed, 1)

            act.dma_start(CON[:, P:NCON1], con[0, :, P:NCON1]).then_inc(con_loaded, 16)
            act.dma_start(ROWS[0:32, 0, :], onehot).then_inc(table_loaded, 16)
            act.dma_start(ROWS[0:32, 1, 0:NH_A], relb).then_inc(table_loaded, 16)
            act.dma_start(ROWS[0:NH_A, 2, :], rowmask.to_broadcast([NH_A, 384])).then_inc(table_loaded, 16)
            act.wait_ge(x_loaded, 16)
            act.wait_ge(zeros_set, 1)
            walk(act, {"norm": norm, "xt": xt, "gu": gu, "post": post, "lam": lam, "pb": pb, "pc": pc, "pf": pf,
                       "cum": cum, "pa": pa, "score": score, "turn": turn_, "out_norm": out_norm,
                       "out_turn": out_turn, "lnb3": lnb3, "gy": gy}, 1, split_high)
            now.blk, now.l = 2, 0
            act.wait_ge(residual_ready, reach("residual_ready", 0))
            walk(act, {"xt": xt, "gu": gu, "score": score, "turn": turn_, "out_turn": out_turn, "gy": gy, "ps": ps,
                       "pk": pk, "pq": pq, "pv": pv, "cumg": cumg, "pz": pz, "taps": taps, "dtr": dtr, "dte": dte,
                       "dtf": dtf, "ddc": ddc, "dla": dla,
                       "du1": evac(lambda i: VW[:, i].rearrange("p a b -> p (a b)"), S),
                       "du2": evac(lambda i: VS[:, i, 0, :], P), "du3": evac(lambda i: VS[:, i, 1, :], P),
                       "du4": du4}, 2, split_high)

        @block.vector
        def _(dve):
            def norm(st):
                for t in range(T):
                    dve.wait_ge(rsqrt_ready, reach("rsqrt_ready", st.at["rsqrt_ready"] - 1 + t))
                    dve.tensor_scalar(DG[:, t, :], IDENT, RS[:, t:t + 1], None, ALU.mult).then_inc(normed_ready, 1)

            def split_low(i):
                if low_sem(i) is low_by_vector:
                    dve.wait_ge(high_ready, reach("high_ready", i + 1))
                    raw, high = RING[:, i % SLOTS, 0:width(i)], HIGH[:, i % SLOTS, 0:width(i)]
                    dve.tensor_tensor(LOW[:, i % SLOTS, 0:width(i)], raw, high.bitcast(F32), ALU.subtract
                                      ).then_inc(low_by_vector, 1)

            def split_here(high, low, whole, drain=True):
                if drain:
                    dve.drain()
                dve.tensor_copy(high, whole)
                dve.drain()
                return dve.tensor_tensor(low, whole, high.bitcast(F32), ALU.subtract)

            def small_split(st):
                w = prm("wf", 1) if now.blk == 1 else prm("ws", 2)
                high, low = (NARROW[:, part, 0:w.shape[1]] for part in range(2))
                split_here(high, low, w).then_inc(small_weights_ready, 1)

            def xt(st):
                for k2, job in enumerate(st.jobs):
                    b = job.bank
                    if now.blk == 2:
                        dve.drain()
                    dve.wait_ge(activation_high_ready,
                                reach("activation_high_ready", st.at["activation_high_ready"] - 3 + k2))
                    if now.blk == 1:
                        g = prm(f"g{st.s}", 1)
                        for kk in range(2):
                            k = 2 * k2 + kk
                            last = dve.scalar_tensor_tensor(out=XTL[:, k, :], in0=PS[:, b, kk * S:(kk + 1) * S],
                                                            scalar=g[:, k:k + 1], in1=XTH[:, k, :].bitcast(F32),
                                                            op0=ALU.mult, op1=ALU.subtract)
                    else:
                        high, low = (v[:, 2 * k2:2 * k2 + 2, :].rearrange("p a b -> p (a b)") for v in XT)
                        last = split_here(high, low, XTF[:, k2 % 2, :], False)
                    last.then_inc(bank_taken[b], 1)

            def gu(st):
                job = st.jobs[0]
                dve.wait_ge(gate_silu_ready, reach("gate_silu_ready", st.at["gate_silu_ready"]))
                hidden = HF[:, st.j % 2, :]
                dve.tensor_tensor(hidden, SG[:, st.j % 2, :], PS[:, job.bank, S:2 * S], ALU.mult
                                  ).then_inc(bank_taken[job.bank], 1)
                split_here(HTH[:, st.j % 4, :], HTL[:, st.j % 4, :], hidden).then_inc(hidden_ready, 1)

            def out_turn(st):
                for p, job in enumerate(st.jobs):
                    c = 2 * p + (4 * st.half if st.br == "a" else 0)
                    high, low = (v[:, c:c + 2, :].rearrange("p a b -> p (a b)")
                                 for v in {"a": (YAH, YAL), "c": Y1[2], "d": Y1[3]}[st.br])
                    dve.wait_ge(activation_high_ready,
                                reach("activation_high_ready", st.at["activation_high_ready"] - 1 + p))
                    if st.br == "c":
                        ins = dve.scalar_tensor_tensor(out=low, in0=PS[:, job.bank, :], scalar=SUBG[:, 0:1],
                                                       in1=high.bitcast(F32), op0=ALU.mult, op1=ALU.subtract)
                    else:
                        ins = dve.tensor_tensor(low, PS[:, job.bank, :], high.bitcast(F32), ALU.subtract)
                    ins.then_inc(bank_taken[job.bank], 1)

            def lnb3(st):
                for job in st.jobs:
                    dve.wait_ge(bank_taken[job.bank], taken_at(job))
                dve.tensor_copy(Y1[1][0], YB1)
                dve.drain()
                dve.tensor_tensor(Y1[1][1], YB1, Y1[1][0].bitcast(F32), ALU.subtract).then_inc(branch_b_ready, 1)

            def post(st):
                dve.wait_ge(feature_rows_loaded, reach("feature_rows_loaded", 16 * (st.s + 1)))
                for t in range(T):
                    dve.wait_ge(rsqrt_ready, reach("rsqrt_ready", st.at["rsqrt_ready"] - 1 + t))
                    for n in range(2):
                        b = st.acc.jobs[2 * t + n].bank
                        cols = slice(n * HALF, (n + 1) * HALF)
                        dve.scalar_tensor_tensor(out=XN[:, t, cols], in0=PS[:, b, :], scalar=RS[:, 2 + t:3 + t],
                                                 in1=PG[:, 0, cols], op0=ALU.mult, op1=ALU.mult
                                                 ).then_inc(bank_taken[b], 1)
                    dve.drain()
                    dve.tensor_tensor(H[:, t, :], H[:, t, :], XN[:, t, :], ALU.add).then_inc(residual_ready, 1)

            def lam(st):
                lv = prm("lam", 1, 4)
                for n in range(2):
                    last = dve.tensor_tensor_reduce(TMP[:, n, 0:64], lv[:, 2 * n, :], lv[:, 2 * n + 1, :], 1.0, 0.0,
                                                    ALU.mult, ALU.add, LAM[:, n:n + 1])
                last.then_inc(lambda_dots, 1)
                dve.tensor_scalar(BWH.rearrange("p a b -> p (a b)"), prm("bw", 1), 0.5, None, ALU.mult)
                dve.tensor_tensor(SUBG[:, :], prm("sub", 1), prm("lami", 1)[:, 1:2], ALU.mult)
                dve.wait_ge(lambda_exps, reach("lambda_exps", 1))
                dve.tensor_tensor(NLAM[:, :], ELAM[:, 1:2], ELAM[:, 0:1], ALU.subtract)
                dve.drain()
                dve.tensor_tensor(NLAM[:, :], NLAM[:, :], prm("lami", 1)[:, 0:1], ALU.subtract
                                  ).then_inc(lambda_ready, 1)
                dve.drain()

            def pb(st):
                job = st.jobs[0]
                dve.wait_ge(branch_gate_ready, reach("branch_gate_ready", st.at["branch_gate_ready"]))
                dve.scalar_tensor_tensor(out=ZB[:, st.p, :], in0=TH[:, st.p % 2, 0:S], scalar=1.0,
                                         in1=PS[:, job.bank, 0:S], op0=ALU.add, op1=ALU.mult
                                         ).then_inc(bank_taken[job.bank], 1)

            def convb(st):
                for n in range(st.a, st.b):
                    tap = 30 - n
                    dve.drain()
                    for c in range(4):
                        w = BWH[:, tap, c:c + 1]
                        if n == 0:
                            last = dve.tensor_scalar(ACCB[:, c, :], ZB[:, c, :], w, prm("bb", 1)[:, c:c + 1],
                                                     ALU.mult, ALU.add)
                        else:
                            last = dve.scalar_tensor_tensor(out=ACCB[:, c, n:S], in0=ZB[:, c, 0:S - n], scalar=w,
                                                            in1=ACCB[:, c, n:S], op0=ALU.mult, op1=ALU.add)
                if st.b == 31:
                    last.then_inc(conv_b_ready, 1)

            def pf(st):
                job = st.jobs[0]
                dve.wait_ge(bank_full[job.bank], full_at(job))
                for t in range(T):
                    last = dve.tensor_tensor(ZF[:, t, :], PS[:, job.bank, t * 8:(t + 1) * 8], prm("fb", 1), ALU.add)
                last.then_inc(bank_taken[job.bank], 1)
                dve.drain()
                dve.tensor_scalar(LF[:, :, :], ZF[:, :, :], 0.0, None, ALU.min)
                dve.drain()
                dve.wait_ge(forget_log_ready, reach("forget_log_ready", 1))
                dve.tensor_tensor(LF[:, :, :], LF[:, :, :], ZL[:, :, :], ALU.subtract).then_inc(log_forget_ready, 1)

            def pa(st):
                job = st.jobs[0]
                dve.wait_ge(branch_gate_ready, reach("branch_gate_ready", st.at["branch_gate_ready"]))
                dve.tensor_tensor(ZA[:, st.p, :], TH[:, st.p % 2, 0:S], PS[:, job.bank, S:2 * S], ALU.mult
                                  ).then_inc(bank_taken[job.bank], 1)

            def conva(st):
                job, c2 = st.jobs[0], 2 * st.p
                aw = prm("aw", 1, 3)
                for n in range(3):
                    dve.drain()
                    for c in (c2, c2 + 1):
                        w = aw[:, 2 - n, c:c + 1]
                        if n == 0:
                            dve.tensor_scalar(ACCA[:, c, :], ZA[:, c, :], w, None, ALU.mult)
                        else:
                            dve.scalar_tensor_tensor(out=ACCA[:, c, n:S], in0=ZA[:, c, 0:S - n], scalar=w,
                                                     in1=ACCA[:, c, n:S], op0=ALU.mult, op1=ALU.add)
                dve.drain()
                dve.wait_ge(bank_full[job.bank], full_at(job))
                dst = ACCA[:, c2:c2 + 2, :]
                dve.tensor_tensor(dst.rearrange("p a b -> p (a b)"), dst.rearrange("p a b -> p (a b)"),
                                  PS[:, job.bank, :], ALU.mult).then_inc(bank_taken[job.bank], 1)
                split_here(Y1[0][0][:, c2:c2 + 2, :], Y1[0][1][:, c2:c2 + 2, :], dst).then_inc(branch_a_ready, 1)

            def score(st):
                job, e = st.jobs[0], st.e
                b = job.bank
                dve.wait_ge(bank_full[job.bank], full_at(job))
                if e >= 4:
                    done = named(("turn", st.br, (e - 4) // (2 if st.br == "c" else 1))).jobs[0]
                    dve.wait_ge(bank_full[done.bank], full_at(done))
                    if st.br == "a":
                        dve.wait_ge(sink_exp_ready,
                                    reach("sink_exp_ready", named(("score", "a", e - 4)).at["sink_exp_ready"]))
                elif st.br == "d":
                    done = named(("turn", "c", NH_C - 1)).jobs[0]
                    dve.wait_ge(bank_full[done.bank], full_at(done))
                if st.br == "c" and e == 0:
                    dve.wait_ge(con_loaded, 16)
                if st.br == "a" and e == 0:
                    dve.wait_ge(bias_loaded, reach("bias_loaded", 16 * 4))
                bias = {"c": lambda: cst("alibi", 1, NH_C)[:, e // 2, :], "d": lambda: cst("causal", 1),
                        "a": lambda: BIAS[:, e, :]}[st.br]()
                dve.memset(TOUCH[:, 0:1], 0.0)
                dve.tensor_tensor_reduce(EX[:, e % 4, 0:P], PS[:, b, 0:P], bias[:, P:S], 1.0, -3e38, ALU.add,
                                         ALU.max, MX[:, e % 4, 0:1])
                dve.tensor_tensor_reduce(EX[:, e % 4, P:384], PS[:, b, P:384], bias, 1.0, -3e38, ALU.add,
                                         ALU.max, MX[:, e % 4, 1:2])
                dve.drain()
                if st.br == "a":
                    last = dve.tensor_scalar(NM[:, e % 4, :], MX[:, e % 4, :], SINK8[:, e:e + 1], -QK_SCALE,
                                             ALU.max, ALU.mult)
                else:
                    last = dve.tensor_scalar(NM[:, e % 4, :], MX[:, e % 4, :], -QK_SCALE, None, ALU.mult)
                last.then_inc(bank_taken[b], 1)

            def diff(st):
                h = st.h
                e0, e1 = 2 * h % 4, (2 * h + 1) % 4
                dve.drain()
                dve.wait_ge(probs_ready, reach("probs_ready", named(("score", "c", 2 * h + 1)).at["probs_ready"]))
                if h == 0:
                    dve.wait_ge(lambda_ready, reach("lambda_ready", 1))
                dve.reciprocal(RC[:, 0:4], LS[:, 2 * h:2 * h + 2, :].rearrange("p a b -> p (a b)"))
                dve.drain()
                dve.tensor_scalar(RC[:, 2:4], RC[:, 2:4], NLAM[:, 0:1], None, ALU.mult)
                parts = ((0, slice(0, P)), (1, slice(P, 384)))
                for t, c in parts:
                    dve.tensor_scalar(EX[:, e0, c], EX[:, e0, c], RC[:, t:t + 1], None, ALU.mult)
                dve.drain()
                for t, c in parts:
                    last = dve.scalar_tensor_tensor(out=EX[:, e0, c], in0=EX[:, e1, c], scalar=RC[:, 2 + t:3 + t],
                                                    in1=EX[:, e0, c], op0=ALU.mult, op1=ALU.add)
                last.then_inc(probs_combined, 1)

            def out_norm(st):
                key = st.half if st.br == "a" else st.br
                jobs = named(("oo", key)).jobs
                if st.br == "c":
                    dve.wait_ge(out_rsqrt_ready, reach("out_rsqrt_ready", st.at["out_rsqrt_ready"]))
                    n, w = 4, P
                else:
                    n, w = 8, 64
                    first = 8 * st.half if st.br == "a" else 0
                    dve.wait_ge(values_summed,
                                reach("values_summed", named(("value", st.br, first + 7)).at["values_summed"]))
                    if st.br == "a":
                        dve.wait_ge(sink_exp_ready,
                                    reach("sink_exp_ready", named(("score", "a", first + 7)).at["sink_exp_ready"]))
                        ls = LS[:, first:first + 8, :]
                        dve.tensor_tensor(ls, ls, ES[:, first:first + 8, :], ALU.add)
                        dve.drain()
                    dve.reciprocal(RL[:, first:first + 8, :], LS[:, first:first + 8, :])
                    dve.drain()
                    before = {"d": ("ot", "c"), "a": ("ot", 0)}[st.br]
                    if not (st.br == "a" and st.half == 0):
                        for job in named(before).jobs:
                            dve.wait_ge(bank_full[job.bank], full_at(job))
                for t in range(T):
                    if st.br == "c":
                        r = RSO[:, t * 4:t * 4 + 4].unsqueeze(2)
                    else:
                        r = RL[:, first:first + 8, t].unsqueeze(2)
                    dve.tensor_tensor(ON[:, t, :].rearrange("p (a b) -> p a b", a=n),
                                      PS[:, 6 + t, :].rearrange("p (a b) -> p a b", a=n),
                                      r.to_broadcast([P, n, w]), ALU.mult).then_inc(bank_taken[6 + t], 1)

            def lnb1(st):
                for t, job in enumerate(st.jobs):
                    dve.wait_ge(bank_full[job.bank], full_at(job))
                    dve.bn_stats(ST[:, t, :], PS[:, job.bank, :])
                    dve.drain()
                    dve.bn_aggr(MV[:, t, :], ST[:, t, :]).then_inc(mean_var_ready, 1)
                dve.drain()
                for t, job in enumerate(st.jobs):
                    dve.wait_ge(branch_b_rsqrt_ready,
                                reach("branch_b_rsqrt_ready", st.at["branch_b_rsqrt_ready"] - 1 + t))
                    dve.tensor_scalar(BN[:, t, :], PS[:, job.bank, :], MV[:, t, 0:1], RSB[:, t:t + 1],
                                      ALU.subtract, ALU.mult).then_inc(bank_taken[job.bank], 1)

            def gy(st):
                job, k, i = st.jobs[0], st.k, st.i
                n = i * KB + k
                dve.wait_ge(gate_tanh_ready, reach("gate_tanh_ready", st.at["gate_tanh_ready"]))
                dst = MG[:, k, :] if i == 0 else TMP[:, n % 2, :]
                dve.scalar_tensor_tensor(out=dst, in0=TH[:, n % 2, 0:S], scalar=1.0,
                                         in1=PS[:, job.bank, S:2 * S], op0=ALU.add, op1=ALU.mult
                                         ).then_inc(bank_taken[job.bank], 1)
                if i:
                    dve.drain()
                    dve.tensor_tensor(MG[:, k, :], MG[:, k, :], TMP[:, n % 2, :], ALU.add)
                if i == (3 if now.blk == 1 else 1):
                    high = (MGH1 if now.blk == 1 else MGH2)[:, k, :]
                    split_here(high, MGL[:, k, :], MG[:, k, :]).then_inc(merged_ready, 1)

            def factors(st):
                dve.tensor_scalar(GDH[:, :], prm("dng", 2), 0.5, None, ALU.mult)
                dve.tensor_scalar(SINK8[:, :], prm("sink", 2), 1.0 / QK_SCALE, None, ALU.mult)
                dve.drain()

            def post2(st):
                for t in range(T):
                    dve.wait_ge(residual_ready, reach("residual_ready", 2 * st.s - 1 + t))
                    for n in range(2):
                        job = st.acc.jobs[2 * t + n]
                        cols = slice(n * HALF, (n + 1) * HALF)
                        dve.wait_ge(bank_full[job.bank], full_at(job))
                        dve.scalar_tensor_tensor(out=XN[:, t, cols], in0=PS[:, job.bank, :], scalar=0.5 / ALPHA,
                                                 in1=H[:, t, cols], op0=ALU.mult, op1=ALU.add
                                                 ).then_inc(bank_taken[job.bank], 1)
                    dve.drain()
                    for n in range(2):
                        dve.bn_stats(ST[:, 2 * t + n, :], XN[:, t, n * HALF:(n + 1) * HALF])
                    dve.drain()
                    dve.bn_aggr(MV[:, t, :], ST[:, 2 * t:2 * t + 2, :]).then_inc(mean_var_ready, 1)
                dve.drain()
                for t in range(T):
                    dve.wait_ge(rsqrt_ready, reach("rsqrt_ready", st.at["rsqrt_ready"] - 1 + t))
                    dve.tensor_scalar(XN[:, t, :], XN[:, t, :], MV[:, t, 0:1], RS[:, 2 + t:3 + t],
                                      ALU.subtract, ALU.mult).then_inc(normed_ready, 1)

            def ps(st):
                job = st.jobs[0]
                dve.wait_ge(bank_full[job.bank], full_at(job))
                for t in range(T):
                    c = t * 16
                    dve.tensor_copy(SBT[:, t, 0:8], PS[:, job.bank, c:c + 8])
                    last = dve.tensor_tensor(SBT[:, t, 8:16], PS[:, job.bank, c + 8:c + 16], prm("dtb", 2), ALU.add)
                last.then_inc(bank_taken[job.bank], 1)
                dve.drain()
                dve.tensor_scalar(GG[:, :, :], SBT[:, :, 8:16], 0.0, None, ALU.max)
                dve.drain()
                dve.wait_ge(small_logs_ready, reach("small_logs_ready", 1))
                dve.tensor_tensor(GG[:, :, :], GG[:, :, :], ZL[:, :, :], ALU.add)
                dve.tensor_scalar(BETA[:, :, :], BETA[:, :, :], 0.5, 0.5, ALU.mult, ALU.add)
                dve.drain()
                for t in range(T):
                    last = dve.scalar_tensor_tensor(out=GG[:, t, :], in0=GG[:, t, :], scalar=-1.0, in1=EAL[:, :],
                                                    op0=ALU.mult, op1=ALU.mult)
                last.then_inc(log_decay_ready, 1)
                dve.tensor_scalar(HB[:, :, :], BETA[:, :, :], 0.5, None, ALU.mult)
                dve.drain()

            def cumg(st):
                job = st.jobs[0]
                dve.wait_ge(bank_full[job.bank], full_at(job))
                dve.tensor_copy(G[:, :, :].rearrange("p a b -> p (a b)"), PS[:, job.bank, 0:16])
                dve.tensor_copy(GL[:, :, :].rearrange("p a b -> p (a b)"), PS[:, job.bank, 16:32])
                dve.tensor_copy(GTR[0:8, :], PS[0:8, job.bank, 64:64 + S]
                                ).then_inc(bank_taken[job.bank], 1)
                dve.drain()
                dve.tensor_tensor(ET[:, :, :], GL[:, :, :], G[:, :, :], ALU.subtract).then_inc(decay_diff_ready, 1)
                dve.wait_ge(decay_exps_ready, reach("decay_exps_ready", 1))
                dve.tensor_tensor(BEG[:, :, :], BETA[:, :, :], EG[:, :, :], ALU.mult).then_inc(decay_scalars_ready, 1)
                dve.drain()

            def pz(st):
                job = st.jobs[0]
                dve.wait_ge(z_tanh_ready, reach("z_tanh_ready", st.at["z_tanh_ready"]))
                dve.scalar_tensor_tensor(out=ZS[:, 2 * st.p:2 * st.p + 2, :].rearrange("p a b -> p (a b)"),
                                         in0=TH[:, st.p % 2, :], scalar=1.0, in1=PS[:, job.bank, :],
                                         op0=ALU.add, op1=ALU.mult).then_inc(bank_taken[job.bank], 1)

            def taps(st):
                job, w, c = named(("pconv", st.hp, st.w)).jobs[0], st.w, st.p
                b = job.bank
                cw = prm("cw", 2, 4)
                co = CO[:, 2 * w + c, :]
                dve.wait_ge(bank_full[job.bank], full_at(job))
                if st.hp >= 1 and c == 0:
                    for h in (2 * st.hp - 2, 2 * st.hp - 1):
                        done = named(("dtr", h)).jobs[1]
                        dve.wait_ge(bank_full[done.bank], full_at(done))
                for n in range(4):
                    tap = cw[:, 3 - n, 8 * w + 2 * st.hp + c:8 * w + 2 * st.hp + c + 1]
                    src = PS[:, b, c * S:(c + 1) * S - n]
                    if n == 0:
                        dve.tensor_scalar(co[:, :], src, tap, None, ALU.mult)
                    else:
                        last = dve.scalar_tensor_tensor(out=co[:, n:S], in0=src, scalar=tap, in1=co[:, n:S],
                                                        op0=ALU.mult, op1=ALU.add)
                    if n < 3:
                        dve.drain()
                last.then_inc(conv_ready, 1)
                if c:
                    dve.drain().then_inc(bank_taken[b], 1)

            def silu(st):
                dve.wait_ge(conv_tanh_ready,
                            reach("conv_tanh_ready", named(("taps", st.hp, st.w, 1)).at["conv_tanh_ready"]))
                flat = CO[:, 2 * st.w:2 * st.w + 2, :].rearrange("p a b -> p (a b)")
                dve.scalar_tensor_tensor(out=flat, in0=TC[:, :], scalar=1.0, in1=flat, op0=ALU.add, op1=ALU.mult
                                         ).then_inc(conv_silu_ready, 1)

            def dte(st):
                i, h = st.h % 2, st.h
                b = named(("dtr", h)).jobs[1].bank
                sc, rd = SC[:, i, :], RD[:, i, :]
                dve.wait_ge(qk_rsqrt_ready, reach("qk_rsqrt_ready", named(("dtr", h)).at["qk_rsqrt_ready"]))
                dve.tensor_scalar(sc[:, 0:2], rd[:, 0:2], 128.0 ** -0.5, None, ALU.mult)
                dve.tensor_copy(sc[:, 2:4], rd[:, 2:4])
                dve.tensor_tensor(sc[:, 4:6], rd[:, 2:4], BETA[:, :, h], ALU.mult)
                dve.tensor_tensor(sc[:, 6:7], rd[:, 2:3], ET[:, 0, h:h + 1], ALU.mult)
                dve.tensor_scalar(sc[:, 7:8], rd[:, 3:4], BEG[:, 1, h:h + 1], -1.0, ALU.mult, ALU.mult)
                dve.tensor_scalar(sc[:, 8:9], rd[:, 1:2], EG[:, 1, h:h + 1], 128.0 ** -0.5, ALU.mult, ALU.mult
                                  ).then_inc(head_scalars_ready, 1)
                dve.drain()
                for n, src, s in ((2, 0, 2), (3, 1, 3), (4, 0, 4), (5, 1, 5), (6, 0, 6), (7, 1, 7)):
                    last = dve.tensor_scalar(TM[:, i, n, :], PS[:, b, src * P:(src + 1) * P], sc[:, s:s + 1], None,
                                             ALU.mult)
                last.then_inc(bank_taken[b], 1)

            def ddc(st):
                job, i, h = st.jobs[0], st.h % 2, st.h
                dve.wait_ge(bank_full[job.bank], full_at(job))
                for t in range(T):
                    last = dve.scalar_tensor_tensor(out=DD[:, i, t, :], in0=PS[:, job.bank, t * P:(t + 1) * P],
                                                    scalar=G[:, t, h:h + 1], in1=cst("maskt", 2),
                                                    op0=ALU.subtract, op1=ALU.add)
                last.then_inc(bank_taken[job.bank], 1)

            def dtf(st):
                job = st.jobs[1]
                dve.wait_ge(bank_full[job.bank], full_at(job))
                dve.tensor_copy(FBM[:, st.h % 2].rearrange("p a b -> p (a b)"), PS[:, job.bank, 0:384]
                                ).then_inc(bank_taken[job.bank], 1)

            def dkk(st):
                job, i = st.jobs[0], st.h % 2
                dve.wait_ge(bank_full[job.bank], full_at(job))
                dve.wait_ge(strict_decay_ready,
                            reach("strict_decay_ready", named(("ddc", st.h)).at["strict_decay_ready"]))
                dve.tensor_tensor(AL[:, i].rearrange("p a b -> p (a b)"), PS[:, job.bank, :],
                                  DEC[:, i].rearrange("p a b -> p (a b)"), ALU.mult
                                  ).then_inc(bank_taken[job.bank], 1)
                dve.drain()
                for t in range(T):
                    last = dve.tensor_tensor(MT[:, i, t, :], AL[:, i, 2 * t, :], cst("level", 2), ALU.mult)
                last.then_inc(level_masked, 1)

            def dl0(st):
                job, i = st.jobs[0], st.h % 2
                dve.wait_ge(bank_full[job.bank], full_at(job))
                for t in range(T):
                    dve.tensor_tensor(TT[:, i, t, :], IDENT, PS[:, job.bank, t * P:(t + 1) * P], ALU.subtract)
                for t in range(T):
                    last = dve.tensor_tensor(TT[:, i, 2 + t, :], IDENT, MT[:, i, t, :], ALU.subtract)
                last.then_inc(bank_taken[job.bank], 1)

            def dlb(st):
                job, i = st.jobs[0], st.h % 2
                dve.drain()
                dve.wait_ge(bank_full[job.bank], full_at(job))
                dve.memset(TOUCH[:, 0:1], 0.0)
                masks = cst("masks", 2).bitcast(mybir.dt.uint8).rearrange("p (s o n) -> p s o n", o=2, n=P)
                for o in range(0 if st.s < LEVELS - 1 else 1, 2):
                    new = PS[:, job.bank, o * S:(o + 1) * S].rearrange("p (a b) -> p a b", a=T)
                    last = dve.copy_predicated(TT[:, i, 2 * o:2 * o + 2, :],
                                               masks[:, st.s - 1, o:o + 1, :].to_broadcast([P, T, P]), new)
                last.then_inc(bank_taken[job.bank], 1)

            def du4(st):
                job, i = st.jobs[0], st.h % 2
                dve.wait_ge(out_rsqrt_ready, reach("out_rsqrt_ready", st.at["out_rsqrt_ready"]))
                for t in range(T):
                    last = dve.tensor_scalar(OD[:, i, t, :], PS[:, job.bank, t * P:(t + 1) * P],
                                             RSO[:, 2 * i + t:2 * i + t + 1], None, ALU.mult)
                last.then_inc(bank_taken[job.bank], 1)

            def dot(st):
                job, i, h = st.jobs[0], st.h % 2, st.h
                dve.wait_ge(bank_full[job.bank], full_at(job))
                dve.scalar_tensor_tensor(out=TMP[:, h % 2, :], in0=PS[:, job.bank, 0:S], scalar=GDH[:, 0:1],
                                         in1=ZS[:, h, :], op0=ALU.mult, op1=ALU.mult
                                         ).then_inc(bank_taken[job.bank], 1)
                split_here(YBH[:, h, :], YBL[:, h, :], TMP[:, h % 2, :]).then_inc(delta_out_ready, 1)

            dve.wait_ge(x_loaded, 16)
            dve.drain().then_inc(residual_ready, 2)
            dve.wait_ge(ident_loaded, 16)
            walk(dve, {"norm": norm, "small_split": small_split, "xt": xt, "gu": gu, "post": post, "lam": lam, "pb": pb, "convb": convb,
                       "pf": pf, "pa": pa, "conva": conva, "score": score, "diff": diff, "out_norm": out_norm,
                       "lnb1": lnb1, "lnb3": lnb3, "out_turn": out_turn, "gy": gy}, 1, split_low)
            dve.drain()
            dve.tensor_copy(XN[:, :, :], H[:, :, :]).then_inc(normed_ready, T)
            dve.wait_ge(prologue_row, 1)
            dve.scalar_tensor_tensor(out=ROWS[0:NH_A, 3, :], in0=PS[0:NH_A, 0, 0:384], scalar=1.0 / QK_SCALE,
                                     in1=ROWS[0:NH_A, 2, :], op0=ALU.mult, op1=ALU.add).then_inc(prologue_done, 1)
            walk(dve, {"xt": xt, "gu": gu, "score": score, "out_norm": out_norm, "gy": gy, "factors": factors,
                       "small_split": small_split,
                       "post2": post2, "ps": ps, "cumg": cumg, "pz": pz, "taps": taps, "silu": silu, "dte": dte, "ddc": ddc,
                       "dtf": dtf, "dkk": dkk, "dl0": dl0, "dlb": dlb, "du4": du4, "dot": dot,
                       "out_turn": out_turn}, 2, split_low)


def _cols_unit(w, c):
    return w[:, c * 256:(c + 1) * 256].reshape(-1, P, 256).transpose(1, 0, 2).reshape(P, UNIT)


def _pair_unit(v, i, w, j):
    return _cols_unit(np.concatenate([v[:, i * P:(i + 1) * P], w[:, j * P:(j + 1) * P]], 1), 0)


def _rows_unit(w, r):
    return w[r * 256:(r + 1) * 256].reshape(2, P, D).transpose(1, 0, 2).reshape(P, UNIT)


def _by_feature(v):
    v = v.reshape(-1, v.shape[-1] // P, P)
    return v.transpose(2, 0, 1).reshape(P, -1)


def _rows(v):
    return np.broadcast_to(v.reshape(1, -1), (P, v.size))


def lay_out(a):
    s1 = np.zeros((L, PLANS[1].units, P, UNIT), np.float32)
    s2 = np.empty((L, PLANS[2].units, P, UNIT), np.float32)
    prms = np.zeros((2 * L + 1, P, max(NCOL1, NCOL2)), np.float32)
    order = [8 * (b // 4) + b % 4 + 4 * u for b in range(8) for u in range(2)]
    for l in range(L):
        w_in = a["w_in"][l]
        w_main = np.concatenate([w_in[:, :5632], w_in[:, 5640:]], 1)
        outs = [a[n][l] for n in ("a_w_out", "b_w_out", "c_w_out", "d_w_out")]
        for i, key in enumerate(PLANS[1].stream):
            f = "ffn1" if key[0] in ("gu", "d") and key[1] == 0 else "ffn2"
            if key[0] == "gu":
                u = _pair_unit(a[f + "_w_gate"][l], key[2], a[f + "_w_up"][l], key[2])
            elif key[0] == "d":
                u = _rows_unit(a[f + "_w_down"][l], key[2])
            elif key[0] == "ba":
                u = _pair_unit(w_main, 12 + key[1], w_main, 16 + key[1])
            elif key[0] == "aa":
                u = _pair_unit(w_main, 4 + key[1], w_main, 8 + key[1])
            elif key[0] == "w":
                u = _cols_unit(w_main, key[1])
            elif key[0] == "gy":
                k, g = key[2], 44 + 8 * key[1] + key[2]
                u = np.zeros((P, UNIT), np.float32)
                rows = np.concatenate([w_main[:, g * P:(g + 1) * P], outs[key[1]][:, k * P:(k + 1) * P]])
                u[:, :12 * P] = rows.reshape(12, P, P).transpose(1, 0, 2).reshape(P, 12 * P)
            else:
                u = _rows_unit(a["w_o"][l], key[1])
            s1[l, i] = u
        lam_init = 0.8 - 0.6 * math.exp(-0.3 * l)
        parts = {"g0": _by_feature(a["ffn1_pre_g"][l]), "g1": _by_feature(a["mix_pre_g"][l]),
                 "g2": _by_feature(a["ffn2_pre_g"][l]), "aw": _by_feature(a["a_conv_w"][l]),
                 "bw": _by_feature(a["b_conv_w"][l]), "bb": _by_feature(a["b_conv_b"][l]),
                 "blg": _by_feature(a["b_ln_g"][l]), "blb": _by_feature(a["b_ln_b"][l]),
                 "sub": _by_feature(a["c_subln_g"][l]),
                 "lami": _rows(np.array([lam_init, 1.0 - lam_init], np.float32)),
                 "fb": _rows(a["d_forget_b"][l]),
                 "lam": _rows(np.concatenate([a[n][l] for n in ("c_lam_q1", "c_lam_k1", "c_lam_q2", "c_lam_k2")])),
                 "wf": w_in[:, 5632:5640].reshape(KB, P, 8).transpose(1, 0, 2).reshape(P, 64)}
        for name, (c0, c1) in COL1.items():
            prms[l, :, c0:c1] = parts[name]
        none = (np.ones(D, np.float32), np.zeros(D, np.float32))
        into = [np.stack([a[name][l - 1, 2] if l else none[n], a[name][l, 0], a[name][l, 1]])
                for n, name in enumerate(("ln_g_2", "ln_b_2"))]
        w_in = a["w_in_2"][l]
        qa = w_in[:, :1024].reshape(D, NH_A, 64)[:, order].reshape(D, 1024)
        w_main = np.concatenate([qa, w_in[:, 1024:4608], w_in[:, 4624:]], 1)
        for i, key in enumerate(PLANS[2].stream):
            f = 0 if key[0] in ("gu", "d") and key[1] == 0 else 1
            if key[0] == "gu":
                w13 = a["ffn_w13_2"][l, f]
                u = _pair_unit(w13, key[2], w13, FB + key[2])
            elif key[0] == "d":
                u = _rows_unit(a["ffn_w2_2"][l, f], key[2])
            elif key[0] == "w":
                u = _cols_unit(w_main, key[1])
            elif key[0] == "gy":
                out = a["w_branch_a_2" if key[1] == 0 else "w_branch_b_2"][l]
                u = _pair_unit(w_main, 44 + 8 * key[1] + key[2], out, key[2])
            else:
                u = _rows_unit(a["w_out_2"][l], key[1])
            s2[l, i] = u
        parts = {"cw": _by_feature(a["conv_w_2"][l]), "dng": _by_feature(a["dn_norm_g_2"][l]),
                 "sink": _rows(a["sinks_2"][l]), "dtb": _rows(a["dt_bias_2"][l]), "alog": _rows(a["a_log_2"][l]),
                 "ing": _by_feature(into[0]), "inb": _by_feature(into[1]),
                 "ws": w_in[:, 4608:4624].reshape(KB, P, 16).transpose(1, 0, 2).reshape(P, 128)}
        for name, (c0, c1) in COL2.items():
            prms[L + l, :, c0:c1] = parts[name]
    feat1 = np.stack([a["ffn1_post_g"], a["mix_post_g"], a["ffn2_post_g"]], 1)
    feat2 = np.stack([a["ln_g_2"], a["ln_b_2"]], 2)
    onehot, rowmask = bias_table()
    return {"x": a["x"], "stream1": s1, "stream2": s2, "prms": prms, "feat1": feat1, "feat2": feat2,
            "con": constants(), "onehot": onehot, "rowmask": rowmask.reshape(1, 384), "relb": a["rel_bias_2"]}


def kernel(**inputs):
    import concourse.bacc as _bacc
    from concourse.bass_utils import run_bass_kernel_spmd as _run

    a = {k: np.asarray(v) for k, v in inputs.items()}
    arrays = {k: np.ascontiguousarray(v) for k, v in lay_out(a).items()}
    nc = _bacc.Bacc("TRN2", target_bir_lowering=False, num_devices=1)
    aps = {n: nc.dram_tensor(n, v.shape, F32, kind="ExternalInput").ap() for n, v in arrays.items()}
    aps["toep"] = nc.dram_tensor("toeplitz_rows", (NH_A, P, 384), F32, kind="Internal").ap()
    aps["out"] = nc.dram_tensor("out", (1, S, D), F32, kind="ExternalOutput").ap()
    build_kernel(nc, **aps)
    r = _run(nc, [arrays], core_ids=[0])
    return r.results[0]["out"]
```
